# Optimizing a Trainium2 kernel written in Bass

```python
import jax, jax.numpy as jnp
from jax import lax
import numpy as np
import math

D_MODEL = 1024
BATCH = 1
SEQ = 256
DEPTH = 2

BLOCK = 128
NORM_EPS = 1e-6
SWA_WINDOW = 128
SWA_HEADS = 4
SWA_KV_HEADS = 2
SWA_HEAD_DIM = 64
CONV_WIDTH = 256
CONV_K = 3
MLA_HEADS = 4
MLA_Q_RANK = 256
MLA_KV_RANK = 128
MLA_NOPE_DIM = 64
MLA_ROPE_DIM = 32
MLA_V_DIM = 64
ROPE_THETA = 10000.0
SB_HEADS = 4
SB_HEAD_DIM = 64
GROUP_WIDTH = 256
N_GROUPS = 4
D_MIX = GROUP_WIDTH * N_GROUPS

A_Q = SWA_HEADS * SWA_HEAD_DIM
A_KV = SWA_KV_HEADS * SWA_HEAD_DIM
SB_W = SB_HEADS * SB_HEAD_DIM
IN_SIZES = (A_Q, A_KV, A_KV,
            CONV_WIDTH, CONV_WIDTH, CONV_WIDTH,
            MLA_Q_RANK, MLA_KV_RANK, MLA_ROPE_DIM,
            SB_W, SB_W, SB_W,
            D_MIX)
D_IN = int(sum(IN_SIZES))
SPLIT_IDX = [int(v) for v in np.cumsum(IN_SIZES)[:-1]]


def rmsnorm(x, g):
    x32 = x.astype(jnp.float32)
    y = x32 * lax.rsqrt(jnp.mean(x32 * x32, axis=-1, keepdims=True) + NORM_EPS)
    return (y * g.astype(jnp.float32)).astype(x.dtype)

def to_blocks(t):
    b, s = t.shape[:2]
    t = t.reshape((b, s // BLOCK, BLOCK) + t.shape[2:])
    return jnp.moveaxis(t, 1, 0)

def from_blocks(t):
    t = jnp.moveaxis(t, 0, 1)
    return t.reshape((t.shape[0], t.shape[1] * t.shape[2]) + t.shape[3:])

def rope(x, pos):
    half = x.shape[-1] // 2
    freqs = ROPE_THETA ** (-jnp.arange(half, dtype=jnp.float32) / half)
    ang = pos.astype(jnp.float32)[..., None] * freqs
    ang = ang.reshape(ang.shape[:2] + (1,) * (x.ndim - 3) + (half,))
    cos, sin = jnp.cos(ang), jnp.sin(ang)
    x32 = x.astype(jnp.float32)
    x1, x2 = x32[..., :half], x32[..., half:]
    return jnp.concatenate([x1 * cos - x2 * sin, x1 * sin + x2 * cos], axis=-1).astype(x.dtype)

def swa_sink_attention(q, k, v, sinks):
    b, s, h, d = q.shape
    kvh = k.shape[2]
    g = h // kvh
    nb = s // BLOCK
    qb = q.reshape(b, nb, BLOCK, kvh, g, d).astype(jnp.float32)
    kb = k.reshape(b, nb, BLOCK, kvh, d).astype(jnp.float32)
    vb = v.reshape(b, nb, BLOCK, kvh, d).astype(jnp.float32)
    prev = lambda t: jnp.concatenate([jnp.zeros_like(t[:, :1]), t[:, :-1]], axis=1)
    kk = jnp.concatenate([prev(kb), kb], axis=2)
    vv = jnp.concatenate([prev(vb), vb], axis=2)
    scores = jnp.einsum('bnqhgd,bnkhd->bnhgqk', qb, kk) * (d ** -0.5)
    qi = jnp.arange(BLOCK)[:, None]
    kj = jnp.arange(2 * BLOCK)[None, :]
    diff = qi + BLOCK - kj
    blk = jnp.arange(nb)[:, None, None]
    valid = (diff >= 0) & (diff < SWA_WINDOW) & (blk * BLOCK + kj - BLOCK >= 0)
    scores = jnp.where(valid[None, :, None, None], scores, -jnp.inf)
    sink = jnp.broadcast_to(sinks.astype(jnp.float32).reshape(1, 1, kvh, g, 1, 1), scores.shape[:-1] + (1,))
    probs = jax.nn.softmax(jnp.concatenate([scores, sink], axis=-1), axis=-1)[..., :-1]
    out = jnp.einsum('bnhgqk,bnkhd->bnqhgd', probs, vv)
    return out.reshape(b, s, h * d).astype(q.dtype)

def short_gated_conv(bg, cg, xin, conv_w, conv_b):
    u = cg * xin
    y = lax.conv_general_dilated(u, conv_w[:, None, :], window_strides=(1,),
                                 padding=[(CONV_K - 1, 0)],
                                 dimension_numbers=('NWC', 'WIO', 'NWC'),
                                 feature_group_count=u.shape[-1])
    return bg * (y + conv_b)

def causal_softmax_attention(q, k, v):
    b, s, h, dk = q.shape
    scale = dk ** -0.5
    kf = k.astype(jnp.float32)
    vf = v.astype(jnp.float32)
    kpos = jnp.arange(s)

    def step(args):
        qblk, i = args
        sc = jnp.einsum('bqhd,bkhd->bhqk', qblk.astype(jnp.float32), kf) * scale
        qpos = i * BLOCK + jnp.arange(BLOCK)
        sc = jnp.where(kpos[None, :] <= qpos[:, None], sc, -jnp.inf)
        p = jax.nn.softmax(sc, axis=-1)
        return jnp.einsum('bhqk,bkhd->bqhd', p, vf)

    out = lax.map(step, (to_blocks(q), jnp.arange(s // BLOCK)))
    return from_blocks(out).reshape(b, s, -1).astype(q.dtype)

def mla(cq, ckv, kr, pos, g_q, w_uq, g_kv, w_ukv):
    b, s, _ = cq.shape
    q = (rmsnorm(cq, g_q) @ w_uq).reshape(b, s, MLA_HEADS, MLA_NOPE_DIM + MLA_ROPE_DIM)
    q = jnp.concatenate([q[..., :MLA_NOPE_DIM], rope(q[..., MLA_NOPE_DIM:], pos)], axis=-1)
    kv = (rmsnorm(ckv, g_kv) @ w_ukv).reshape(b, s, MLA_HEADS, MLA_NOPE_DIM + MLA_V_DIM)
    k_nope, v = kv[..., :MLA_NOPE_DIM], kv[..., MLA_NOPE_DIM:]
    k_rope = jnp.broadcast_to(rope(kr, pos)[:, :, None, :], (b, s, MLA_HEADS, MLA_ROPE_DIM))
    k = jnp.concatenate([k_nope, k_rope], axis=-1)
    return causal_softmax_attention(q, k, v)

def stick_breaking_attention(q, k, v):
    b, s, h, d = q.shape
    scale = d ** -0.5
    kf = k.astype(jnp.float32)
    vf = v.astype(jnp.float32)
    kpos = jnp.arange(s)

    def step(args):
        qblk, i = args
        z = jnp.einsum('bqhd,bkhd->bhqk', qblk.astype(jnp.float32), kf) * scale
        qpos = i * BLOCK + jnp.arange(BLOCK)
        mask = kpos[None, :] < qpos[:, None]
        log_keep = jnp.where(mask, jax.nn.log_sigmoid(-z), 0.0)
        after = lax.cumsum(log_keep, axis=3, reverse=True) - log_keep
        a = jnp.where(mask, jnp.exp(jax.nn.log_sigmoid(z) + after), 0.0)
        return jnp.einsum('bhqk,bkhd->bqhd', a, vf)

    out = lax.map(step, (to_blocks(q), jnp.arange(s // BLOCK)))
    return from_blocks(out).reshape(b, s, -1).astype(q.dtype)

def hybrid_layer(x, pos, g_pre, w_in, sinks, conv_w, conv_b, g_cq, w_uq, g_ckv, w_ukv, g_grp, w_out, g_post):
    b, s, _ = x.shape
    h = rmsnorm(x, g_pre) @ w_in
    (a_q, a_k, a_v, b_b, b_c, b_x, c_q, c_kv, c_kr, d_q, d_k, d_v, gate) = jnp.split(h, SPLIT_IDX, axis=-1)
    ya = swa_sink_attention(a_q.reshape(b, s, SWA_HEADS, SWA_HEAD_DIM),
                            a_k.reshape(b, s, SWA_KV_HEADS, SWA_HEAD_DIM),
                            a_v.reshape(b, s, SWA_KV_HEADS, SWA_HEAD_DIM), sinks)
    yb = short_gated_conv(b_b, b_c, b_x, conv_w, conv_b)
    yc = mla(c_q, c_kv, c_kr, pos, g_cq, w_uq, g_ckv, w_ukv)
    yd = stick_breaking_attention(d_q.reshape(b, s, SB_HEADS, SB_HEAD_DIM),
                                  d_k.reshape(b, s, SB_HEADS, SB_HEAD_DIM),
                                  d_v.reshape(b, s, SB_HEADS, SB_HEAD_DIM))
    y = jnp.stack([ya, yb, yc, yd], axis=2)
    y = rmsnorm(y, g_grp.reshape(N_GROUPS, GROUP_WIDTH)).reshape(b, s, D_MIX)
    y = y * jax.nn.silu(gate)
    return x + rmsnorm(y @ w_out, g_post)

def first_inputs(seed: int = 0) -> dict:
    key = jax.random.key(seed)
    ks = jax.random.split(key, 16)
    f32 = jnp.float32
    nrm = lambda k, shape, scale: jax.random.normal(k, shape, f32) * scale
    gain = lambda k, shape: 1.0 + 0.02 * jax.random.normal(k, shape, f32)
    x = jax.random.normal(ks[0], (BATCH, SEQ, D_MODEL), f32)
    positions = jnp.broadcast_to(jnp.arange(SEQ, dtype=jnp.int32)[None, :], (BATCH, SEQ))
    return {
        "x": x,
        "positions": positions,
        "norm_pre": gain(ks[1], (DEPTH, D_MODEL)),
        "w_in": nrm(ks[2], (DEPTH, D_MODEL, D_IN), D_MODEL ** -0.5),
        "attn_sinks": nrm(ks[3], (DEPTH, SWA_HEADS), 0.5),
        "conv_w": nrm(ks[4], (DEPTH, CONV_K, CONV_WIDTH), CONV_K ** -0.5),
        "conv_b": nrm(ks[5], (DEPTH, CONV_WIDTH), 0.01),
        "mla_q_norm": gain(ks[6], (DEPTH, MLA_Q_RANK)),
        "mla_w_uq": nrm(ks[7], (DEPTH, MLA_Q_RANK, MLA_HEADS * (MLA_NOPE_DIM + MLA_ROPE_DIM)), MLA_Q_RANK ** -0.5),
        "mla_kv_norm": gain(ks[8], (DEPTH, MLA_KV_RANK)),
        "mla_w_ukv": nrm(ks[9], (DEPTH, MLA_KV_RANK, MLA_HEADS * (MLA_NOPE_DIM + MLA_V_DIM)), MLA_KV_RANK ** -0.5),
        "group_norm": gain(ks[10], (DEPTH, D_MIX)),
        "w_out": nrm(ks[11], (DEPTH, D_MIX, D_MODEL), D_MIX ** -0.5),
        "norm_post": gain(ks[12], (DEPTH, D_MODEL)),
    }

def first_block(x, positions, norm_pre, w_in, attn_sinks, conv_w, conv_b, mla_q_norm, mla_w_uq,
              mla_kv_norm, mla_w_ukv, group_norm, w_out, norm_post):
    for l in range(DEPTH):
        x = hybrid_layer(x, positions, norm_pre[l], w_in[l], attn_sinks[l], conv_w[l], conv_b[l],
                         mla_q_norm[l], mla_w_uq[l], mla_kv_norm[l], mla_w_ukv[l],
                         group_norm[l], w_out[l], norm_post[l])
    return x


N_META = 16
DN_HEADS = 4
DN_DK = 128
DN_DV = 128
DN_KEY = DN_HEADS * DN_DK
DN_VAL = DN_HEADS * DN_DV
CONV_W = 4
CHUNK = 64
SA_HEADS = 8
SA_DH = 64
SA_W = SA_HEADS * SA_DH
IDX_HEADS = 8
IDX_DH = 64
K_MAX = 256
Q_BLOCK = 128
MIX_W = DN_VAL + SA_W
EXP_PER_GROUP = 8
N_EXPERTS = N_GROUPS * EXP_PER_GROUP
TOP_K_IN_GROUP = 2
D_EXPERT = 256
DEEPNORM_ALPHA = (2.0 * DEPTH) ** 0.25
DEEPNORM_BETA = (8.0 * DEPTH) ** -0.25

SPLIT_SIZES = (DN_KEY, DN_KEY, DN_VAL, DN_VAL, DN_HEADS, DN_HEADS,
               SA_W, SA_W, SA_W, IDX_HEADS * IDX_DH, IDX_DH, IDX_HEADS)
SPLIT_POINTS = tuple(int(s) for s in np.cumsum(SPLIT_SIZES)[:-1])
D_IN_PROJ = int(sum(SPLIT_SIZES))
VALUE_COLS = (2, 8)


F32 = jnp.float32

def layer_norm(x, g, b, eps=1e-5):
    xf = x.astype(F32)
    mu = jnp.mean(xf, -1, keepdims=True)
    var = jnp.mean(jnp.square(xf - mu), -1, keepdims=True)
    return ((xf - mu) * lax.rsqrt(var + eps) * g + b).astype(x.dtype)

def rope_tables(n_pos, dim):
    inv = 1.0 / (ROPE_THETA ** (jnp.arange(0, dim, 2, dtype=F32) / dim))
    ang = jnp.arange(n_pos, dtype=F32)[:, None] * inv[None, :]
    ang = jnp.concatenate([ang, ang], -1)
    return jnp.cos(ang), jnp.sin(ang)

def apply_rope(x, cos, sin):
    half = x.shape[-1] // 2
    rot = jnp.concatenate([-x[..., half:], x[..., :half]], -1)
    shape = (1, cos.shape[0]) + (1,) * (x.ndim - 3) + (cos.shape[-1],)
    return (x * cos.reshape(shape) + rot * sin.reshape(shape)).astype(x.dtype)

def causal_dwconv(x, w):
    c = x.shape[-1]
    return lax.conv_general_dilated(x, w[:, None, :].astype(x.dtype), window_strides=(1,),
                                    padding=[(CONV_W - 1, 0)],
                                    dimension_numbers=('NWC', 'WIO', 'NWC'),
                                    feature_group_count=c)

def l2norm(x, eps=1e-6):
    return x * lax.rsqrt(jnp.sum(x * x, -1, keepdims=True) + eps)

def chunk_gated_delta_rule(q, k, v, g, beta):
    bsz, seq, h, dk = q.shape
    dv = v.shape[-1]
    n = seq // CHUNK

    def chunks(t):
        t = t.reshape((bsz, n, CHUNK, h) + t.shape[3:])
        return jnp.moveaxis(t, 3, 2)

    q, k, v, g, beta = (chunks(t) for t in (q, k, v, g, beta))
    q = q * dk ** -0.5
    gc = jnp.cumsum(g, axis=-1)
    pos = jnp.arange(CHUNK)
    tril = pos[:, None] >= pos[None, :]
    strict = pos[:, None] > pos[None, :]
    decay = jnp.exp(jnp.where(tril, gc[..., :, None] - gc[..., None, :], -jnp.inf))
    kb = k * beta[..., None]
    lower = jnp.where(strict, jnp.einsum('bnhid,bnhjd->bnhij', kb, k) * decay, 0.0)
    eye = jnp.eye(CHUNK, dtype=q.dtype)
    tmat = lax.linalg.triangular_solve(eye + lower, jnp.broadcast_to(eye, lower.shape),
                                       left_side=True, lower=True, unit_diagonal=True)
    u = tmat @ (v * beta[..., None])
    w = tmat @ (kb * jnp.exp(gc)[..., None])
    q_dec = q * jnp.exp(gc)[..., None]
    a_qk = jnp.where(tril, jnp.einsum('bnhid,bnhjd->bnhij', q, k) * decay, 0.0)
    g_last = gc[..., -1]
    k_dec = k * jnp.exp(g_last[..., None] - gc)[..., None]

    def step(state, inp):
        u_n, w_n, qd_n, a_n, kd_n, gl_n = inp
        v_new = u_n - jnp.einsum('bhck,bhkv->bhcv', w_n, state)
        o_n = jnp.einsum('bhck,bhkv->bhcv', qd_n, state) + jnp.einsum('bhij,bhjv->bhiv', a_n, v_new)
        state = state * jnp.exp(gl_n)[..., None, None] + jnp.einsum('bhck,bhcv->bhkv', kd_n, v_new)
        return state, o_n

    xs = tuple(jnp.moveaxis(t, 1, 0) for t in (u, w, q_dec, a_qk, k_dec, g_last))
    s0 = jnp.zeros((bsz, h, dk, dv), q.dtype)
    _, o = lax.scan(step, s0, xs)
    o = jnp.moveaxis(o, 0, 1)
    return jnp.moveaxis(o, 3, 2).reshape(bsz, seq, h, dv)

def deltanet_group(q, k, v, z, b_logit, a_logit, conv_w, a_log, dt_bias, norm_g):
    bsz, seq, _ = q.shape
    qkv = jax.nn.silu(causal_dwconv(jnp.concatenate([q, k, v], -1), conv_w)).astype(F32)
    q, k, v = jnp.split(qkv, [DN_KEY, 2 * DN_KEY], axis=-1)
    q = l2norm(q.reshape(bsz, seq, DN_HEADS, DN_DK))
    k = l2norm(k.reshape(bsz, seq, DN_HEADS, DN_DK))
    v = v.reshape(bsz, seq, DN_HEADS, DN_DV)
    beta = jax.nn.sigmoid(b_logit.astype(F32))
    g = -jnp.exp(a_log.astype(F32)) * jax.nn.softplus(a_logit.astype(F32) + dt_bias.astype(F32))
    pad = (-N_META) % CHUNK
    padf = lambda t: jnp.pad(t, ((0, 0), (pad, 0)) + ((0, 0),) * (t.ndim - 2))
    o = chunk_gated_delta_rule(padf(q), padf(k), padf(v), padf(g), padf(beta))[:, pad:]
    o = o * lax.rsqrt(jnp.mean(o * o, -1, keepdims=True) + 1e-6) * norm_g
    o = o.reshape(bsz, seq, DN_VAL) * jax.nn.silu(z.astype(F32))
    return o.astype(z.dtype)

def dsa_group(q, k, v, qi, ki, wi, cos, sin, cos_i, sin_i, k_top):
    bsz, seq, _ = q.shape
    q = apply_rope(q.reshape(bsz, seq, SA_HEADS, SA_DH), cos, sin)
    k = apply_rope(k.reshape(bsz, seq, SA_HEADS, SA_DH), cos, sin)
    v = v.reshape(bsz, seq, SA_HEADS, SA_DH)
    qi = apply_rope(qi.reshape(bsz, seq, IDX_HEADS, IDX_DH), cos_i, sin_i)
    ki = apply_rope(ki, cos_i, sin_i)
    wi = wi.astype(F32) * IDX_HEADS ** -0.5
    n_blk = -(-seq // Q_BLOCK)
    lq = n_blk * Q_BLOCK

    def blocks(t):
        t = jnp.pad(t, ((0, 0), (0, lq - seq)) + ((0, 0),) * (t.ndim - 2))
        return jnp.moveaxis(t.reshape((bsz, n_blk, Q_BLOCK) + t.shape[2:]), 1, 0)

    key_pos = jnp.arange(seq)
    q_pos = jnp.arange(lq).reshape(n_blk, Q_BLOCK)
    gather = jax.vmap(lambda arr, idx: arr[idx])

    def attend(args):
        qb, qib, wib, pos = args
        causal = key_pos[None, :] <= pos[:, None]
        rel = jax.nn.relu(jnp.einsum('bqhd,bsd->bqhs', qib, ki, preferred_element_type=F32) * IDX_DH ** -0.5)
        score = jnp.einsum('bqhs,bqh->bqs', rel, wib)
        score = jnp.where(causal[None], score, -jnp.inf)
        _, sel = lax.top_k(score, k_top)
        k_sel = gather(k, sel)
        v_sel = gather(v, sel)
        valid = sel <= pos[None, :, None]
        logits = jnp.einsum('bqhd,bqkhd->bhqk', qb, k_sel, preferred_element_type=F32) * SA_DH ** -0.5
        logits = jnp.where(valid[:, None], logits, -jnp.inf)
        p = jax.nn.softmax(logits, axis=-1)
        return jnp.einsum('bhqk,bqkhd->bqhd', p.astype(v.dtype), v_sel)

    out = lax.map(attend, (blocks(q), blocks(qi), blocks(wi), q_pos))
    return jnp.moveaxis(out, 0, 1).reshape(bsz, lq, SA_W)[:, :seq]

def hier_moe(h, w_grp, b_grp, w_rtr, b_rtr, w1, w3, w2):
    bsz, seq, d = h.shape
    t = h.reshape(-1, d)
    grp_prob = jax.nn.softmax((t @ w_grp).astype(F32) + b_grp, axis=-1)
    g_prob, g_sel = lax.top_k(grp_prob, 1)
    exp_logits = ((t @ w_rtr).astype(F32) + b_rtr).reshape(-1, N_GROUPS, EXP_PER_GROUP)
    in_grp = jnp.take_along_axis(exp_logits, g_sel[:, :, None], axis=1)[:, 0]
    e_prob, e_sel = lax.top_k(jax.nn.softmax(in_grp, axis=-1), TOP_K_IN_GROUP)
    gate = g_prob * e_prob / jnp.sum(e_prob, -1, keepdims=True)
    expert_id = g_sel * EXP_PER_GROUP + e_sel
    combine = jnp.sum(jax.nn.one_hot(expert_id, N_EXPERTS, dtype=F32) * gate[..., None], axis=1)
    hid = jax.nn.silu(jnp.einsum('td,edf->tef', t, w1)) * jnp.einsum('td,edf->tef', t, w3)
    y = jnp.einsum('tef,efd->td', hid * combine[..., None].astype(hid.dtype), w2)
    return y.reshape(bsz, seq, d)

def second_inputs(seed: int = 0) -> dict:
    key = jax.random.key(seed)
    ks = jax.random.split(key, 20)
    nrm = lambda k, shape, s: jax.random.normal(k, shape, F32) * s
    d_sc = D_MODEL ** -0.5
    col_scale = np.concatenate([np.full((s,), DEEPNORM_BETA if i in VALUE_COLS else 1.0, np.float32)
                                for i, s in enumerate(SPLIT_SIZES)])
    dt = jnp.exp(jax.random.uniform(ks[5], (DEPTH, DN_HEADS), F32, math.log(1e-3), math.log(1e-1)))
    return {
        'x': nrm(ks[0], (BATCH, SEQ, D_MODEL), 1.0),
        'meta_tokens': nrm(ks[1], (N_META, D_MODEL), 1.0),
        'w_in': nrm(ks[2], (DEPTH, D_MODEL, D_IN_PROJ), d_sc) * jnp.asarray(col_scale),
        'conv_w': nrm(ks[3], (DEPTH, CONV_W, 2 * DN_KEY + DN_VAL), CONV_W ** -0.5),
        'a_log': jnp.log(jax.random.uniform(ks[4], (DEPTH, DN_HEADS), F32, 1.0, 16.0)),
        'dt_bias': dt + jnp.log(-jnp.expm1(-dt)),
        'dn_norm_g': 1.0 + nrm(ks[6], (DEPTH, DN_DV), 0.02),
        'w_out': nrm(ks[7], (DEPTH, MIX_W, D_MODEL), MIX_W ** -0.5 * DEEPNORM_BETA),
        'ln1_g': 1.0 + nrm(ks[8], (DEPTH, D_MODEL), 0.02),
        'ln1_b': nrm(ks[9], (DEPTH, D_MODEL), 0.02),
        'w_grp': nrm(ks[10], (DEPTH, D_MODEL, N_GROUPS), d_sc),
        'b_grp': nrm(ks[11], (DEPTH, N_GROUPS), 0.01),
        'w_rtr': nrm(ks[12], (DEPTH, D_MODEL, N_EXPERTS), d_sc),
        'b_rtr': nrm(ks[13], (DEPTH, N_EXPERTS), 0.01),
        'w1': nrm(ks[14], (DEPTH, N_EXPERTS, D_MODEL, D_EXPERT), d_sc),
        'w3': nrm(ks[15], (DEPTH, N_EXPERTS, D_MODEL, D_EXPERT), d_sc),
        'w2': nrm(ks[16], (DEPTH, N_EXPERTS, D_EXPERT, D_MODEL), D_EXPERT ** -0.5 * DEEPNORM_BETA),
        'ln2_g': 1.0 + nrm(ks[17], (DEPTH, D_MODEL), 0.02),
        'ln2_b': nrm(ks[18], (DEPTH, D_MODEL), 0.02),
    }

def second_block(x, meta_tokens, w_in, conv_w, a_log, dt_bias, dn_norm_g, w_out, ln1_g, ln1_b,
              w_grp, b_grp, w_rtr, b_rtr, w1, w3, w2, ln2_g, ln2_b):
    bsz, seq, _ = x.shape
    total = seq + N_META
    k_top = min(K_MAX, seq // 4)
    meta = jnp.broadcast_to(meta_tokens[None].astype(x.dtype), (bsz, N_META, D_MODEL))
    h = jnp.concatenate([meta, x], axis=1)
    cos, sin = rope_tables(total, SA_DH)
    cos_i, sin_i = rope_tables(total, IDX_DH)
    for l in range(DEPTH):
        proj = h @ w_in[l]
        dq, dk, dv, dz, db, da, sq, sk, sv, iq, ik, iw = jnp.split(proj, SPLIT_POINTS, axis=-1)
        o_dn = deltanet_group(dq, dk, dv, dz, db, da, conv_w[l], a_log[l], dt_bias[l], dn_norm_g[l])
        o_sa = dsa_group(sq, sk, sv, iq, ik, iw, cos, sin, cos_i, sin_i, k_top)
        mix = jnp.concatenate([o_dn, o_sa.astype(o_dn.dtype)], axis=-1) @ w_out[l]
        h = layer_norm(DEEPNORM_ALPHA * h + mix, ln1_g[l], ln1_b[l])
        ffn = hier_moe(h, w_grp[l], b_grp[l], w_rtr[l], b_rtr[l], w1[l], w3[l], w2[l])
        h = layer_norm(DEEPNORM_ALPHA * h + ffn, ln2_g[l], ln2_b[l])
    return h[:, N_META:]


def setup_inputs(seed=0):
    out = dict(first_inputs(seed))
    for name, value in second_inputs(seed + 1).items():
        if name != "x":
            out[name + "_2"] = value
    return out


def reference(
    x, positions, norm_pre, w_in, attn_sinks, conv_w, conv_b, mla_q_norm, mla_w_uq, mla_kv_norm,
    mla_w_ukv, group_norm, w_out, norm_post, meta_tokens_2, w_in_2, conv_w_2, a_log_2,
    dt_bias_2, dn_norm_g_2, w_out_2, ln1_g_2, ln1_b_2, w_grp_2, b_grp_2, w_rtr_2, b_rtr_2, w1_2,
    w3_2, w2_2, ln2_g_2, ln2_b_2,
):
    x = first_block(
        x, positions, norm_pre, w_in, attn_sinks, conv_w, conv_b, mla_q_norm, mla_w_uq,
        mla_kv_norm, mla_w_ukv, group_norm, w_out, norm_post,
    )
    return second_block(
        x, meta_tokens_2, w_in_2, conv_w_2, a_log_2, dt_bias_2, dn_norm_g_2, w_out_2, ln1_g_2,
        ln1_b_2, w_grp_2, b_grp_2, w_rtr_2, b_rtr_2, w1_2, w3_2, w2_2, ln2_g_2, ln2_b_2,
    )


_drawn_inputs = setup_inputs


def setup_inputs(seed=0):
    import zlib

    import numpy as np

    out = dict(_drawn_inputs(seed))
    spreads = {}
    factors = {'attn_sinks': 2.828,
     'conv_b': 4.582,
     'mla_q_norm': 2.947,
     'dn_norm_g_2': 8.0,
     'b_grp_2': 8.0,
     'b_rtr_2': 7.144}
    for name, (base, spread) in spreads.items():
        noise = np.random.default_rng([zlib.crc32(name.encode()), seed]).standard_normal(out[name].shape)
        drawn = base * np.exp(spread * noise) if base else spread * noise
        out[name] = __import__('jax').numpy.asarray(drawn.astype(out[name].dtype))
    for name, factor in factors.items():
        out[name] = (out[name] * factor).astype(out[name].dtype)
    return out
```

```python
from contextlib import ExitStack

import numpy as np

import concourse.bass as bass
from concourse import mybir

F32 = mybir.dt.float32
I32 = mybir.dt.int32
ALU = mybir.AluOpType
ACT = mybir.ActivationFunctionType
AX = mybir.AxisListType.X

P = 128
D = 1024
KC = D // P
SEQ = 256
META = 16
T = SEQ + META
LAYERS = 2
COL = [0, META, META + P]
ROWS = [META, P, P]
NEG = -1.0e30
SLOTS = 6
SLOT = 2048
CREDIT = 32

SQ, SK, SV, CB, CC, CX, MQ, MKV, MKR, DQ, DK, DV, GATE = 0, 2, 4, 5, 7, 9, 11, 13, 14, 15, 17, 19, 21
N1 = 29
ITEMS_P1 = (N1 + 1) // 2
ITEMS_WO = 4
ITEMS1 = ITEMS_P1 + ITEMS_WO
SLOT0_1 = 0
NQ, NK_, NV, NZ, AQ, AK, AV, IQ, IK, SM = 0, 4, 8, 12, 16, 20, 24, 28, 32, 33
N2 = 34
ITEMS_P2 = N2 // 2
EXPERTS = 32
GROUPS = 4
D_EXP = 256
TURNS = EXPERTS // 2 - 1
PER_GROUP = EXPERTS // GROUPS
GROUP_SLOTS = P
ITEMS_MIX2 = ITEMS_P2 + ITEMS_WO
ITEMS2 = ITEMS_MIX2 + 3 * EXPERTS
SLOT0_2 = (1 - ITEMS2) % SLOTS
TOPK = 64
ROPE_CHUNKS = [*range(AQ, AQ + 4), *range(AK, AK + 4), *range(IQ, IQ + 4), IK]
ALPHA = float((2.0 * LAYERS) ** 0.25)

P1 = {}
P2 = {}
CONSTS = {}


def _columns(table, entries):
    at = 0
    for name, n in entries:
        table[name] = (at, at + n)
        at += n
    return at


NP1 = _columns(P1, [("g_pre", KC), ("g_q", 2), ("g_kv", 1), ("conv_w", 6), ("conv_b", 2), ("g_grp", KC),
                    ("sinks", 4), ("w_uq", 2 * 384), ("w_ukv", 512), ("g_post", D)])
NP2S = _columns(P2, [("conv_w", 48), ("norm_g", 1), ("a_log", 1), ("dt", 1), ("br", 36), ("wr", KC * 36),
                     ("ln1_g", D), ("ln1_b", D), ("ln2_g", D), ("ln2_b", D)])
NP2 = NP2S
NLEV = 7
NC_ = _columns(CONSTS, [("ident", P), ("ones", P), ("tri", P), ("upper", P), ("strict", P),
                        ("swa_mask", 2 * P), ("mla_mask", 2 * P), ("lev_u", NLEV * P), ("lev_l", NLEV * P),
                        ("rot", P), ("rot96", 32), ("freq", 1), ("cos", T), ("sin", T),
                        ("sel", 4 * P), ("selb", 4 * P), ("caus", T), ("caus2", T), ("desc", 32), ("sel2", 2 * P),
                        ("slots", GROUP_SLOTS)])


def constants():
    c = np.zeros((P, NC_), np.float32)

    def put(name, a, rows=slice(None)):
        lo, hi = CONSTS[name]
        c[rows, lo:hi] = np.asarray(a, np.float32).reshape(-1, hi - lo)

    p, f = np.arange(P)[:, None], np.arange(P)[None, :]
    put("ident", p == f)
    put("ones", np.ones((P, P)))
    put("tri", p >= f)
    put("upper", f >= p)
    put("strict", f > p)
    causal = np.where(f <= p, 0.0, NEG)
    put("swa_mask", np.concatenate([np.where(f > p, 0.0, NEG), causal], 1))
    put("mla_mask", np.concatenate([0.0 * causal, causal], 1))
    lev = []
    for n in range(NLEV):
        s = 1 << n
        lev.append((p // (2 * s) == f // (2 * s)) & (p % (2 * s) < s) & (f % (2 * s) >= s))
    put("lev_u", np.concatenate(lev, 1))
    put("lev_l", np.concatenate([m.T for m in lev], 1))
    rot = np.zeros((P, P))
    for h in range(2):
        for i in range(32):
            rot[64 * h + 32 + i, 64 * h + i] = -1.0
            rot[64 * h + i, 64 * h + 32 + i] = 1.0
    put("rot", rot)
    r96 = np.zeros((P, 32))
    for i in range(16):
        r96[64 + 16 + i, i] = -1.0
        r96[64 + i, 16 + i] = 1.0
    put("rot96", r96)
    half = np.float32(10000.0) ** (-np.arange(16, dtype=np.float32) / np.float32(16))
    put("freq", np.tile(half, 8)[:, None])
    inv = np.float32(1.0) / (np.float32(10000.0) ** (np.arange(0, 64, 2, dtype=np.float32) / np.float32(64)))
    ang = (np.arange(T, dtype=np.float32)[:, None] * inv[None, :]).astype(np.float32)
    put("cos", np.tile(np.cos(ang).T, (4, 1)))
    put("sin", np.tile(np.sin(ang).T, (4, 1)))
    sel = np.zeros((P, 4 * P))
    selb = np.zeros((P, 4 * P))
    for h in range(4):
        sel[h, h * P:(h + 1) * P] = 1.0
        selb[32 + h, h * P:(h + 1) * P] = 1.0
    put("sel", sel)
    put("selb", selb)
    key = np.arange(T)[None, :]
    put("caus", np.where(key <= META + p, 0.0, NEG))
    put("caus2", np.where(key <= META + P + p, 0.0, NEG))
    put("desc", np.broadcast_to(np.arange(32, 0, -1), (P, 32)))
    sel2 = np.zeros((P, 2 * P))
    sel2[0, :P] = 1.0
    sel2[1, P:] = 1.0
    put("sel2", sel2)
    put("slots", np.broadcast_to(np.arange(GROUP_SLOTS), (P, GROUP_SLOTS)))
    return c


class Linked:

    def __init__(self, eng, own):
        self.eng, self.own, self.n = eng, own, {}

    def __call__(self, ins, sem=None):
        sem = self.own if sem is None else sem
        ins.then_inc(sem, 1)
        self.n[sem.num] = self.n.get(sem.num, 0) + 1
        self.eng.wait_ge(sem, self.n[sem.num])


def ring_slot(block, i):
    return ((SLOT0_1 if block == 1 else SLOT0_2) + i) % SLOTS


def uses_before(block, i, slot):
    return sum(ring_slot(block, k) == slot for k in range(i))


def program(nc, A, out):
    with ExitStack() as ctx:
        def sb(name, *shape):
            return ctx.enter_context(nc.sbuf_tensor(name, [P, *shape], F32))

        layer_sems = []

        def sem(name):
            return ctx.enter_context(nc.semaphore(name))

        def lsem(name):
            layer_sems.append(sem(name))
            return layer_sems[-1]

        ring = sb("ring", SLOTS, SLOT)
        projT = sb("projT", N2, T)
        res = sb("res", 3, D)
        hT = sb("hT", KC, T)
        prm = sb("prm", max(NP1, NP2))
        cst = sb("cst", NC_)
        cosT = sb("cosT", SEQ)[:, :]
        sinT = sb("sinT", SEQ)[:, :]
        small = sb("small", 160)
        AR = 15232
        arena = sb("arena", AR)
        posi = ctx.enter_context(nc.sbuf_tensor("posi", [P, SEQ], I32))
        ps = ctx.enter_context(nc.psum_tensor("ps", [P, 8, 512], F32))
        comb_dram = nc.dram_tensor("comb_dram", (EXPERTS, T), F32, kind="Internal").ap()

        def carve(sizes):
            at, got = 0, []
            for s in sizes:
                n = int(np.prod(s))
                v = arena[:, at:at + n]
                if len(s) == 2:
                    v = v.rearrange("p (a b) -> p a b", b=s[1])
                if len(s) == 3:
                    v = v.rearrange("p (a b c) -> p a b c", b=s[1], c=s[2])
                got.append(v)
                at += n
            assert at <= AR, at
            return got

        def const(name):
            lo, hi = CONSTS[name]
            return cst[:, lo:hi]

        ident, ones, tri = const("ident"), const("ones"), const("tri")

        slot_in = [sem(f"slot_in{i}") for i in range(SLOTS)]
        ring_used = sem("ring_used")
        up_used = sem("up_used")
        down_used = sem("down_used")
        start_in = sem("start_in")
        meta_in = sem("meta_in")
        layer_done = sem("layer_done")
        layer_go = sem("layer_go")
        out_done = sem("out_done")
        seen = sem("seen")
        layer_seen = sem("layer_seen")
        tables_done = sem("tables_done")
        tables_vec = sem("tables_vec")

        names = ["act_order", "vec_order", "pool_order", "params_in", "rstd_ready", "xn_ready", "ht_done", "ht_ready",
                 "proj_done", "proj_ev_act", "proj_ev_vec", "v_done", "v_evicted",
                 "mla_sq", "mla_ss", "mla_rs", "mla_n", "mla_qk", "mla_qh", "mla_kh", "mla_rot", "mla_v", "mla_rope",
                 "s_ready", "stt_done", "nm_ready", "exp_done", "p_ready", "pt_done", "pt_evicted", "o_done",
                 "o_evicted", "sb_z", "sb_u", "sb_l", "sb_sp", "sb_r", "sb_d", "sb_a", "sb_am", "sb_o", "sb_oe",
                 "gate_exp", "conv_ready", "y_sq", "y_ss", "y_rs", "y_ready",
                 "out_ready", "out_ss", "res_ready",
                 "g_sm", "g_ln", "g_scan", "g_bc", "g_bcev", "g_cols", "g_colsev",                  "cv_ready", "cv_exp", "cv_silu", "cv_sq", "cv_ss", "cv_rs", "cv_norm", "kv_done", "kv_ev",
                 "gq_done", "d_diff", "d_exp", "d_u", "d_lt", "d_l", "d_ls", "d_p", "d_pev", "d_q", "d_y",
                 "d_ks", "d_r", "d_vn", "d_vnev", "d_kd", "d_o", "d_oev", "d_st", "d_stv",
                 "z_exp", "od_sq", "od_ss", "od_rs", "od_ready",
                 "rp_done", "rp_ready", "ix_s", "ix_relu", "ix_used",                  "ln_mean", "ln_rstd", "ln_done", "m_ht", "m_htev", "m_lg", "m_e1", "m_e1d",
                 "m_comb", "m_combT", "m_combev", "m_combst", "m_up", "m_exp", "m_cb", "m_hid", "m_y", "m_yadd", "vec_loop", "vec_turns",
                 "m_flag", "x_cg", "vec_sel", "act_group", "x_sel", "x_g", "x_ge", "x_exp", "x_hid", "x_t", "x_te", "x_ye",
                 "m_back", "cin"]
        S = {n: lsem(n) for n in names}

        def s(n):
            return S[n]

        block = ctx.enter_context(nc.Block())

        def new_layer(eng, l, base, value):
            eng.sem_inc(layer_done, 1)
            eng.wait_ge(layer_go, base + l + 1)

        w1p = A["w_in_1"]
        w2p = A["w_in_2"]

        @block.sync
        def _(sp):
            def load(blk, base, l, i, src):
                slot = ring_slot(blk, i)
                n = ITEMS1 if blk == 1 else ITEMS2
                ago = (-slot) % SLOTS
                used = base - ago if i < SLOTS else base + i - SLOTS + 1
                sp.wait_ge(ring_used, l * n + (used + CREDIT))
                sp.dma_start(ring[:, slot, :] if len(src.shape) == 2 else
                             ring[:, slot, :].rearrange("p (c n) -> p c n", c=src.shape[1]),
                             src).then_inc(slot_in[slot], 16)

            def rows2(w, first):
                return w[bass.ds(first, 256), :].rearrange("(c p) n -> p c n", p=P)

            with sp.Fori(0, LAYERS) as l:
                for i in range(ITEMS_P1):
                    load(1, 0, l, i, w1p[bass.ds((l * ITEMS_P1 + i) * P, P), :])
                for i in range(ITEMS_WO):
                    load(1, 0, l, ITEMS_P1 + i, rows2(A["w_out_1"], l * D + 256 * i))
            base = LAYERS * ITEMS1
            with sp.Fori(0, LAYERS) as l:
                for i in range(ITEMS_P2):
                    load(2, base, l, i, w2p[bass.ds((l * ITEMS_P2 + i) * P, P), :])
                for i in range(ITEMS_WO):
                    load(2, base, l, ITEMS_P2 + i, rows2(A["w_out_2"], l * D + 256 * i))
                def expert(n, j, first=False):
                    for k, name in enumerate(("w1_2", "w3_2", "w2_2")):
                        i = 3 * j + k
                        slot = ring_slot(2, ITEMS_MIX2 + i)
                        if first:
                            sp.wait_ge(ring_used, l * ITEMS2 + (base + ITEMS_MIX2 + i - SLOTS + 1 + CREDIT))
                        else:
                            sp.wait_ge(up_used if k < 2 else down_used, l * EXPERTS + n - 1)
                        if k == 2:
                            src = rows2(A[name], (l * EXPERTS + n) * D_EXP)
                            dst = ring[:, slot, :].rearrange("p (c n) -> p c n", c=2)
                        else:
                            src = A[name][bass.ds((l * EXPERTS + n) * P, P), :]
                            dst = ring[:, slot, :]
                        sp.dma_start(dst, src).then_inc(slot_in[slot], 16)

                expert(0, 0, True)
                expert(1, 1, True)
                with sp.Fori(0, TURNS) as g:
                    expert(g * 2 + 2, 0)
                    expert(g * 2 + 3, 1)
            sp.wait_ge(layer_done, 4 * 2 * LAYERS)
            sp.dma_start(out[0, 0:P, :], res[:, 1, :]).then_inc(out_done, 16)
            sp.dma_start(out[0, P:SEQ, :], res[:, 2, :]).then_inc(out_done, 16)
            sp.wait_ge(out_done, 32)

        def slot_wait(pe, blk, l, i, g=None):
            slot = ring_slot(blk, i)
            before = LAYERS * uses_before(1, ITEMS1, slot) if blk == 2 else 0
            per = uses_before(blk, ITEMS1 if blk == 1 else ITEMS2, slot)
            v = l * (16 * per) + 16 * (before + uses_before(blk, i, slot) + 1)
            if g is not None:
                v = v + g * 16
            pe.wait_ge(slot_in[slot], v)
            return ring[:, slot, :]

        (xn, vA, vD, vC, qh, kh, cn, sq3) = carve([(2, D), (2, P), (2, 256), (2, 512), (4, SEQ), (4, SEQ), (3, SEQ), (3, SEQ)])
        at1 = 2048 + 256 + 512 + 1024 + 2048 + 768 + 768
        def more(at, *shape):
            n = int(np.prod(shape))
            v = arena[:, at:at + n]
            if len(shape) == 2:
                v = v.rearrange("p (a b) -> p a b", b=shape[1])
            if len(shape) == 3:
                v = v.rearrange("p (a b c) -> p a b c", b=shape[1], c=shape[2])
            assert at + n <= AR, at + n
            return v, at + n
        s1, at1 = more(at1, 2, 4, T)
        pT1, at1 = more(at1, 3, 4 * P)
        yT, at1 = more(at1, KC, SEQ)
        sg, at1 = more(at1, KC, SEQ)
        u1 = arena[:, 0:1024].rearrange("p (a b) -> p a b", a=4)
        u2 = arena[:, 1024:1536].rearrange("p (a b) -> p a b", a=4)
        sp1 = projT[:, 0:4, 0:SEQ]
        sp2 = projT[:, 4:8, 0:P]
        l1 = projT[:, 7:11, 0:SEQ] if False else projT[:, 8:12, 0:SEQ]
        l2 = projT[:, 12:14, :].rearrange("p a b -> p (a b)")[:, 0:512].rearrange("p (a b) -> p a b", a=4)
        ysq = projT[:, 0:8, 0:SEQ]
        yrs = projT[:, 8:12, 0:SEQ]

        cv, a2 = more(0, 12, T)
        gcb, a2 = more(a2, 4, T)
        btb, a2 = more(a2, 4, T)
        ebc, a2 = more(a2, 4, T)
        gsm, a2 = more(a2, T)
        gtmp, a2 = more(a2, T)
        cols, a2 = more(a2, 3, P)
        kN, a2 = more(a2, 4, P)
        vN, a2 = more(a2, 4, P)
        dif, a2 = more(a2, 4, P)
        atT, a2 = more(a2, 4, P)
        uT, a2 = more(a2, 4, P)
        lT, a2 = more(a2, 4, P)
        lS, a2 = more(a2, 4, P)
        yU, a2 = more(a2, 4, P)
        yL, a2 = more(a2, 4, P)
        pP, a2 = more(a2, 4, P)
        rr, a2 = more(a2, 4, P)
        vn, a2 = more(a2, 4, P)
        kd, a2 = more(a2, 4, P)
        st, a2 = more(a2, 4, P)
        end2 = a2
        mixT = hT
        vS, a3 = more(0, 3, 512)
        sc, a3 = more(a3, T)
        wk, a3 = more(a3, T)
        mk, a3 = more(a3, T)
        rl, a3 = more(a3, 4, T)
        s2, a3 = more(a3, 2, 4, T)
        pT2, a3 = more(a3, 3, 4 * P)
        h2T = projT[:, 0:KC, :]
        yacc = projT[:, 8:16, :]
        hid = projT[:, 16:20, :]
        e1b = projT[:, 20:24, :]
        cbb = projT[:, 24:26, :]
        comb2f, _ = more(1300, (EXPERTS // 2) * T)
        comb2 = comb2f.rearrange("p (g t) -> p g t", t=T)
        combT = projT[0:EXPERTS, 27, :]
        rtmp = arena[:, end2 - 1024:end2 - 1024 + T]
        bcones4 = ones[0:4, :]
        junk = arena[:, end2 - D:end2]
        lg = arena[:, 0:3 * 400].rearrange("p (t n) -> p t n", n=400)

        def prm1(name):
            lo, hi = P1[name]
            return prm[:, lo:hi]

        def prm2(name):
            lo, hi = P2[name]
            return prm[:, lo:hi]

        rstd = small[:, 0:4]
        ssum = small[:, 4:8]
        mx = small[:, 8:16]
        rsum = small[:, 16:24]
        sinkn = small[:, 24:32]
        eps6 = small[:, 32:33]
        eps5 = small[:, 33:34]
        nega = small[:, 34:35]
        lnm = small[:, 36:40]
        lnv = small[:, 40:44]
        kdf = small[:, 44:48]
        neg_e = small[:, 48:60]
        max8 = small[:, 60:68]
        ssq = small[:, 68:72]
        wi = small[:, 72:96]
        elast = small[:, 96:108]
        ecol = small[:, 108:120]

        xy, ax = more(1300, GROUPS, D)
        xg, ax = more(ax, KC, P)
        xselT, ax = more(ax, GROUPS, T)
        XSELT = ax - GROUPS * T
        xsel, ax = more(ax, 3, P)
        xe, ax = more(ax, 2, 256)
        xh, ax = more(ax, 2, 256)
        xhT, ax = more(ax, 2, 256)
        xcg, ax = more(ax, PER_GROUP)
        flag = ctx.enter_context(nc.sbuf_tensor("flag", [P, 1], I32))

        def branch(eng):
            eng.wait_ge(s("m_flag"), 1)
            return eng.value_load(flag[0:1, 0:1], min_val=0, max_val=1)

        def bc(ap, n, axis):
            shape = list(ap.shape)
            shape.insert(axis, n)
            return ap.unsqueeze(axis).broadcast_to(shape)

        JOBS1 = [("swa", 1), ("swa", 2), ("mla", 1), ("mla", 2)]
        JOBS2 = [("dsa", t, half) for t in (0, 1, 2) for half in (0, 1)]

        def job_keys(job):
            t = job[1]
            first = COL[1] if job[0] != "dsa" else 0
            tiles = range(1 if job[0] != "dsa" else 0, t + 1)
            return first, COL[t] + ROWS[t] - first, tiles

        def job_qk(job, h):
            t = job[1]
            first, nk, _ = job_keys(job)
            qc = slice(COL[t], COL[t] + ROWS[t])
            kcols = slice(first, first + nk)
            r = slice(64 * (h % 2), 64 * (h % 2) + 64)
            if job[0] == "swa":
                return projT[r, SQ + h // 2, qc], projT[r, SK + h // 2, kcols]
            if job[0] == "mla":
                return (qh[0:96, h, COL[t] - META:COL[t] - META + P], kh[0:96, h, 0:nk])
            c = 2 * job[2] + h // 2
            return projT[r, AQ + c, qc], projT[r, AK + c, kcols]

        def job_v(job, h, kt):
            n = ROWS[kt]
            if job[0] == "swa":
                return vA[0:n, kt - 1, 64 * (h // 2):64 * (h // 2) + 64]
            if job[0] == "mla":
                return vC[0:n, kt - 1, P * h + 64:P * h + P]
            c = 256 * job[2] + 64 * h
            return vS[0:n, kt, c:c + 64]

        def pe_scores(pe, jobs, j):
            job = jobs[j]
            nk = job_keys(job)[1]
            if j:
                pe.wait_ge(s("stt_done"), j)
            for h in range(4):
                q, k = job_qk(job, h)
                mm = pe.matmul(ps[0:ROWS[job[1]], h, 0:nk], q, k, start=True, stop=True)
            mm.then_inc(s("s_ready"), 1)

        def pe_attend(pe, jobs, j, ready=None):
            for jj in range(j, j + 1):
                job = jobs[jj]
                rows = ROWS[job[1]]
                first, nk, tiles = job_keys(job)
                sbuf = s1 if job[0] != "dsa" else s2
                pTx = pT1 if job[0] != "dsa" else pT2
                pe.wait_ge(s("p_ready"), jj + 1)
                if jj:
                    pe.wait_ge(s("pt_evicted"), jj)
                for kt in tiles:
                    c0 = COL[kt] - first
                    for h in range(4):
                        tr = pe.transpose(ps[0:ROWS[kt], 4 + kt, h * rows:(h + 1) * rows],
                                          sbuf[0:rows, jj % 2, h, c0:c0 + ROWS[kt]], ident[0:rows, 0:rows])
                tr.then_inc(s("pt_done"), 1)
                pe.wait_ge(s("pt_evicted"), jj + 1)
                if jj >= 2:
                    pe.wait_ge(s("o_evicted"), jj - 1)
                for h in range(4):
                    o = ps[64 * (h % 2):64 * (h % 2) + 64, 7,
                           256 * (jj % 2) + P * (h // 2):256 * (jj % 2) + P * (h // 2) + rows]
                    for kt in tiles:
                        mm = pe.matmul(o, job_v(job, h, kt), pTx[0:ROWS[kt], kt, h * rows:(h + 1) * rows],
                                       start=(kt == tiles[0]), stop=(kt == tiles[-1]))
                mm.then_inc(s("o_done"), 1)

        def vec_mask(v, V, jobs, j):
            job = jobs[j]
            rows = ROWS[job[1]]
            _, nk, _ = job_keys(job)
            sbuf = (s1 if job[0] != "dsa" else s2)[0:rows, j % 2, :, 0:nk]
            scale = {"swa": 64, "mla": 96, "dsa": 64}[job[0]] ** -0.5
            v.wait_ge(s("s_ready"), j + 1)
            if job[0] == "dsa":
                mask = mk[0:rows, 0:nk]
            else:
                mask = const(job[0] + "_mask")[:, 2 * P - nk:2 * P]
            V(v.scalar_tensor_tensor(out=sbuf, in0=ps[0:rows, 0:4, 0:nk], scalar=scale, in1=bc(mask, 4, 1),
                                     op0=ALU.mult, op1=ALU.add), s("stt_done"))
            k = slice(4 * (j % 2), 4 * (j % 2) + 4)
            V(v.tensor_reduce(mx[0:rows, k], sbuf, AX, ALU.max))
            if job[0] == "swa":
                V(v.tensor_tensor(mx[:, k], mx[:, k], prm1("sinks"), ALU.max))
            V(v.tensor_scalar(mx[0:rows, k], mx[0:rows, k], -1.0, None, ALU.mult))
            V(v.tensor_tensor(sinkn[:, k], mx[:, k], prm1("sinks") if job[0] == "swa" else mx[:, k], ALU.add)
              if job[0] == "swa" else v.tensor_copy(sinkn[0:rows, k], mx[0:rows, k]), s("nm_ready"))

        def act_exp(a, L, jobs, j):
            job = jobs[j]
            rows = ROWS[job[1]]
            _, nk, _ = job_keys(job)
            sbuf = s1 if job[0] != "dsa" else s2
            a.wait_ge(s("nm_ready"), j + 1)
            k0 = 4 * (j % 2)
            if job[0] == "swa":
                L(a.activation(sinkn[:, k0:k0 + 4], sinkn[:, k0:k0 + 4], ACT.Exp))
            for h in range(4):
                L(a.activation(sbuf[0:rows, j % 2, h, 0:nk], sbuf[0:rows, j % 2, h, 0:nk], ACT.Exp,
                               bias=mx[0:rows, k0 + h:k0 + h + 1], accum_out=rsum[0:rows, k0 + h:k0 + h + 1]),
                  s("exp_done") if h == 3 else None)

        def vec_norm(v, V, jobs, j):
            job = jobs[j]
            rows = ROWS[job[1]]
            _, nk, _ = job_keys(job)
            sbuf = (s1 if job[0] != "dsa" else s2)[0:rows, j % 2, :, 0:nk]
            k = slice(4 * (j % 2), 4 * (j % 2) + 4)
            v.wait_ge(s("exp_done"), j + 1)
            if job[0] == "swa":
                V(v.tensor_tensor(rsum[:, k], rsum[:, k], sinkn[:, k], ALU.add))
            V(v.reciprocal(rsum[0:rows, k], rsum[0:rows, k]))
            V(v.tensor_tensor(sbuf, sbuf, bc(rsum[0:rows, k], nk, 2), ALU.mult), s("p_ready"))

        def act_evict(a, L, jobs, j):
            job = jobs[j]
            rows = ROWS[job[1]]
            _, _, tiles = job_keys(job)
            pTx = pT1 if job[0] != "dsa" else pT2
            a.wait_ge(s("pt_done"), j + 1)
            if 0 in tiles:
                L(a.activation(pTx[0:META, 0, 0:4 * rows], ps[0:META, 4, 0:4 * rows], ACT.Copy),
                  s("pt_evicted") if len(tiles) == 1 else None)
            if tiles[-1] > 0:
                L(a.activation(pTx[:, 1:tiles[-1] + 1, :], ps[:, 5:5 + tiles[-1], :], ACT.Copy), s("pt_evicted"))
            a.wait_ge(s("o_done"), j + 1)
            o = ps[:, 7, 256 * (j % 2):256 * (j % 2) + 256].rearrange("p (a b) -> p a b", a=2)[:, :, 0:rows]
            c0 = COL[job[1]]
            if job[0] == "dsa":
                c = 4 + 2 * job[2]
                dst = mixT[:, c:c + 2, c0:c0 + rows]
            else:
                c = 0 if job[0] == "swa" else 4
                dst = yT[:, c:c + 2, c0 - META:c0 - META + rows]
            L(a.activation(dst, o, ACT.Copy), s("o_evicted"))

        def rsqrt_act(a, L, dst, src, scale, eps, last):
            L(a.activation(dst, src, ACT.Ln, bias=eps, scale=scale))
            L(a.activation(dst, dst, ACT.Exp, scale=-0.5), last)

        @block.tensor
        def _(pe):
            pe.sem_inc(ring_used, CREDIT)
            pe.wait_ge(start_in, 16 * 4)
            pe.wait_ge(tables_done, 2)

            def project(blk, l, n, ncols, c0):
                pe.wait_ge(s("ht_ready"), KC)
                for j in range(n):
                    w = slot_wait(pe, blk, l, j // 2) if j % 2 == 0 else ring[:, ring_slot(blk, j // 2), :]
                    w = w.rearrange("p (c k m) -> p c k m", c=2, k=KC)
                    if j >= 4:
                        pe.wait_ge(s("proj_ev_vec" if j % 2 else "proj_ev_act"), (j - 4) // 2 + 1)
                    for k in range(KC):
                        mm = pe.matmul(ps[:, 4 + j % 4, 0:ncols], w[:, j % 2, k, :], hT[:, k, c0:c0 + ncols],
                                       start=(k == 0), stop=(k == KC - 1))
                    mm.then_inc(s("proj_done"), 1)
                    if j % 2 == 1 or j == n - 1:
                        pe.wait_ge(s("proj_done"), j + 1)
                        pe.sem_inc(ring_used, 1)
                pe.wait_ge(s("proj_ev_act"), (n + 1) // 2)
                pe.wait_ge(s("proj_ev_vec"), n // 2)

            def project_out(blk, l, tiles, src, first_item):
                for i in range(ITEMS_WO):
                    w = slot_wait(pe, blk, l, first_item + i).rearrange("p (c n) -> p c n", c=2)
                    for c in range(2):
                        k = 2 * i + c
                        for t in tiles:
                            for half in range(2):
                                c0 = COL[t] - (META if blk == 1 else 0)
                                mm = pe.matmul(ps[0:ROWS[t], 2 * (t - tiles[0]) + half, :],
                                               src[:, k, c0:c0 + ROWS[t]], w[:, c, 512 * half:512 * half + 512],
                                               start=(k == 0), stop=(k == KC - 1))
                    mm.then_inc(s("out_ready"), 1)
                    pe.wait_ge(s("out_ready"), i + 1)
                    pe.sem_inc(ring_used, 1)

            with pe.Fori(0, LAYERS) as l:
                pe.wait_ge(s("xn_ready"), 2)
                for k in range(KC):
                    if k >= 4:
                        pe.wait_ge(s("ht_ready"), k - 3)
                    for t in range(2):
                        tr = pe.transpose(ps[:, k % 4, t * P:(t + 1) * P], xn[:, t, k * P:(k + 1) * P], ident)
                    tr.then_inc(s("ht_done"), 1)
                project(1, l, N1, SEQ, META)

                for t in range(2):
                    cs = slice(COL[t + 1], COL[t + 1] + P)
                    pe.transpose(ps[:, 5, t * P:(t + 1) * P], projT[:, SV, cs], ident)
                    for c in range(2):
                        tr = pe.transpose(ps[:, 6, (2 * t + c) * P:(2 * t + c + 1) * P], projT[:, DV + c, cs], ident)
                tr.then_inc(s("v_done"), 1)
                pe.wait_ge(s("mla_sq"), 1)
                for c in range(2):
                    pe.matmul(ps[:, 0, 0:SEQ], ones, sq3[:, c, :], start=(c == 0), stop=(c == 1))
                pe.matmul(ps[:, 0, SEQ:2 * SEQ], ones, sq3[:, 2, :], start=True, stop=True).then_inc(s("mla_ss"), 1)
                pe.wait_ge(s("mla_n"), 1)
                pe.wait_ge(s("v_evicted"), 1)
                uq = prm1("w_uq").rearrange("p (c n) -> p c n", c=2)
                for h in range(4):
                    for c in range(2):
                        pe.matmul(ps[0:96, h, 0:SEQ], uq[:, c, 96 * h:96 * h + 96], cn[:, c, :],
                                  start=(c == 0), stop=(c == 1))
                for h in range(4):
                    mm = pe.matmul(ps[0:64, 4 + h, 0:SEQ], prm1("w_ukv")[:, P * h:P * h + 64], cn[:, 2, :],
                                   start=True, stop=True)
                mm.then_inc(s("mla_qk"), 1)
                pe.wait_ge(s("mla_qh"), 1)
                for t in range(2):
                    mm = pe.matmul(ps[:, t, :], cn[:, 2, t * P:(t + 1) * P], prm1("w_ukv"), start=True, stop=True)
                for h in range(2):
                    pe.matmul(ps[64:96, 2 + h, :], const("rot96")[0:96, :], qh[0:96, 2 * h:2 * h + 2, :],
                              start=True, stop=True)
                pe.wait_ge(s("mla_kh"), 1)
                pe.matmul(ps[64:96, 4, 0:SEQ], const("rot96")[0:96, :], projT[0:96, MKR, META:T],
                          start=True, stop=True).then_inc(s("mla_rot"), 1)
                pe.wait_ge(s("mla_rope"), 1)
                pe.wait_ge(s("mla_v"), 1)
                pe_scores(pe, JOBS1, 0)
                for j in range(len(JOBS1)):
                    if j + 1 < len(JOBS1):
                        pe_scores(pe, JOBS1, j + 1)
                    pe_attend(pe, JOBS1, j)

                pe.wait_ge(s("stt_done"), len(JOBS1))
                pe.wait_ge(s("o_evicted"), len(JOBS1))
                for kt in (1, 2):
                    for h in range(4):
                        r = slice(64 * (h % 2), 64 * (h % 2) + 64)
                        mm = pe.matmul(ps[:, 4 * (kt - 1) + h, 0:SEQ - P * (kt - 1)],
                                       projT[r, DK + h // 2, COL[kt]:COL[kt] + P],
                                       projT[r, DQ + h // 2, COL[kt]:T], start=True, stop=True)
                mm.then_inc(s("sb_z"), 1)
                pe.wait_ge(s("sb_sp"), 1)
                for h in range(4):
                    pe.matmul(ps[:, h, 0:SEQ], tri, sp1[:, h, :], start=True, stop=False)
                    pe.matmul(ps[:, h, P:SEQ], ones, sp2[:, h, :], start=False, stop=True)
                    mm = pe.matmul(ps[:, 4 + h, 0:P], tri, sp2[:, h, :], start=True, stop=True)
                mm.then_inc(s("sb_r"), 1)
                pe.wait_ge(s("sb_am"), 1)
                for h in range(4):
                    o = ps[64 * (h % 2):64 * (h % 2) + 64, h // 2, :]
                    pe.matmul(o[:, 0:SEQ], vD[:, 0, 64 * h:64 * h + 64], sp1[:, h, :], start=True, stop=False)
                    mm = pe.matmul(o[:, P:SEQ], vD[:, 1, 64 * h:64 * h + 64], sp2[:, h, :], start=False, stop=True)
                mm.then_inc(s("sb_o"), 1)

                pe.wait_ge(s("y_sq"), 1)
                for g in range(4):
                    for c in range(2):
                        mm = pe.matmul(ps[:, 4 + g, 0:SEQ], ones, ysq[:, 2 * g + c, :], start=(c == 0), stop=(c == 1))
                mm.then_inc(s("y_ss"), 1)
                pe.wait_ge(s("y_ready"), 1)
                project_out(1, l, (1, 2), yT, ITEMS_P1)
                new_layer(pe, l, 0, 0)

            with pe.Fori(0, LAYERS) as l:
                for k in range(KC):
                    if k >= 4:
                        pe.wait_ge(s("ht_ready"), k - 3)
                    for t in range(3):
                        tr = pe.transpose(ps[:, k % 4, COL[t]:COL[t] + ROWS[t]],
                                          res[0:ROWS[t], t, k * P:(k + 1) * P], ident[0:ROWS[t], 0:ROWS[t]])
                    tr.then_inc(s("ht_done"), 1)
                project(2, l, N2, T, 0)

                pe.wait_ge(s("g_scan"), 1)
                for h in range(4):
                    pe.matmul(ps[:, h, 0:T], const("sel")[0:4, h * P:(h + 1) * P], gsm[0:4, :], start=True, stop=True)
                    mm = pe.matmul(ps[:, 4 + h, 0:T], const("selb")[32:36, h * P:(h + 1) * P], gsm[32:36, :],
                                   start=True, stop=True)
                mm.then_inc(s("g_bc"), 1)
                pe.wait_ge(s("g_bcev"), 2)
                for t in range(3):
                    tr = pe.transpose(ps[0:ROWS[t], 0, t * P:(t + 1) * P], gsm[:, COL[t]:COL[t] + ROWS[t]], ident)
                tr.then_inc(s("g_cols"), 1)

                for j in range(8):
                    pe.wait_ge(s("cv_sq"), j // 4 + 1)
                    if j >= 4:
                        pe.wait_ge(s("cv_rs"), 1)
                    mm = pe.matmul(ps[:, 4 + j % 4, 0:T], ones, projT[:, j, :], start=True, stop=True)
                    if j % 4 == 3:
                        mm.then_inc(s("cv_ss"), 1)
                pe.wait_ge(s("cv_norm"), 1)
                pe.wait_ge(s("g_colsev"), 1)

                lev = 0
                for t in range(3):
                    n = ROWS[t]
                    cs = slice(COL[t], COL[t] + n)
                    if t:
                        pe.wait_ge(s("d_stv"), t)
                        pe.wait_ge(s("d_oev"), t)
                    for h in range(4):
                        pe.transpose(ps[0:n, 0, h * P:(h + 1) * P], cv[:, 4 + h, cs], ident)
                        tr = pe.transpose(ps[0:n, 1, h * P:(h + 1) * P], cv[:, 8 + h, cs], ident)
                    tr.then_inc(s("kv_done"), 1)
                    for h in range(4):
                        pe.matmul(ps[0:n, 2, h * n:(h + 1) * n], cv[:, 4 + h, cs], cv[:, 4 + h, cs], start=True, stop=True)
                        mm = pe.matmul(ps[0:n, 3, h * n:(h + 1) * n], cv[:, 4 + h, cs], cv[:, h, cs], start=True, stop=True)
                    mm.then_inc(s("gq_done"), 1)
                    pe.wait_ge(s("d_u"), t + 1)
                    pe.wait_ge(s("kv_ev"), t + 1)
                    for h in range(4):
                        tr = pe.transpose(ps[0:n, 0, h * n:(h + 1) * n], uT[0:n, h, 0:n], ident[0:n, 0:n])
                    tr.then_inc(s("d_lt"), 1)
                    nlev = n.bit_length() - 2
                    for i in range(nlev):
                        pe.wait_ge(s("d_ls"), lev + 1)
                        pe.wait_ge(s("d_y"), lev + t + 1)
                        for h in range(4):
                            mm = pe.matmul(ps[0:n, 4, h * n:(h + 1) * n], lS[0:n, h, 0:n], yU[0:n, h, 0:n],
                                           start=True, stop=True)
                        mm.then_inc(s("d_p"), 1)
                        pe.wait_ge(s("d_pev"), lev + 1)
                        for h in range(4):
                            mm = pe.matmul(ps[0:n, 5, h * n:(h + 1) * n], yL[0:n, h, 0:n], pP[0:n, h, 0:n],
                                           start=True, stop=True)
                            if i < nlev - 1:
                                mm = pe.matmul(ps[0:n, 6, h * n:(h + 1) * n], pP[0:n, h, 0:n], yL[0:n, h, 0:n],
                                               start=True, stop=True)
                        mm.then_inc(s("d_q"), 1)
                        lev += 1
                    if t:
                        for h in range(4):
                            mm = pe.matmul(ps[0:n, 1, h * P:(h + 1) * P], cv[:, 4 + h, cs], st[:, h, :],
                                           start=True, stop=True)
                        mm.then_inc(s("d_ks"), 1)
                    pe.wait_ge(s("d_r"), t + 1)
                    pe.wait_ge(s("d_y"), lev + t + 1)
                    for h in range(4):
                        mm = pe.matmul(ps[0:n, 2, h * P:(h + 1) * P], yU[0:n, h, 0:n], rr[0:n, h, :], start=True, stop=True)
                    mm.then_inc(s("d_vn"), 1)
                    pe.wait_ge(s("d_vnev"), t + 1)
                    for h in range(4):
                        o = ps[:, 3, h * n:(h + 1) * n]
                        if t:
                            pe.matmul(o, st[:, h, :], ebc[:, h, cs], start=True, stop=False)
                        mm = pe.matmul(o, vn[0:n, h, :], atT[0:n, h, 0:n], start=(t == 0), stop=True)
                    mm.then_inc(s("d_o"), 1)
                    if t < 2:
                        pe.wait_ge(s("d_kd"), t + 1)
                        for h in range(4):
                            mm = pe.matmul(ps[:, 7, h * P:(h + 1) * P], kd[0:n, h, :], vn[0:n, h, :],
                                           start=True, stop=True)
                        mm.then_inc(s("d_st"), 1)
                pe.wait_ge(s("od_sq"), 1)
                for h in range(4):
                    mm = pe.matmul(ps[:, h, 0:T], ones, projT[:, h, :], start=True, stop=True)
                mm.then_inc(s("od_ss"), 1)

                pe.wait_ge(s("od_rs"), 1)
                for i, c in enumerate(ROPE_CHUNKS):
                    if i >= 4:
                        pe.wait_ge(s("rp_ready"), i - 3)
                    pe.matmul(ps[:, 4 + i % 4, 0:T], const("rot"), projT[:, c, :], start=True, stop=True)\
                        .then_inc(s("rp_done"), 1)
                pe.wait_ge(s("rp_ready"), len(ROPE_CHUNKS))
                for t in range(3):
                    for c in range(4):
                        tr = pe.transpose(ps[0:ROWS[t], 4 + t, c * P:(c + 1) * P], projT[:, AV + c, COL[t]:COL[t] + ROWS[t]],
                                          ident)
                tr.then_inc(s("v_done"), 1)
                pe.wait_ge(s("v_evicted"), 1)

                nix = 0
                for j, job in enumerate(JOBS2):
                    t = job[1]
                    if job[2] == 0 and t > 0:
                        for half in range(2):
                            nk = COL[t] + ROWS[t]
                            pe.wait_ge(s("stt_done"), j)
                            if nix:
                                pe.wait_ge(s("ix_relu"), nix)
                            for h in range(4):
                                r = slice(64 * (h % 2), 64 * (h % 2) + 64)
                                mm = pe.matmul(ps[0:ROWS[t], h, 0:nk],
                                               projT[r, IQ + 2 * half + h // 2, COL[t]:COL[t] + ROWS[t]],
                                               projT[r, IK, 0:nk], start=True, stop=True)
                            mm.then_inc(s("ix_s"), 1)
                            nix += 1
                        pe.wait_ge(s("ix_relu"), nix)
                    pe_scores(pe, JOBS2, j)
                    pe_attend(pe, JOBS2, j)
                pe.wait_ge(s("o_evicted"), len(JOBS2))
                pe.wait_ge(s("od_ready"), 1)
                project_out(2, l, (0, 1, 2), mixT, ITEMS_P2)

                pe.wait_ge(s("ln_done"), 3)
                for k in range(KC):
                    if k >= 2:
                        pe.wait_ge(s("m_htev"), k - 1)
                    for t in range(3):
                        tr = pe.transpose(ps[:, 6 + k % 2, COL[t]:COL[t] + ROWS[t]],
                                          res[0:ROWS[t], t, :].rearrange("p (m k) -> p k m", k=KC)[:, k, :],
                                          ident[0:ROWS[t], 0:ROWS[t]])
                    tr.then_inc(s("m_ht"), 1)
                pe.wait_ge(s("m_htev"), KC)
                wr = prm2("wr").rearrange("p (k n) -> p k n", k=KC)
                for t in range(3):
                    for k in range(KC):
                        mm = pe.matmul(ps[0:ROWS[t], 6, 64 * t:64 * t + 36], h2T[:, k, COL[t]:COL[t] + ROWS[t]], wr[:, k, :],
                                       start=(k == 0), stop=(k == KC - 1))
                mm.then_inc(s("m_lg"), 1)
                pe.wait_ge(s("m_comb"), 3)
                for t in range(3):
                    tr = pe.transpose(ps[0:EXPERTS, 7, COL[t]:COL[t] + ROWS[t]], lg[0:ROWS[t], t, 256:288],
                                      ident[0:ROWS[t], 0:ROWS[t]])
                for t in range(3):
                    n = ROWS[t]
                    for u in range(t + 1):
                        m = ROWS[u]
                        pe.matmul(ps[0:n, 6, 256 + 8 * t:260 + 8 * t], const("strict" if u == t else "ones")[0:m, 0:n],
                                  lg[0:m, u, 52:56], start=(u == 0), stop=(u == t))
                for t in range(3):
                    mm = pe.matmul(ps[:, 6, 288:292], ones[0:ROWS[t], :], lg[0:ROWS[t], t, 52:56],
                                   start=(t == 0), stop=(t == 2))
                mm.then_inc(s("m_combT"), 1)


                def expert_wait(k, half, j):
                    slot = ring_slot(2, ITEMS_MIX2 + 3 * j + k)
                    before = LAYERS * uses_before(1, ITEMS1, slot) + uses_before(2, ITEMS_MIX2, slot)
                    per = uses_before(2, ITEMS2, slot)
                    pe.wait_ge(slot_in[slot], l * (16 * per) + half * 16 + 16 * (before + 1))
                    return slot

                def up_all(n, j, half):
                    w1 = ring[:, expert_wait(0, half, j), :].rearrange("p (k n) -> p k n", k=KC)
                    pe.wait_ge(s("m_cb"), n + 1)
                    pe.matmul(ps[:, 4, 0:T], const("sel2")[0:2, j * P:(j + 1) * P],
                              comb2f[0:2, bass.ds(half * T, T)] if not isinstance(half, int) else
                              comb2f[0:2, half * T:half * T + T], start=True, stop=True)
                    w3 = ring[:, expert_wait(1, half, j), :].rearrange("p (k n) -> p k n", k=KC)
                    for f in range(2):
                        pe.wait_ge(s("m_hid"), n * 2 + (f + 1))
                        for k in range(KC):
                            pe.matmul(ps[:, f, 0:T], w1[:, k, P * f:P * f + P], h2T[:, k, :],
                                      start=(k == 0), stop=(k == KC - 1))
                        for k in range(KC):
                            mm = pe.matmul(ps[:, 2 + f, 0:T], w3[:, k, P * f:P * f + P], h2T[:, k, :],
                                           start=(k == 0), stop=(k == KC - 1))
                        mm.then_inc(s("m_up"), 1)
                    pe.wait_ge(s("m_up"), n * 2 + 2)
                    pe.sem_inc(up_used, 1)

                def down_all(n, j, half):
                    w = ring[:, expert_wait(2, half, j), :].rearrange("p (c n) -> p c n", c=2)
                    pe.wait_ge(s("m_hid"), n * 2 + 4)
                    for d in range(KC):
                        ago = 3 if d > 2 else (2, 2, 5)[d]
                        pe.wait_ge(s("m_yadd"), n * KC + (d - ago + 1 + 3))
                        for f in range(2):
                            mm = pe.matmul(ps[:, 5 + d % 3, 0:T], w[:, f, P * d:P * d + P], hid[:, 2 * j + f, :],
                                           start=(f == 0), stop=(f == 1))
                        mm.then_inc(s("m_y"), 1)
                    pe.wait_ge(s("m_y"), n * KC + KC)
                    pe.sem_inc(down_used, 1)

                def experts_all():
                    pe.wait_ge(s("cin"), 16)
                    up_all(0, 0, 0)
                    with pe.Fori(0, TURNS) as g:
                        up_all(g * 2 + 1, 1, g)
                        down_all(g * 2, 0, g)
                        up_all(g * 2 + 2, 0, g + 1)
                        down_all(g * 2 + 1, 1, g)
                    up_all(EXPERTS - 1, 1, TURNS)
                    down_all(EXPERTS - 2, 0, TURNS)
                    down_all(EXPERTS - 1, 1, TURNS)
                    pe.wait_ge(s("m_yadd"), KC * EXPERTS + 3)
                    for t in range(3):
                        for d in range(KC):
                            tr = pe.transpose(ps[0:ROWS[t], 2 * t + d // 4, (d % 4) * P:(d % 4 + 1) * P],
                                              yacc[:, d, COL[t]:COL[t] + ROWS[t]], ident)
                    tr.then_inc(s("m_back"), 1)

                def gather(g):
                    pe.wait_ge(s("x_sel"), g + 1)
                    for k in range(KC):
                        for t in range(3):
                            n = ROWS[t]
                            pe.matmul(ps[:, 6 + k // 4, (k % 4) * P:(k % 4 + 1) * P],
                                      res[0:n, t, :].rearrange("p (m k) -> p k m", k=KC)[:, k, :], xsel[0:n, t, :],
                                      start=(t == 0), stop=(t == 2))
                    for t in range(3):
                        n = ROWS[t]
                        pe.transpose(ps[:, 3, COL[t]:COL[t] + n], xsel[0:n, t, :], ident[0:n, 0:n])
                    for t in range(3):
                        n = ROWS[t]
                        w = (lg[0:n, t, 256 + PER_GROUP * g:256 + PER_GROUP * (g + 1)] if isinstance(g, int)
                             else lg[0:n, t, bass.ds(g * PER_GROUP + 256, PER_GROUP)])
                        mm = pe.matmul(ps[:, 3, 288:288 + PER_GROUP], xsel[0:n, t, :], w, start=(t == 0), stop=(t == 2))
                    mm.then_inc(s("x_g"), 1)

                def up(g, e):
                    if e == 0:
                        pe.wait_ge(s("x_ge"), g + 1)
                    half = g * (PER_GROUP // 2) + e // 2
                    slot = expert_wait(0, half, e % 2)
                    expert_wait(1, half, e % 2)
                    w = ring[:, slot:slot + 2, :].rearrange("p w (k n) -> p w k n", k=KC)
                    pe.wait_ge(s("x_hid"), g * PER_GROUP + (e + 1))
                    for k in range(KC):
                        mm = pe.matmul(ps[:, e % 2, :].rearrange("p (w n) -> p w n", w=2), xg[:, k, :], w[:, :, k, :],
                                       start=(k == 0), stop=(k == KC - 1))
                    mm.then_inc(up_used, 1)

                def turn(g, e):
                    pe.wait_ge(s("x_hid"), g * PER_GROUP + (e + 3))
                    for f in range(2):
                        tr = pe.transpose(ps[:, 2, 256 * (e % 2) + P * f:256 * (e % 2) + P * (f + 1)],
                                          xh[:, e % 2, P * f:P * (f + 1)], ident)
                    tr.then_inc(s("x_t"), 1)

                def down(g, e):
                    w = ring[:, expert_wait(2, g * (PER_GROUP // 2) + e // 2, e % 2), :].rearrange("p (c n) -> p c n", c=2)
                    pe.wait_ge(s("x_te"), g * PER_GROUP + (e + 1))
                    if e == 0:
                        pe.wait_ge(s("x_ye"), g + 1)
                    for f in range(2):
                        for half in range(2):
                            mm = pe.matmul(ps[:, 4 + half, :], xhT[:, e % 2, P * f:P * (f + 1)],
                                           w[:, f, 512 * half:512 * half + 512],
                                           start=(e == 0 and f == 0), stop=(e == PER_GROUP - 1 and f == 1))
                    mm.then_inc(down_used, 1)

                def group(g, last):
                    up(g, 0)
                    for e in range(PER_GROUP):
                        if e < PER_GROUP - 1:
                            up(g, e + 1)
                        elif not last:
                            gather(g + 1)
                        turn(g, e)
                        down(g, e)

                def experts_grouped():
                    gather(0)
                    with pe.Fori(0, GROUPS - 1) as g:
                        group(g, False)
                    group(GROUPS - 1, True)
                    pe.wait_ge(s("x_ye"), GROUPS + 1)
                    for t in range(3):
                        for half in range(2):
                            for g in range(GROUPS):
                                mm = pe.matmul(ps[0:ROWS[t], 2 * t + half, :], xselT[:, g, COL[t]:COL[t] + ROWS[t]],
                                               xy[:, g, 512 * half:512 * half + 512],
                                               start=(g == 0), stop=(g == GROUPS - 1))
                    mm.then_inc(s("m_back"), 1)

                crowded = branch(pe)
                with pe.If(crowded > 0):
                    experts_all()
                with pe.Else():
                    experts_grouped()
                pe.wait_ge(s("m_back"), 1)
                pe.sem_inc(ring_used, 3 * EXPERTS)
                new_layer(pe, l, LAYERS, 1)

        @block.scalar
        def _(a):
            a.dma_start(cst[:, :], A["consts"]).then_inc(start_in, 16)
            a.dma_start(res[:, 1:3, :], A["x"][0].rearrange("(t p) d -> p t d", p=P)).then_inc(start_in, 16)
            a.dma_start(res[0:META, 0, :], A["meta_tokens_2"]).then_inc(start_in, 16)
            a.dma_start(posi[:, :], A["positions"].broadcast_to([P, SEQ])).then_inc(start_in, 16)
            a.wait_ge(seen, 1)
            a.activation(sinT, sinT, ACT.Sin).then_inc(tables_done, 1)
            a.activation(cosT, cosT, ACT.Sin).then_inc(tables_done, 1)
            a.wait_ge(tables_done, 2)

            with a.Fori(0, LAYERS) as l:
                L = Linked(a, s("act_order"))
                a.dma_start(prm[:, 0:NP1], A["params_1"][bass.ds(l * P, P), :]).then_inc(s("params_in"), 16)
                for t in (1, 2):
                    L(a.activation(yT[:, 0:4, :], res[:, t, :], ACT.Square, accum_out=ssum[:, t:t + 1]))
                rsqrt_act(a, L, rstd[:, 1:3], ssum[:, 1:3], 1.0 / D, eps6, s("rstd_ready"))
                for j in range(0, N1, 2):
                    a.wait_ge(s("proj_done"), j + 1)
                    L(a.activation(projT[:, j, META:T], ps[:, 4 + j % 4, 0:SEQ], ACT.Copy), s("proj_ev_act"))
                a.wait_ge(s("proj_ev_vec"), N1 // 2)
                L(a.activation(sq3, projT[:, MQ:MQ + 3, META:T], ACT.Square), s("mla_sq"))
                a.wait_ge(s("v_done"), 1)
                L(a.activation(vA, ps[:, 5, 0:2 * P], ACT.Copy))
                L(a.activation(vD, ps[:, 6, :], ACT.Copy), s("v_evicted"))
                a.wait_ge(s("mla_ss"), 1)
                rs = sq3[:, 0:2, :]
                L(a.activation(rs[:, 0, :], ps[:, 0, 0:SEQ], ACT.Ln, bias=eps6, scale=1.0 / 256))
                L(a.activation(rs[:, 1, :], ps[:, 0, SEQ:2 * SEQ], ACT.Ln, bias=eps6, scale=1.0 / P))
                L(a.activation(rs, rs, ACT.Exp, scale=-0.5), s("mla_rs"))
                a.wait_ge(s("mla_qk"), 1)
                L(a.activation(qh[0:96], ps[0:96, 0:4, 0:SEQ], ACT.Copy), s("mla_qh"))
                a.wait_ge(s("mla_rot"), 1)
                L(a.activation(vC, ps[:, 0:2, :], ACT.Copy), s("mla_v"))
                for j in range(len(JOBS1)):
                    if j == 0:
                        act_exp(a, L, JOBS1, 0)
                    if j + 1 < len(JOBS1):
                        act_exp(a, L, JOBS1, j + 1)
                    act_evict(a, L, JOBS1, j)
                a.wait_ge(s("sb_u"), 2)
                for u, lo in ((u1, l1), (u2, l2)):
                    L(a.activation(lo, u, ACT.Abs))
                    L(a.activation(lo, lo, ACT.Exp, scale=-1.0))
                    L(a.activation(lo, lo, ACT.Ln, bias=ones[:, 0:1]), s("sb_l"))
                a.wait_ge(s("sb_d"), 2)
                L(a.activation(sp1, u1, ACT.Exp))
                L(a.activation(sp2, u2, ACT.Exp), s("sb_a"))
                L(a.activation(sg, projT[:, GATE:GATE + KC, META:T], ACT.Exp, scale=-1.0), s("gate_exp"))
                a.wait_ge(s("sb_o"), 1)
                L(a.activation(yT[:, 6:8, :], ps[:, 0:2, 0:SEQ], ACT.Copy), s("sb_oe"))
                a.wait_ge(s("conv_ready"), 1)
                L(a.activation(ysq, yT, ACT.Square), s("y_sq"))
                a.wait_ge(s("y_ss"), 1)
                rsqrt_act(a, L, yrs, ps[:, 4:8, 0:SEQ], 1.0 / 256, eps6, s("y_rs"))
                a.wait_ge(s("out_ready"), ITEMS_WO)
                for t in (1, 2):
                    L(a.activation(xn, ps[:, 2 * t - 2:2 * t, :], ACT.Square, accum_out=ssum[:, t:t + 1])
                      if False else
                      a.activation(xn[:, t - 1, :], ps[:, 2 * t - 2:2 * t, :].rearrange("p a b -> p (a b)"), ACT.Square,
                                   accum_out=ssum[:, t:t + 1]))
                rsqrt_act(a, L, rstd[:, 1:3], ssum[:, 1:3], 1.0 / D, eps6, s("out_ss"))
                new_layer(a, l, 0, 0)

            with a.Fori(0, LAYERS) as l:
                L = Linked(a, s("act_order"))
                a.dma_start(prm[:, 0:NP2], A["params_2"][bass.ds(l * P, P), :]).then_inc(s("params_in"), 16)
                for j in range(0, N2, 2):
                    a.wait_ge(s("proj_done"), j + 1)
                    L(a.activation(projT[:, j, :], ps[:, 4 + j % 4, 0:T], ACT.Copy), s("proj_ev_act"))
                a.wait_ge(s("g_sm"), 1)
                L(a.activation(gtmp[0:4, :], gsm[0:4, :], ACT.Abs))
                L(a.activation(gtmp[0:4, :], gtmp[0:4, :], ACT.Exp, scale=-1.0))
                L(a.activation(gtmp[0:4, :], gtmp[0:4, :], ACT.Ln, bias=ones[0:4, 0:1]))
                L(a.activation(nega[0:4, :], prm2("a_log")[0:4, :], ACT.Exp))
                L(a.activation(gsm[32:36, :], projT[32:36, SM, :], ACT.Exp, scale=-1.0), s("g_ln"))
                a.wait_ge(s("g_bc"), 1)
                L(a.activation(gcb, ps[:, 0:4, 0:T], ACT.Copy), s("g_bcev"))
                L(a.activation(btb, ps[:, 4:8, 0:T], ACT.Copy), s("g_bcev"))
                L(a.activation(ebc, gcb, ACT.Exp))
                a.wait_ge(s("g_cols"), 1)
                L(a.activation(cols[0:META, 0, :], ps[0:META, 0, 0:P], ACT.Copy))
                L(a.activation(cols[:, 1:3, :], ps[:, 0, P:3 * P].rearrange("p (a b) -> p a b", a=2), ACT.Copy))
                L(a.activation(ecol[:, 4:12].rearrange("p (a b) -> p a b", a=2), cols[:, 1:3, 0:4], ACT.Exp),
                  s("g_colsev"))
                a.wait_ge(s("cv_ready"), 1)
                L(a.activation(projT[:, 0:12, :], cv, ACT.Exp, scale=-1.0), s("cv_exp"))
                a.wait_ge(s("cv_silu"), 1)
                L(a.activation(projT[:, 0:4, :], cv[:, 0:4, :], ACT.Square), s("cv_sq"))
                L(a.activation(projT[:, 4:8, :], cv[:, 4:8, :], ACT.Square), s("cv_sq"))
                L(a.activation(projT[:, 8:12, :], projT[:, NZ:NZ + 4, :], ACT.Exp, scale=-1.0), s("z_exp"))
                for i in range(2):
                    a.wait_ge(s("cv_ss"), i + 1)
                    rsqrt_act(a, L, projT[:, 4 * i:4 * i + 4, :], ps[:, 4:8, 0:T], 1.0, eps6, s("cv_rs"))
                lev = 0
                for t in range(3):
                    n = ROWS[t]
                    a.wait_ge(s("kv_done"), t + 1)
                    if t:
                        a.wait_ge(s("d_kd"), t)
                        a.wait_ge(s("d_r"), t)
                    L(a.activation(kN[0:n], ps[0:n, 0, :], ACT.Copy))
                    L(a.activation(vN[0:n], ps[0:n, 1, :], ACT.Copy), s("kv_ev"))
                    a.wait_ge(s("d_diff"), t + 1)
                    L(a.activation(kdf[0:n, :], kdf[0:n, :], ACT.Exp))
                    L(a.activation(dif[0:n, :, 0:n], dif[0:n, :, 0:n], ACT.Exp), s("d_exp"))
                    a.wait_ge(s("d_lt"), t + 1)
                    if t:
                        a.wait_ge(s("d_ls"), lev)
                    L(a.activation(lT[0:n, :, 0:n], ps[0:n, 0, 0:4 * n].rearrange("p (a b) -> p a b", a=4), ACT.Copy),
                      s("d_l"))
                    for i in range(n.bit_length() - 2):
                        a.wait_ge(s("d_p"), lev + 1)
                        L(a.activation(pP[0:n, :, 0:n], ps[0:n, 4, 0:4 * n].rearrange("p (a b) -> p a b", a=4), ACT.Copy),
                          s("d_pev"))
                        lev += 1
                    a.wait_ge(s("d_vn"), t + 1)
                    L(a.activation(vn[0:n], ps[0:n, 2, :], ACT.Copy), s("d_vnev"))
                    a.wait_ge(s("d_o"), t + 1)
                    L(a.activation(mixT[:, 0:4, COL[t]:COL[t] + n],
                                   ps[:, 3, 0:4 * n].rearrange("p (a b) -> p a b", a=4), ACT.Copy), s("d_oev"))
                a.wait_ge(s("cv_norm"), 1)
                L(a.activation(projT[:, 0:4, :], mixT[:, 0:4, :], ACT.Square), s("od_sq"))
                a.wait_ge(s("od_ss"), 1)
                rsqrt_act(a, L, projT[:, 0:4, :], ps[:, 0:4, 0:T], 1.0 / P, eps6, s("od_rs"))
                a.wait_ge(s("v_done"), 1)
                L(a.activation(vS[0:META, 0, :], ps[0:META, 4, :], ACT.Copy))
                L(a.activation(vS[:, 1:3, :], ps[:, 5:7, :], ACT.Copy), s("v_evicted"))
                nix = 0
                for j, job in enumerate(JOBS2):
                    if job[2] == 0 and job[1] > 0:
                        nk = COL[job[1]] + P
                        for half in range(2):
                            a.wait_ge(s("ix_s"), nix + 1)
                            if nix:
                                a.wait_ge(s("ix_used"), nix)
                            L(a.activation(rl[:, :, 0:nk], ps[:, 0:4, 0:nk], ACT.Relu, scale=64 ** -0.5), s("ix_relu"))
                            nix += 1
                    act_exp(a, L, JOBS2, j)
                    act_evict(a, L, JOBS2, j)
                for norm in range(2):
                    for t in range(3):
                        n = ROWS[t]
                        k = 3 * norm + t + 1
                        a.wait_ge(s("ln_mean"), k)
                        L(a.activation(junk[0:n], res[0:n, t, :], ACT.Square, bias=lnm[0:n, t:t + 1],
                                       accum_out=ssq[0:n, t:t + 1]))
                        rsqrt_act(a, L, rstd[0:n, t:t + 1], ssq[0:n, t:t + 1], 1.0 / D, eps5[0:n], s("ln_rstd"))
                    if norm:
                        break
                    for k in range(KC):
                        a.wait_ge(s("m_ht"), k + 1)
                        L(a.activation(h2T[:, k, :], ps[:, 6 + k % 2, 0:T], ACT.Copy), s("m_htev"))
                    for t in range(3):
                        n = ROWS[t]
                        a.wait_ge(s("m_e1"), t + 1)
                        L(a.activation(lg[0:n, t, 40:44], lg[0:n, t, 40:44], ACT.Exp, accum_out=lg[0:n, t, 45:46]))
                        L(a.activation(lg[0:n, t, 99:100], lg[0:n, t, 99:100], ACT.Exp), s("m_e1d"))
                    def gate_exp(n, j):
                        for f in range(2):
                            a.wait_ge(s("m_up"), n * 2 + (f + 1))
                            if f == 0:
                                a.activation(cbb[:, j, :], ps[:, 4, 0:T], ACT.Copy).then_inc(s("m_cb"), 1)
                            a.activation(e1b[:, 2 * j + f, :], ps[:, f, 0:T], ACT.Exp, scale=-1.0)\
                                .then_inc(s("m_exp"), 1)

                    def experts_all():
                        a.wait_ge(s("m_combev"), 1)
                        a.dma_start(comb_dram, combT).then_inc(s("m_combst"), 16)
                        a.wait_ge(s("m_combst"), 16)
                        a.dma_start(comb2[0:2], comb_dram.rearrange("(g j) t -> j g t", j=2)).then_inc(s("cin"), 16)
                        a.sem_inc(s("m_cb"), 1)
                        gate_exp(0, 0)
                        with a.Fori(0, TURNS) as g:
                            gate_exp(g * 2 + 1, 1)
                            gate_exp(g * 2 + 2, 0)
                        gate_exp(EXPERTS - 1, 1)

                    def exp_gate(g, e):
                        a.wait_ge(up_used, l * EXPERTS + g * PER_GROUP + (e + 1))
                        a.activation(xe[:, e % 2, :], ps[:, e % 2, 0:256], ACT.Exp, scale=-1.0).then_inc(s("x_exp"), 1)

                    def tokens_in(g):
                        a.wait_ge(s("x_g"), g + 1)
                        to = xselT[:, g, :] if isinstance(g, int) else \
                            arena[:, bass.ds(g * T + XSELT, T)]
                        a.activation(to, ps[:, 3, 0:T], ACT.Copy).then_inc(s("act_group"), 1)
                        a.activation(xg, ps[:, 6:8, :], ACT.Copy).then_inc(s("x_ge"), 1)
                        a.wait_ge(s("x_hid"), g * PER_GROUP + 2)
                        a.activation(xcg, ps[:, 3, 288:288 + PER_GROUP], ACT.Copy).then_inc(s("x_cg"), 1)

                    def group(g, last):
                        exp_gate(g, 0)
                        for e in range(PER_GROUP):
                            if e < PER_GROUP - 1:
                                exp_gate(g, e + 1)
                            elif not last:
                                tokens_in(g + 1)
                            a.wait_ge(s("x_t"), g * PER_GROUP + (e + 1))
                            a.activation(xhT[:, e % 2, :], ps[:, 2, 256 * (e % 2):256 * (e % 2) + 256], ACT.Copy)\
                                .then_inc(s("x_te"), 1)
                        a.wait_ge(down_used, l * EXPERTS + g * PER_GROUP + PER_GROUP)
                        to = xy[:, g, :] if isinstance(g, int) else arena[:, bass.ds(g * D + 1300, D)]
                        a.activation(to, ps[:, 4:6, :].rearrange("p a b -> p (a b)"), ACT.Copy).then_inc(s("x_ye"), 1)

                    def experts_grouped():
                        a.sem_inc(s("x_ye"), 1)
                        tokens_in(0)
                        with a.Fori(0, GROUPS - 1) as g:
                            group(g, False)
                        group(GROUPS - 1, True)

                    crowded = branch(a)
                    with a.If(crowded > 0):
                        experts_all()
                    with a.Else():
                        experts_grouped()
                new_layer(a, l, LAYERS, 1)

        @block.vector
        def _(v):
            MAGIC = 12582912.0
            C1, C2 = 6.28125, 0.0019353071795864769
            V0 = Linked(v, tables_vec)
            V0(v.memset(eps6, 1e-6))
            V0(v.memset(eps5, 1e-5))
            V0(v.memset(small[:, 0:32], 0.0))
            V0(v.memset(gsm, 0.0))
            v.wait_ge(start_in, 16 * 4)
            V0(v.tensor_copy(cosT, posi[:, :]))
            V0(v.tensor_scalar(cosT, cosT, const("freq"), None, ALU.mult))
            V0(v.tensor_scalar(sinT, cosT, float(1.0 / (2.0 * np.pi)), MAGIC, ALU.mult, ALU.add))
            V0(v.tensor_scalar(sinT, sinT, -MAGIC, None, ALU.add))
            V0(v.scalar_tensor_tensor(out=cosT, in0=sinT, scalar=-C1, in1=cosT, op0=ALU.mult, op1=ALU.add))
            V0(v.scalar_tensor_tensor(out=cosT, in0=sinT, scalar=-C2, in1=cosT, op0=ALU.mult, op1=ALU.add))
            V0(v.tensor_scalar(sinT, cosT, 3.1415925, -3.1415925, ALU.min, ALU.max))
            V0(v.tensor_scalar(cosT, sinT, float(np.pi / 2), None, ALU.add))
            V0(v.tensor_scalar(arena[:, 0:SEQ], cosT, float(np.pi), float(-2 * np.pi), ALU.is_gt, ALU.mult))
            V0(v.tensor_tensor(cosT, cosT, arena[:, 0:SEQ], ALU.add))
            V0(v.tensor_scalar(cosT, cosT, 3.1415925, -3.1415925, ALU.min, ALU.max), seen)

            with v.Fori(0, LAYERS) as l:
                V = Linked(v, s("vec_order"))
                v.wait_ge(s("rstd_ready"), 1)
                for t in (1, 2):
                    V(v.tensor_scalar(xn[:, t - 1, :], res[:, t, :], rstd[:, t:t + 1], None, ALU.mult), s("xn_ready"))
                v.wait_ge(s("params_in"), 16)
                for k in range(KC):
                    v.wait_ge(s("ht_done"), k + 1)
                    V(v.tensor_scalar(hT[:, k, META:T], ps[:, k % 4, 0:SEQ], prm1("g_pre")[:, k:k + 1], None, ALU.mult),
                      s("ht_ready"))
                for j in range(1, N1, 2):
                    v.wait_ge(s("proj_done"), j + 1)
                    V(v.tensor_copy(projT[:, j, META:T], ps[:, 4 + j % 4, 0:SEQ]), s("proj_ev_vec"))
                v.wait_ge(s("proj_ev_act"), (N1 + 1) // 2)
                v.wait_ge(s("mla_rs"), 1)
                rs = sq3[:, 0:2, :]
                for c in range(3):
                    g = prm1("g_q")[:, c:c + 1] if c < 2 else prm1("g_kv")
                    V(v.scalar_tensor_tensor(out=cn[:, c, :], in0=projT[:, MQ + c, META:T], scalar=g,
                                             in1=rs[:, c // 2, :], op0=ALU.mult, op1=ALU.mult),
                      s("mla_n") if c == 2 else None)
                v.wait_ge(s("mla_qk"), 1)
                V(v.tensor_copy(kh[0:64], ps[0:64, 4:8, 0:SEQ]), s("mla_kh"))
                R = slice(64, 96)
                v.wait_ge(s("mla_rot"), 1)
                tq = yT[R, 0:4, :]
                V(v.tensor_tensor(tq, ps[R, 2:4, :].rearrange("p a (b c) -> p (a b) c", b=2), bc(sinT[R], 4, 1), ALU.mult))
                V(v.tensor_tensor(qh[R], qh[R], bc(cosT[R], 4, 1), ALU.mult))
                V(v.tensor_tensor(qh[R], qh[R], tq, ALU.add))
                V(v.tensor_tensor(yT[R, 0, :], ps[R, 4, 0:SEQ], sinT[R], ALU.mult))
                V(v.tensor_tensor(yT[R, 1, :], projT[R, MKR, META:T], cosT[R], ALU.mult))
                V(v.tensor_tensor(kh[R], bc(yT[R, 0, :], 4, 1), bc(yT[R, 1, :], 4, 1), ALU.add), s("mla_rope"))
                for j in range(len(JOBS1)):
                    if j == 0:
                        vec_mask(v, V, JOBS1, 0)
                    if j + 1 < len(JOBS1):
                        vec_mask(v, V, JOBS1, j + 1)
                    vec_norm(v, V, JOBS1, j)
                cw = prm1("conv_w")
                for c in range(2):
                    y = yT[:, 2 + c, :]
                    u = sq3[:, c, :]
                    V(v.tensor_tensor(u, projT[:, CC + c, META:T], projT[:, CX + c, META:T], ALU.mult))
                    V(v.tensor_scalar(y, u, cw[:, 4 + c:5 + c], prm1("conv_b")[:, c:c + 1], ALU.mult, ALU.add))
                    for d in (1, 2):
                        k = 2 - d
                        V(v.scalar_tensor_tensor(out=y[:, d:SEQ], in0=u[:, 0:SEQ - d], scalar=cw[:, 2 * k + c:2 * k + c + 1],
                                                 in1=y[:, d:SEQ], op0=ALU.mult, op1=ALU.add))
                    V(v.tensor_tensor(y, y, projT[:, CB + c, META:T], ALU.mult))
                v.wait_ge(s("sb_z"), 1)
                V(v.tensor_scalar(u1, ps[:, 0:4, 0:SEQ], 0.125, None, ALU.mult), s("sb_u"))
                V(v.tensor_scalar(u2, ps[:, 4:8, 0:P], 0.125, None, ALU.mult), s("sb_u"))
                strict4 = bc(const("strict"), 4, 1)
                for i, (u, lo, sp_) in enumerate(((u1, l1, sp1), (u2, l2, sp2))):
                    v.wait_ge(s("sb_l"), i + 1)
                    V(v.scalar_tensor_tensor(out=sp_, in0=u, scalar=0.0, in1=lo, op0=ALU.max, op1=ALU.add))
                    V(v.tensor_tensor(sp_[:, :, 0:P], sp_[:, :, 0:P], strict4, ALU.mult), s("sb_sp") if i else None)
                v.wait_ge(s("sb_r"), 1)
                for i, (u, r) in enumerate(((u1, ps[:, 0:4, 0:SEQ]), (u2, ps[:, 4:8, 0:P]))):
                    V(v.scalar_tensor_tensor(out=u, in0=r, scalar=-1.0, in1=u, op0=ALU.mult, op1=ALU.add))
                    V(v.tensor_scalar(u, u, 0.0, None, ALU.min), s("sb_d"))
                v.wait_ge(s("sb_a"), 1)
                V(v.tensor_tensor(sp1[:, :, 0:P], sp1[:, :, 0:P], strict4, ALU.mult))
                V(v.tensor_tensor(sp2, sp2, strict4, ALU.mult), s("sb_am"))
                v.wait_ge(s("gate_exp"), 1)
                V(v.tensor_scalar(sg, sg, 1.0, None, ALU.add))
                V(v.reciprocal(sg, sg))
                V(v.tensor_tensor(sg, sg, projT[:, GATE:GATE + KC, META:T], ALU.mult))
                v.wait_ge(s("sb_oe"), 1)
                V(v.tensor_copy(small[:, 120:121], ones[:, 0:1]), s("conv_ready"))
                v.wait_ge(s("y_rs"), 1)
                for c in range(KC):
                    V(v.scalar_tensor_tensor(out=yT[:, c, :], in0=yT[:, c, :], scalar=prm1("g_grp")[:, c:c + 1],
                                             in1=yrs[:, c // 2, :], op0=ALU.mult, op1=ALU.mult))
                V(v.tensor_tensor(yT, yT, sg, ALU.mult), s("y_ready"))
                v.wait_ge(s("out_ss"), 1)
                for t in (1, 2):
                    o = ps[:, 2 * t - 2:2 * t, :].rearrange("p a b -> p (a b)")
                    V(v.scalar_tensor_tensor(out=xn[:, t - 1, :], in0=o, scalar=rstd[:, t:t + 1], in1=prm1("g_post"),
                                             op0=ALU.mult, op1=ALU.mult))
                    V(v.tensor_tensor(res[:, t, :], res[:, t, :], xn[:, t - 1, :], ALU.add), s("res_ready"))
                new_layer(v, l, 0, 0)

            with v.Fori(0, LAYERS) as l:
                V = Linked(v, s("vec_order"))
                for k in range(KC):
                    v.wait_ge(s("ht_done"), k + 1)
                    V(v.tensor_copy(hT[:, k, :], ps[:, k % 4, 0:T]), s("ht_ready"))
                for j in range(1, N2, 2):
                    v.wait_ge(s("proj_done"), j + 1)
                    V(v.tensor_copy(projT[:, j, :], ps[:, 4 + j % 4, 0:T]), s("proj_ev_vec"))
                v.wait_ge(s("proj_ev_act"), N2 // 2)
                v.wait_ge(s("params_in"), 16)
                V(v.memset(gsm, 0.0))
                V(v.tensor_scalar(gsm[0:4, :], projT[0:4, SM, :], prm2("dt")[0:4, :], None, ALU.add), s("g_sm"))
                V(v.tensor_copy(gsm[64:72, :], projT[64:72, SM, :]))
                v.wait_ge(s("g_ln"), 1)
                V(v.scalar_tensor_tensor(out=gtmp[0:4, :], in0=gsm[0:4, :], scalar=0.0, in1=gtmp[0:4, :],
                                         op0=ALU.max, op1=ALU.add))
                V(v.tensor_scalar(gtmp[0:4, :], gtmp[0:4, :], nega[0:4, :], -1.0, ALU.mult, ALU.mult))
                V(v.tensor_scalar(gsm[32:36, :], gsm[32:36, :], 1.0, None, ALU.add))
                V(v.reciprocal(gsm[32:36, :], gsm[32:36, :]))
                for t in range(3):
                    cs = slice(COL[t], COL[t] + ROWS[t])
                    V(v.tensor_tensor_scan(gsm[0:4, cs], bcones4[:, 0:ROWS[t]], gtmp[0:4, cs], 0.0, ALU.mult, ALU.add),
                      s("g_scan") if t == 2 else None)
                cw = prm2("conv_w").rearrange("p (c k) -> p c k", k=4)
                for c in range(12):
                    V(v.tensor_scalar(cv[:, c, :], projT[:, c, :], cw[:, c, 3:4], None, ALU.mult))
                    for d in (1, 2, 3):
                        V(v.scalar_tensor_tensor(out=cv[:, c, d:T], in0=projT[:, c, 0:T - d],
                                                 scalar=cw[:, c, 3 - d:4 - d], in1=cv[:, c, d:T], op0=ALU.mult, op1=ALU.add),
                          s("cv_ready") if (c, d) == (11, 3) else None)
                v.wait_ge(s("cv_exp"), 1)
                V(v.tensor_scalar(projT[:, 0:12, :], projT[:, 0:12, :], 1.0, None, ALU.add))
                V(v.reciprocal(projT[:, 0:12, :], projT[:, 0:12, :]))
                V(v.tensor_tensor(cv, cv, projT[:, 0:12, :], ALU.mult), s("cv_silu"))
                v.wait_ge(s("g_colsev"), 1)
                for t in range(3):
                    V(v.tensor_copy(elast[:, 4 * t:4 * t + 4], ebc[:, :, COL[t] + ROWS[t] - 1]))
                V(v.tensor_scalar(neg_e[:, 4:12], ecol[:, 4:12], -1.0, None, ALU.mult))
                V(v.tensor_scalar(wi[:, 8:24].rearrange("p (a b) -> p a b", a=2), cols[:, 1:3, 64:72], 8 ** -0.5, None,
                                  ALU.mult))
                v.wait_ge(s("cv_rs"), 2)
                V(v.scalar_tensor_tensor(out=cv[:, 0:4, :], in0=cv[:, 0:4, :], scalar=float(P) ** -0.5,
                                         in1=projT[:, 0:4, :], op0=ALU.mult, op1=ALU.mult))
                V(v.tensor_tensor(cv[:, 4:8, :], cv[:, 4:8, :], projT[:, 4:8, :], ALU.mult))
                V(v.tensor_tensor(ebc, ebc, cv[:, 0:4, :], ALU.mult), s("cv_norm"))
                v.wait_ge(s("z_exp"), 1)
                V(v.tensor_scalar(projT[:, 8:12, :], projT[:, 8:12, :], 1.0, None, ALU.add))
                V(v.reciprocal(projT[:, 8:12, :], projT[:, 8:12, :]))
                V(v.tensor_tensor(projT[:, NZ:NZ + 4, :], projT[:, NZ:NZ + 4, :], projT[:, 8:12, :], ALU.mult))

                lev = 0
                for t in range(3):
                    n = ROWS[t]
                    cs = slice(COL[t], COL[t] + n)

                    def psv(b, w=n):
                        return ps[0:n, b, 0:4 * w].rearrange("p (a b) -> p a b", a=4)

                    for h in range(4):
                        V(v.tensor_scalar(dif[0:n, h, 0:n], gcb[0:n, h, cs], cols[0:n, t, h:h + 1], 0.0,
                                          ALU.subtract, ALU.min))
                    V(v.tensor_tensor(kdf[0:n, :], gcb[0:n, :, COL[t] + n - 1], cols[0:n, t, 0:4], ALU.subtract), s("d_diff"))
                    v.wait_ge(s("d_exp"), t + 1)
                    V(v.tensor_tensor(dif[0:n, :, 0:n], dif[0:n, :, 0:n], bc(const("upper")[0:n, 0:n], 4, 1), ALU.mult))
                    v.wait_ge(s("gq_done"), t + 1)
                    if t:
                        v.wait_ge(s("d_o"), t)
                    V(v.tensor_tensor(atT[0:n, :, 0:n], psv(3), dif[0:n, :, 0:n], ALU.mult))
                    V(v.tensor_tensor(uT[0:n, :, 0:n], psv(2), dif[0:n, :, 0:n], ALU.mult))
                    V(v.tensor_tensor(uT[0:n, :, 0:n], uT[0:n, :, 0:n], btb[0:n, :, cs], ALU.mult))
                    V(v.tensor_tensor(uT[0:n, :, 0:n], uT[0:n, :, 0:n], bc(const("strict")[0:n, 0:n], 4, 1), ALU.mult),
                      s("d_u"))
                    v.wait_ge(s("d_l"), t + 1)
                    levu = const("lev_u").rearrange("p (i m) -> p i m", m=P)
                    levl = const("lev_l").rearrange("p (i m) -> p i m", m=P)
                    idn = bc(ident[0:n, 0:n], 4, 1)
                    V(v.tensor_tensor(yU[0:n, :, 0:n], uT[0:n, :, 0:n], bc(levu[0:n, 0, 0:n], 4, 1), ALU.mult))
                    V(v.tensor_tensor(yU[0:n, :, 0:n], idn, yU[0:n, :, 0:n], ALU.subtract))
                    V(v.tensor_tensor(yL[0:n, :, 0:n], lT[0:n, :, 0:n], bc(levl[0:n, 0, 0:n], 4, 1), ALU.mult))
                    V(v.tensor_tensor(yL[0:n, :, 0:n], idn, yL[0:n, :, 0:n], ALU.subtract), s("d_y"))
                    nlev = n.bit_length() - 2
                    for i in range(nlev):
                        v.wait_ge(s("d_q"), lev + 1)
                        if i < nlev - 1:
                            V(v.tensor_tensor(yL[0:n, :, 0:n], yL[0:n, :, 0:n], psv(6), ALU.subtract))
                        V(v.tensor_tensor(yU[0:n, :, 0:n], yU[0:n, :, 0:n], psv(5), ALU.subtract), s("d_y"))
                        lev += 1
                    v.wait_ge(s("kv_ev"), t + 1)
                    beta = bc(cols[0:n, t, 32:36], P, 2)
                    if t:
                        v.wait_ge(s("d_ks"), t)
                        V(v.tensor_tensor(rr[0:n], psv(1, P), bc(neg_e[0:n, 4 * t:4 * t + 4], P, 2), ALU.mult))
                        V(v.tensor_tensor(rr[0:n], rr[0:n], vN[0:n], ALU.add))
                        V(v.tensor_tensor(rr[0:n], rr[0:n], beta, ALU.mult), s("d_r"))
                    else:
                        V(v.tensor_tensor(rr[0:n], vN[0:n], beta, ALU.mult), s("d_r"))
                    if t < 2:
                        V(v.tensor_tensor(kd[0:n], kN[0:n], bc(kdf[0:n, :], P, 2), ALU.mult), s("d_kd"))
                        v.wait_ge(s("d_st"), t + 1)
                        sview = ps[:, 7, :].rearrange("p (a b) -> p a b", a=4)
                        if t:
                            V(v.tensor_tensor(st, st, bc(elast[:, 4 * t:4 * t + 4], P, 2), ALU.mult))
                            V(v.tensor_tensor(st, st, sview, ALU.add), s("d_stv"))
                        else:
                            V(v.tensor_copy(st, sview), s("d_stv"))
                v.wait_ge(s("od_rs"), 1)
                V(v.scalar_tensor_tensor(out=mixT[:, 0:4, :], in0=mixT[:, 0:4, :], scalar=prm2("norm_g"),
                                         in1=projT[:, 0:4, :], op0=ALU.mult, op1=ALU.mult))
                V(v.tensor_tensor(mixT[:, 0:4, :], mixT[:, 0:4, :], projT[:, NZ:NZ + 4, :], ALU.mult), s("od_ready"))
                for i, c in enumerate(ROPE_CHUNKS):
                    v.wait_ge(s("rp_done"), i + 1)
                    V(v.tensor_tensor(rtmp, ps[:, 4 + i % 4, 0:T], const("sin"), ALU.mult))
                    V(v.tensor_tensor(projT[:, c, :], projT[:, c, :], const("cos"), ALU.mult))
                    V(v.tensor_tensor(projT[:, c, :], projT[:, c, :], rtmp, ALU.add), s("rp_ready"))
                nix = 0
                v.wait_ge(s("v_evicted"), 1)
                for j, job in enumerate(JOBS2):
                    t = job[1]
                    if job[2] == 0:
                        nk = COL[t] + ROWS[t]
                        if t == 0:
                            V(v.tensor_copy(mk[0:META, 0:META], const("mla_mask")[0:META, P:P + META]))
                        else:
                            caus = const("caus" if t == 1 else "caus2")[:, 0:nk]
                            for half in range(2):
                                v.wait_ge(s("ix_relu"), nix + 1)
                                for h in range(4):
                                    w = wi[:, 8 * t + 4 * half + h:8 * t + 4 * half + h + 1]
                                    last = s("ix_used") if h == 3 else None
                                    if half == 0 and h == 0:
                                        V(v.tensor_scalar(sc[:, 0:nk], rl[:, h, 0:nk], w, None, ALU.mult), last)
                                    else:
                                        V(v.scalar_tensor_tensor(out=sc[:, 0:nk], in0=rl[:, h, 0:nk], scalar=w,
                                                                 in1=sc[:, 0:nk], op0=ALU.mult, op1=ALU.add), last)
                                nix += 1
                            V(v.tensor_tensor(sc[:, 0:nk], sc[:, 0:nk], caus, ALU.add))
                            cur, nxt = sc, wk
                            for r in range(TOPK // 8):
                                V(v.max(max8, cur[:, 0:nk]))
                                V(v.match_replace(nxt[:, 0:nk], max8, cur[:, 0:nk], -3.0e38))
                                cur, nxt = nxt, cur
                            V(v.tensor_scalar(cur[:, 0:nk], cur[:, 0:nk], -2.0e38, NEG, ALU.is_gt, ALU.mult))
                            V(v.tensor_tensor(mk[:, 0:nk], cur[:, 0:nk], caus, ALU.add))
                    vec_mask(v, V, JOBS2, j)
                    vec_norm(v, V, JOBS2, j)

                def layer_norm(t, which, add):
                    n = ROWS[t]
                    r = res[0:n, t, :]
                    V(v.scalar_tensor_tensor(out=r, in0=r, scalar=ALPHA, in1=add, op0=ALU.mult, op1=ALU.add,
                                             accum_out=ssum[0:n, t:t + 1]))
                    V(v.tensor_scalar(lnm[0:n, t:t + 1], ssum[0:n, t:t + 1], -1.0 / D, None, ALU.mult), s("ln_mean"))
                    v.wait_ge(s("ln_rstd"), 3 * (which - 1) + t + 1)
                    V(v.tensor_scalar(r, r, lnm[0:n, t:t + 1], rstd[0:n, t:t + 1], ALU.add, ALU.mult))
                    V(v.tensor_tensor(r, r, prm2(f"ln{which}_g")[0:n], ALU.mult))
                    V(v.tensor_tensor(r, r, prm2(f"ln{which}_b")[0:n], ALU.add), s("ln_done"))

                v.wait_ge(s("out_ready"), ITEMS_WO)
                for t in range(3):
                    layer_norm(t, 1, ps[0:ROWS[t], 2 * t:2 * t + 2, :].rearrange("p a b -> p (a b)"))

                v.wait_ge(s("m_lg"), 1)
                for t in range(3):
                    n = ROWS[t]
                    q = lg[0:n, t, :]

                    def c(i, w=1):
                        return q[:, i:i + w]

                    desc = const("desc")[0:n]
                    V(v.tensor_tensor(c(0, 36), ps[0:n, 6, 64 * t:64 * t + 36], prm2("br")[0:n], ALU.add))
                    V(v.tensor_reduce(c(36), c(0, 4), AX, ALU.max))
                    V(v.tensor_scalar(c(40, 4), c(0, 4), c(36), None, ALU.subtract))
                    V(v.tensor_scalar(c(48, 4), c(0, 4), c(36), None, ALU.is_equal))
                    V(v.tensor_tensor(c(48, 4), c(48, 4), desc[:, 0:4], ALU.mult))
                    V(v.tensor_reduce(c(37), c(48, 4), AX, ALU.max))
                    V(v.tensor_scalar(c(52, 4), c(48, 4), c(37), None, ALU.is_equal))
                    V(v.tensor_scalar(c(56, 4), c(52, 4), -NEG, NEG, ALU.mult, ALU.add))
                    V(v.tensor_tensor(c(64, 32).rearrange("p (a b) -> p a b", a=4),
                                      c(4, 32).rearrange("p (a b) -> p a b", a=4), bc(c(56, 4), 8, 2), ALU.add))
                    for k in range(2):
                        src = 64 if k == 0 else 164
                        m, oh = 96 + 2 * k, 132 + 64 * k
                        V(v.tensor_reduce(c(m), c(src, 32), AX, ALU.max))
                        V(v.tensor_scalar(c(300, 32), c(src, 32), c(m), None, ALU.is_equal))
                        V(v.tensor_tensor(c(300, 32), c(300, 32), desc, ALU.mult))
                        V(v.tensor_reduce(c(m + 1), c(300, 32), AX, ALU.max))
                        V(v.tensor_scalar(c(oh, 32), c(300, 32), c(m + 1), None, ALU.is_equal))
                        if k == 0:
                            V(v.scalar_tensor_tensor(out=c(164, 32), in0=c(132, 32), scalar=NEG, in1=c(64, 32),
                                                     op0=ALU.mult, op1=ALU.add))
                    V(v.tensor_tensor(c(99), c(98), c(96), ALU.subtract), s("m_e1"))
                    v.wait_ge(s("m_e1d"), t + 1)
                    V(v.tensor_scalar(c(100), c(99), 1.0, None, ALU.add))
                    V(v.tensor_tensor(c(100), c(100), c(45), ALU.mult))
                    V(v.reciprocal(c(100), c(100)))
                    V(v.tensor_tensor(c(101), c(100), c(99), ALU.mult))
                    V(v.tensor_scalar(c(256, 32), c(132, 32), c(100), None, ALU.mult))
                    V(v.scalar_tensor_tensor(out=c(256, 32), in0=c(196, 32), scalar=c(101), in1=c(256, 32),
                                             op0=ALU.mult, op1=ALU.add), s("m_comb"))
                v.wait_ge(s("m_combT"), 1)
                for t in range(3):
                    n = ROWS[t]
                    V(v.tensor_scalar(lg[0:n, t, 332:336], lg[0:n, t, 52:56], -1000.0, 1000.0, ALU.mult, ALU.add))
                    V(v.tensor_tensor(lg[0:n, t, 332:336], lg[0:n, t, 332:336], ps[0:n, 6, 256 + 8 * t:260 + 8 * t],
                                      ALU.add))
                V(v.tensor_reduce(mx[:, 0:1], ps[:, 6, 288:292], AX, ALU.max))
                V(v.tensor_scalar(mx[:, 0:1], mx[:, 0:1], GROUP_SLOTS + 0.5, None, ALU.is_gt))
                V(v.tensor_copy(flag[:, :], mx[:, 0:1]), s("m_flag"))

                def hidden(n, j, at=0):
                    for f in range(2):
                        e = e1b[:, 2 * j + f, :]
                        v.wait_ge(s("m_exp"), n * 2 + (f + 1))
                        v.tensor_scalar(e, e, 1.0, None, ALU.add).then_inc(s("vec_loop"), 1)
                        v.wait_ge(s("vec_loop"), at + 4 * f + 1)
                        v.reciprocal(e, e).then_inc(s("vec_loop"), 1)
                        v.wait_ge(s("vec_loop"), at + 4 * f + 2)
                        v.tensor_tensor(e, e, ps[:, f, 0:T], ALU.mult).then_inc(s("vec_loop"), 1)
                        v.wait_ge(s("vec_loop"), at + 4 * f + 3)
                        v.tensor_tensor(e, e, ps[:, 2 + f, 0:T], ALU.mult).then_inc(s("vec_loop"), 1)
                        v.wait_ge(s("vec_loop"), at + 4 * f + 4)
                        v.tensor_tensor(hid[:, 2 * j + f, :], e, cbb[:, j, :], ALU.mult).then_inc(s("m_hid"), 1)
                        v.wait_ge(s("m_hid"), n * 2 + (f + 1 + 2))

                def add_up(n):
                    for d in range(KC):
                        v.wait_ge(s("m_y"), n * KC + (d + 1))
                        v.tensor_tensor(yacc[:, d, :], yacc[:, d, :], ps[:, 5 + d % 3, 0:T], ALU.add)\
                            .then_inc(s("m_yadd"), 1)
                    v.wait_ge(s("m_yadd"), n * KC + (KC + 3))

                def experts_all():
                    v.tensor_copy(combT, ps[0:EXPERTS, 7, 0:T]).then_inc(s("m_combev"), 1)
                    v.memset(yacc, 0.0).then_inc(s("vec_loop"), 1)
                    v.wait_ge(s("vec_loop"), 1)
                    v.sem_clear(s("vec_loop"))
                    v.sem_inc(s("m_hid"), 2)
                    v.sem_inc(s("m_yadd"), 3)
                    hidden(0, 0)
                    v.sem_inc(s("vec_turns"), 1)
                    v.sem_clear(s("vec_loop"))
                    with v.Fori(0, TURNS) as g:
                        hidden(g * 2 + 1, 1)
                        add_up(g * 2)
                        hidden(g * 2 + 2, 0, 8)
                        add_up(g * 2 + 1)
                        v.sem_inc(s("vec_turns"), 1)
                        v.sem_clear(s("vec_loop"))
                    hidden(EXPERTS - 1, 1)
                    add_up(EXPERTS - 2)
                    add_up(EXPERTS - 1)

                def select(g):
                    for t in range(3):
                        n = ROWS[t]
                        at = lg[0:n, t, 332 + g:333 + g] if isinstance(g, int) else lg[0:n, t, bass.ds(g + 332, 1)]
                        v.tensor_scalar(xsel[0:n, t, :], const("slots")[0:n], at, None, ALU.is_equal)\
                            .then_inc(s("x_sel") if t == 2 else s("vec_sel"), 1)
                    

                def group(g, last):
                    at = 0
                    v.wait_ge(s("x_cg"), g + 1)
                    for e in range(PER_GROUP):
                        x = xe[:, e % 2, :]
                        v.wait_ge(s("x_exp"), g * PER_GROUP + (e + 1))
                        v.tensor_scalar(x, x, 1.0, None, ALU.add).then_inc(s("vec_loop"), 1)
                        v.wait_ge(s("vec_loop"), at + 1)
                        v.reciprocal(x, x).then_inc(s("vec_loop"), 1)
                        v.wait_ge(s("vec_loop"), at + 2)
                        v.tensor_tensor(x, x, ps[:, e % 2, 0:256], ALU.mult).then_inc(s("vec_loop"), 1)
                        at += 3
                        v.wait_ge(s("vec_loop"), at)
                        v.scalar_tensor_tensor(out=xh[:, e % 2, :], in0=ps[:, e % 2, 256:512], scalar=xcg[:, e:e + 1], in1=x,
                                               op0=ALU.mult, op1=ALU.mult).then_inc(s("x_hid"), 1)
                        if e == PER_GROUP - 3 and not last:
                            select(g + 1)
                    if not last:
                        v.sem_clear(s("vec_loop"))

                def experts_grouped():
                    v.sem_inc(s("x_hid"), 2)
                    select(0)
                    with v.Fori(0, GROUPS - 1) as g:
                        group(g, False)
                    group(GROUPS - 1, True)

                crowded = branch(v)
                with v.If(crowded > 0):
                    experts_all()
                with v.Else():
                    experts_grouped()
                for t in range(3):
                    v.wait_ge(s("m_back"), 1)
                    layer_norm(t, 2, ps[0:ROWS[t], 2 * t:2 * t + 2, :].rearrange("p a b -> p (a b)"))
                new_layer(v, l, LAYERS, 1)

        @block.gpsimd
        def _(g):
            def clear(base, l):
                g.wait_ge(layer_done, l * 4 + (4 * base + 3))
                g.sem_inc(layer_seen, 1)
                g.sem_clear(range(layer_sems[0].num, layer_sems[-1].num + 1))
                g.sem_inc(layer_done, 1)
                g.sem_inc(layer_go, 1)

            with g.Fori(0, LAYERS) as l:
                clear(0, l)
            with g.Fori(0, LAYERS) as l:
                G = Linked(g, s("pool_order"))
                levl = const("lev_l").rearrange("p (i m) -> p i m", m=P)
                lev = 0
                for t in range(3):
                    n = ROWS[t]
                    g.wait_ge(s("d_l"), t + 1)
                    for i in range(n.bit_length() - 2):
                        if lev:
                            g.wait_ge(s("d_p"), lev)
                        G(g.tensor_tensor(lS[0:n, :, 0:n], lT[0:n, :, 0:n], bc(levl[0:n, i + 1, 0:n], 4, 1), ALU.mult),
                          s("d_ls"))
                        lev += 1
                clear(LAYERS, l)


def _ins(inputs):
    f = {k: np.ascontiguousarray(v) for k, v in inputs.items()}
    a1 = np.cumsum([0, 256, 128, 128, 256, 256, 256, 256, 128, 32, 256, 256, 256, 1024])
    r = [np.arange(a1[i], a1[i + 1]) for i in range(13)]
    kv0, kv1 = r[1][:64], r[1][64:]
    cols1 = np.concatenate([r[0], kv0, kv0, kv1, kv1, r[2], r[3], r[4], r[5], r[6], r[7],
                            np.tile(r[8], 4), r[9], r[10], r[11], r[12], np.tile(r[8], 4)])
    a2 = np.cumsum([0, 512, 512, 512, 512, 4, 4, 512, 512, 512, 512, 64, 8])
    q = [np.arange(a2[i], a2[i + 1]) for i in range(12)]
    cols2 = np.concatenate([q[0], q[1], q[2], q[3], q[6], q[7], q[8], q[9], q[10], q[10],
                            np.tile(q[5], 8), np.tile(q[4], 8), np.tile(q[11], 8)])

    def items(w, cols):
        n = len(cols) // 256
        w = w[:, :, cols].reshape(LAYERS, KC, P, n, 2, P)
        return np.ascontiguousarray(w.transpose(0, 3, 2, 4, 1, 5)).reshape(LAYERS * n * P, 2 * D)

    def col(v, n):
        return v.reshape(LAYERS, n, P).transpose(0, 2, 1)

    def rows(v):
        return np.broadcast_to(v[:, None, :], (LAYERS, P, v.shape[-1]))

    def pad4(v):
        return np.tile(v, (1, P // 4))[:, :, None]

    p1 = np.concatenate([col(f["norm_pre"], KC), col(f["mla_q_norm"], 2), col(f["mla_kv_norm"], 1),
                         f["conv_w"].reshape(LAYERS, 6, P).transpose(0, 2, 1), col(f["conv_b"], 2),
                         col(f["group_norm"], KC), rows(f["attn_sinks"]),
                         f["mla_w_uq"].reshape(LAYERS, 2, P, 384).transpose(0, 2, 1, 3).reshape(LAYERS, P, 768),
                         f["mla_w_ukv"], rows(f["norm_post"])], 2)
    wr = np.concatenate([f["w_grp_2"], f["w_rtr_2"]], 2).reshape(LAYERS, P, KC * 36)
    br = np.concatenate([f["b_grp_2"], f["b_rtr_2"]], 1)
    p2 = np.concatenate([f["conv_w_2"].reshape(LAYERS, 4, 12, P).transpose(0, 3, 2, 1).reshape(LAYERS, P, 48),
                         f["dn_norm_g_2"][:, :, None], pad4(f["a_log_2"]), pad4(f["dt_bias_2"]), rows(br), wr,
                         rows(f["ln1_g_2"]), rows(f["ln1_b_2"]), rows(f["ln2_g_2"]), rows(f["ln2_b_2"])], 2)
    return {
        "x": f["x"], "meta_tokens_2": f["meta_tokens_2"], "positions": f["positions"], "consts": constants(),
        "w_in_1": items(f["w_in"], cols1), "w_in_2": items(f["w_in_2"], cols2),
        "w_out_1": f["w_out"].reshape(LAYERS * D, D), "w_out_2": f["w_out_2"].reshape(LAYERS * D, D),
        "params_1": np.ascontiguousarray(p1).reshape(LAYERS * P, NP1),
        "params_2": np.ascontiguousarray(p2).reshape(LAYERS * P, NP2),
        "w1_2": f["w1_2"].reshape(LAYERS * EXPERTS * P, 2 * D), "w3_2": f["w3_2"].reshape(LAYERS * EXPERTS * P, 2 * D),
        "w2_2": f["w2_2"].reshape(LAYERS * EXPERTS * D_EXP, D),
    }


def kernel(**inputs):
    import concourse.bacc as bacc
    from concourse.bass_utils import run_bass_kernel_spmd

    nc = bacc.Bacc("TRN2", target_bir_lowering=False, num_devices=1)
    arrays = _ins(inputs)
    aps = {k: nc.dram_tensor(k, v.shape, mybir.dt.from_np(v.dtype), kind="ExternalInput").ap() for k, v in arrays.items()}
    out = nc.dram_tensor("out", (1, SEQ, D), F32, kind="ExternalOutput").ap()
    program(nc, aps, out)
    r = run_bass_kernel_spmd(nc, [arrays], core_ids=[0])
    return r.results[0]["out"]
```

```python
from contextlib import ExitStack

import numpy as np

import concourse.bass as bass
from concourse import mybir

F32 = mybir.dt.float32
I32 = mybir.dt.int32
ALU = mybir.AluOpType
ACT = mybir.ActivationFunctionType
AX = mybir.AxisListType.X

P = 128
D = 1024
KC = D // P
SEQ = 256
META = 16
T = SEQ + META
LAYERS = 2
COL = [0, META, META + P]
ROWS = [META, P, P]
NEG = -1.0e30
SLOTS = 6
SLOT = 2048
CREDIT = 32

SQ, SK, SV, CB, CC, CX, MQ, MKV, MKR, DQ, DK, DV, GATE = 0, 2, 4, 5, 7, 9, 11, 13, 14, 15, 17, 19, 21
N1 = 29
ITEMS_P1 = (N1 + 1) // 2
ITEMS_WO = 4
ITEMS1 = ITEMS_P1 + ITEMS_WO
SLOT0_1 = 0
SM, IK, NQ, NK_, NV, NZ, AQ, AK, AV, IQ = 0, 1, 2, 6, 10, 14, 18, 22, 26, 30
N2 = 34
ITEMS_P2 = N2 // 2
EXPERTS = 32
GROUPS = 4
D_EXP = 256
TURNS = EXPERTS // 2 - 1
PER_GROUP = EXPERTS // GROUPS
GROUP_SLOTS = P
ITEMS_MIX2 = ITEMS_P2 + ITEMS_WO
ITEMS2 = ITEMS_MIX2 + 3 * EXPERTS
SLOT0_2 = (1 - ITEMS2) % SLOTS
TOPK = 64
ROPE_CHUNKS = [IK, *range(AQ, AQ + 4), *range(AK, AK + 4), *range(IQ, IQ + 4)]
ALPHA = float((2.0 * LAYERS) ** 0.25)



def levels(t):
    return ROWS[t].bit_length() - 2


def delta_steps():
    steps = []
    for t in range(3):
        steps += [("scores", t), ("lower", t)]
        for i in range(levels(t)):
            steps += [("level_p", t, i), ("level_q", t, i)]
        steps += [("values", t), ("outputs", t)]
    return steps


def mixer_order():
    order = []
    delta = delta_steps()
    rope = [("rope", i) for i in range(len(ROPE_CHUNKS))]
    attention = []
    for t in (1, 2):
        attention += [("index", t, q) for q in range(4)] + [("strike", t, r) for r in range(4)] + [("mask", t)]
    attention.append(("tokens",))

    def more_delta():
        if delta:
            order.append(delta.pop(0))

    for j in range(N2):
        order.append(("project", j))
        if j == SM:
            order.append(("gates",))
        if j == NQ + 1:
            order.append(("decay_rows",))
        if j == NQ + 2:
            order.append(("beta_rows",))
        if j == NQ + 3:
            order.append(("gate_columns",))
        c = j - NQ
        if 0 <= c < 12:
            order.append(("conv", c))
        if 1 <= c < 13:
            order.append(("sigmoid", c - 1))
        if 2 <= c < 14:
            order.append(("silu", c - 2))
        if c in (6, 10):
            order.append(("length", (c - 6) // 4))
        if c in (8, 12):
            order.append(("unit", (c - 8) // 4))
        if j >= NZ + 1:
            more_delta()
        if j == NZ + 3:
            order.append(("silu_z",))
        if j > NZ + 3 and (j % 2 or not delta) and rope and ROPE_CHUNKS[rope[0][1]] < j - 1:
            order.append(rope.pop(0))
    fill = rope + attention
    while delta or fill:
        more_delta()
        if fill:
            order.append(fill.pop(0))
    return order


P1 = {}
P2 = {}
CONSTS = {}


def _columns(table, entries):
    at = 0
    for name, n in entries:
        table[name] = (at, at + n)
        at += n
    return at


NP1 = _columns(P1, [("g_pre", KC), ("g_q", 2), ("g_kv", 1), ("conv_w", 6), ("conv_b", 2), ("g_grp", KC),
                    ("sinks", 4), ("w_uq", 2 * 384), ("w_ukv", 512), ("g_post", D)])
NP2S = _columns(P2, [("conv_w", 48), ("norm_g", 1), ("a_log", 1), ("dt", 1), ("br", 36), ("wr", KC * 36),
                     ("ln1_g", D), ("ln1_b", D), ("ln2_g", D), ("ln2_b", D)])
NP2 = NP2S
NLEV = 7
NC_ = _columns(CONSTS, [("ident", P), ("ones", P), ("tri", P), ("upper", P), ("strict", P),
                        ("swa_mask", 2 * P), ("mla_mask", 2 * P), ("lev_u", NLEV * P), ("lev_l", NLEV * P),
                        ("rot", P), ("rot96", 32), ("freq", 1), ("cos", T), ("sin", T),
                        ("sel", 4 * P), ("selb", 4 * P), ("caus", T), ("caus2", T), ("desc", 32), ("sel2", 2 * P),
                        ("slots", GROUP_SLOTS)])


def constants():
    c = np.zeros((P, NC_), np.float32)

    def put(name, a, rows=slice(None)):
        lo, hi = CONSTS[name]
        c[rows, lo:hi] = np.asarray(a, np.float32).reshape(-1, hi - lo)

    p, f = np.arange(P)[:, None], np.arange(P)[None, :]
    put("ident", p == f)
    put("ones", np.ones((P, P)))
    put("tri", p >= f)
    put("upper", f >= p)
    put("strict", f > p)
    causal = np.where(f <= p, 0.0, NEG)
    put("swa_mask", np.concatenate([np.where(f > p, 0.0, NEG), causal], 1))
    put("mla_mask", np.concatenate([0.0 * causal, causal], 1))
    lev = []
    for n in range(NLEV):
        s = 1 << n
        lev.append((p // (2 * s) == f // (2 * s)) & (p % (2 * s) < s) & (f % (2 * s) >= s))
    put("lev_u", np.concatenate(lev, 1))
    put("lev_l", np.concatenate([m.T for m in lev], 1))
    rot = np.zeros((P, P))
    for h in range(2):
        for i in range(32):
            rot[64 * h + 32 + i, 64 * h + i] = -1.0
            rot[64 * h + i, 64 * h + 32 + i] = 1.0
    put("rot", rot)
    r96 = np.zeros((P, 32))
    for i in range(16):
        r96[64 + 16 + i, i] = -1.0
        r96[64 + i, 16 + i] = 1.0
    put("rot96", r96)
    half = np.float32(10000.0) ** (-np.arange(16, dtype=np.float32) / np.float32(16))
    put("freq", np.tile(half, 8)[:, None])
    inv = np.float32(1.0) / (np.float32(10000.0) ** (np.arange(0, 64, 2, dtype=np.float32) / np.float32(64)))
    ang = (np.arange(T, dtype=np.float32)[:, None] * inv[None, :]).astype(np.float32)
    put("cos", np.tile(np.cos(ang).T, (4, 1)))
    put("sin", np.tile(np.sin(ang).T, (4, 1)))
    sel = np.zeros((P, 4 * P))
    selb = np.zeros((P, 4 * P))
    for h in range(4):
        sel[h, h * P:(h + 1) * P] = 1.0
        selb[32 + h, h * P:(h + 1) * P] = 1.0
    put("sel", sel)
    put("selb", selb)
    key = np.arange(T)[None, :]
    put("caus", np.where(key <= META + p, 0.0, NEG))
    put("caus2", np.where(key <= META + P + p, 0.0, NEG))
    put("desc", np.broadcast_to(np.arange(32, 0, -1), (P, 32)))
    sel2 = np.zeros((P, 2 * P))
    sel2[0, :P] = 1.0
    sel2[1, P:] = 1.0
    put("sel2", sel2)
    put("slots", np.broadcast_to(np.arange(GROUP_SLOTS), (P, GROUP_SLOTS)))
    return c


class Linked:

    def __init__(self, eng, own):
        self.eng, self.own, self.n = eng, own, {}

    def __call__(self, ins, sem=None):
        sem = self.own if sem is None else sem
        ins.then_inc(sem, 1)
        self.n[sem.num] = self.n.get(sem.num, 0) + 1
        self.eng.wait_ge(sem, self.n[sem.num])


def ring_slot(block, i):
    return ((SLOT0_1 if block == 1 else SLOT0_2) + i) % SLOTS


def uses_before(block, i, slot):
    return sum(ring_slot(block, k) == slot for k in range(i))


def program(nc, A, out):
    with ExitStack() as ctx:
        def sb(name, *shape):
            return ctx.enter_context(nc.sbuf_tensor(name, [P, *shape], F32))

        layer_sems = []

        def sem(name):
            return ctx.enter_context(nc.semaphore(name))

        def lsem(name):
            layer_sems.append(sem(name))
            return layer_sems[-1]

        ring = sb("ring", SLOTS, SLOT)
        projT = sb("projT", N2, T)
        res = sb("res", 3, D)
        hT = sb("hT", KC, T)
        prm = sb("prm", max(NP1, NP2))
        cst = sb("cst", NC_)
        cosT = sb("cosT", SEQ)[:, :]
        sinT = sb("sinT", SEQ)[:, :]
        small = sb("small", 160)
        AR = 15232
        arena = sb("arena", AR)
        posi = ctx.enter_context(nc.sbuf_tensor("posi", [P, SEQ], I32))
        ps = ctx.enter_context(nc.psum_tensor("ps", [P, 8, 512], F32))
        comb_dram = nc.dram_tensor("comb_dram", (EXPERTS, T), F32, kind="Internal").ap()

        def carve(sizes):
            at, got = 0, []
            for s in sizes:
                n = int(np.prod(s))
                v = arena[:, at:at + n]
                if len(s) == 2:
                    v = v.rearrange("p (a b) -> p a b", b=s[1])
                if len(s) == 3:
                    v = v.rearrange("p (a b c) -> p a b c", b=s[1], c=s[2])
                got.append(v)
                at += n
            assert at <= AR, at
            return got

        def const(name):
            lo, hi = CONSTS[name]
            return cst[:, lo:hi]

        ident, ones, tri = const("ident"), const("ones"), const("tri")

        slot_in = [sem(f"slot_in{i}") for i in range(SLOTS)]
        ring_used = sem("ring_used")
        up_used = sem("up_used")
        down_used = sem("down_used")
        start_in = sem("start_in")
        meta_in = sem("meta_in")
        layer_done = sem("layer_done")
        layer_go = sem("layer_go")
        out_done = sem("out_done")
        seen = sem("seen")
        layer_seen = sem("layer_seen")
        tables_done = sem("tables_done")
        tables_vec = sem("tables_vec")

        names = ["act_order", "vec_order", "pool_order", "params_in", "rstd_ready", "xn_ready", "ht_done", "ht_ready",
                 "proj_done", "proj_ev_act", "proj_ev_vec", "v_done", "v_evicted",
                 "mla_sq", "mla_ss", "mla_rs", "mla_n", "mla_qk", "mla_qh", "mla_kh", "mla_rot", "mla_v", "mla_rope",
                 "s_ready", "stt_done", "nm_ready", "exp_done", "p_ready", "pt_done", "pt_evicted", "o_done",
                 "o_evicted", "sb_z", "sb_u", "sb_l", "sb_sp", "sb_r", "sb_d", "sb_a", "sb_am", "sb_o", "sb_oe",
                 "gate_exp", "conv_ready", "y_sq", "y_ss", "y_rs", "y_ready",
                 "out_ready", "out_ss", "res_ready",
                 "g_sm", "g_ln", "g_scan", "g_bc", "g_bcev", "g_cols", "g_colsev",                  "cv_ready", "cv_exp", "cv_silu", "cv_sq", "cv_ss", "cv_rs", "cv_norm", "kv_done", "kv_ev",
                 "gq_done", "d_diff", "d_exp", "d_u", "d_lt", "d_l", "d_ls", "d_p", "d_pev", "d_q", "d_q2", "d_y", "rp_used",
                 "d_ks", "d_r", "d_vn", "d_vnev", "d_kd", "d_o", "d_oev", "d_st", "d_stv",
                 "z_exp", "od_sq", "od_ss", "od_rs", "od_ready",
                 "rp_done", "rp_ready", "ix_s", "ix_relu", "ix_used",                  "ln_mean", "ln_rstd", "ln_done", "m_ht", "m_htev", "m_lg", "m_e1", "m_e1d",
                 "m_comb", "m_combT", "m_combev", "m_combst", "m_up", "m_exp", "m_cb", "m_hid", "m_y", "m_yadd", "vec_loop", "vec_turns",
                 "m_flag", "params_late", "m_lt", "m_ltev", "m_grp", "m_sizes","x_cg", "vec_sel", "act_group", "x_sel", "x_g", "x_ge", "x_exp", "x_hid", "x_t", "x_te", "x_ye",
                 "m_back", "cin"]
        S = {n: lsem(n) for n in names}

        def s(n):
            return S[n]

        block = ctx.enter_context(nc.Block())

        def new_layer(eng, l, base, value):
            eng.sem_inc(layer_done, 1)
            eng.wait_ge(layer_go, base + l + 1)

        w1p = A["w_in_1"]
        w2p = A["w_in_2"]

        @block.sync
        def _(sp):
            def load(blk, base, l, i, src):
                slot = ring_slot(blk, i)
                n = ITEMS1 if blk == 1 else ITEMS2
                ago = (-slot) % SLOTS
                used = base - ago if i < SLOTS else base + i - SLOTS + 1
                sp.wait_ge(ring_used, l * n + (used + CREDIT))
                sp.dma_start(ring[:, slot, :] if len(src.shape) == 2 else
                             ring[:, slot, :].rearrange("p (c n) -> p c n", c=src.shape[1]),
                             src).then_inc(slot_in[slot], 16)

            def rows2(w, first):
                return w[bass.ds(first, 256), :].rearrange("(c p) n -> p c n", p=P)

            with sp.Fori(0, LAYERS) as l:
                for i in range(ITEMS_P1):
                    load(1, 0, l, i, w1p[bass.ds((l * ITEMS_P1 + i) * P, P), :])
                for i in range(ITEMS_WO):
                    load(1, 0, l, ITEMS_P1 + i, rows2(A["w_out_1"], l * D + 256 * i))
            base = LAYERS * ITEMS1
            with sp.Fori(0, LAYERS) as l:
                for i in range(ITEMS_P2):
                    load(2, base, l, i, w2p[bass.ds((l * ITEMS_P2 + i) * P, P), :])
                for i in range(ITEMS_WO):
                    load(2, base, l, ITEMS_P2 + i, rows2(A["w_out_2"], l * D + 256 * i))
                def expert(n, j, first=False):
                    for k, name in enumerate(("w1_2", "w3_2", "w2_2")):
                        i = 3 * j + k
                        slot = ring_slot(2, ITEMS_MIX2 + i)
                        if first:
                            sp.wait_ge(ring_used, l * ITEMS2 + (base + ITEMS_MIX2 + i - SLOTS + 1 + CREDIT))
                        else:
                            sp.wait_ge(up_used if k < 2 else down_used, l * EXPERTS + n - 1)
                        if k == 2:
                            src = rows2(A[name], (l * EXPERTS + n) * D_EXP)
                            dst = ring[:, slot, :].rearrange("p (c n) -> p c n", c=2)
                        else:
                            src = A[name][bass.ds((l * EXPERTS + n) * P, P), :]
                            dst = ring[:, slot, :]
                        sp.dma_start(dst, src).then_inc(slot_in[slot], 16)

                expert(0, 0, True)
                expert(1, 1, True)
                with sp.Fori(0, TURNS) as g:
                    expert(g * 2 + 2, 0)
                    expert(g * 2 + 3, 1)
            sp.wait_ge(layer_done, 4 * 2 * LAYERS)
            sp.dma_start(out[0, 0:P, :], res[:, 1, :]).then_inc(out_done, 16)
            sp.dma_start(out[0, P:SEQ, :], res[:, 2, :]).then_inc(out_done, 16)
            sp.wait_ge(out_done, 32)

        def slot_wait(pe, blk, l, i, g=None):
            slot = ring_slot(blk, i)
            before = LAYERS * uses_before(1, ITEMS1, slot) if blk == 2 else 0
            per = uses_before(blk, ITEMS1 if blk == 1 else ITEMS2, slot)
            v = l * (16 * per) + 16 * (before + uses_before(blk, i, slot) + 1)
            if g is not None:
                v = v + g * 16
            pe.wait_ge(slot_in[slot], v)
            return ring[:, slot, :]

        (xn, vA, vD, vC, qh, kh, cn, sq3) = carve([(2, D), (2, P), (2, 256), (2, 512), (4, SEQ), (4, SEQ), (3, SEQ), (3, SEQ)])
        at1 = 2048 + 256 + 512 + 1024 + 2048 + 768 + 768
        def more(at, *shape):
            n = int(np.prod(shape))
            v = arena[:, at:at + n]
            if len(shape) == 2:
                v = v.rearrange("p (a b) -> p a b", b=shape[1])
            if len(shape) == 3:
                v = v.rearrange("p (a b c) -> p a b c", b=shape[1], c=shape[2])
            assert at + n <= AR, at + n
            return v, at + n
        s1, at1 = more(at1, 2, 4, T)
        pT1, at1 = more(at1, 3, 4 * P)
        yT, at1 = more(at1, KC, SEQ)
        sg, at1 = more(at1, KC, SEQ)
        u1 = arena[:, 0:1024].rearrange("p (a b) -> p a b", a=4)
        u2 = arena[:, 1024:1536].rearrange("p (a b) -> p a b", a=4)
        sp1 = projT[:, 0:4, 0:SEQ]
        sp2 = projT[:, 4:8, 0:P]
        l1 = projT[:, 7:11, 0:SEQ] if False else projT[:, 8:12, 0:SEQ]
        l2 = projT[:, 12:14, :].rearrange("p a b -> p (a b)")[:, 0:512].rearrange("p (a b) -> p a b", a=4)
        ysq = projT[:, 0:8, 0:SEQ]
        yrs = projT[:, 8:12, 0:SEQ]

        cv, a2 = more(0, 12, T)
        gcb, a2 = more(a2, 4, T)
        btb, a2 = more(a2, 4, T)
        ebc, a2 = more(a2, 4, T)
        gsm, a2 = more(a2, T)
        gtmp, a2 = more(a2, T)
        cols, a2 = more(a2, 3, P)
        kN, a2 = more(a2, 4, P)
        vN, a2 = more(a2, 4, P)
        dif, a2 = more(a2, 4, P)
        atT, a2 = more(a2, 4, P)
        uT, a2 = more(a2, 4, P)
        lT, a2 = more(a2, 4, P)
        lS, a2 = more(a2, 4, P)
        yU, a2 = more(a2, 4, P)
        yL, a2 = more(a2, 4, P)
        pP, a2 = more(a2, 4, P)
        rr, a2 = more(a2, 4, P)
        vn, a2 = more(a2, 4, P)
        kd, a2 = more(a2, 4, P)
        st, a2 = more(a2, 4, P)
        end2 = a2
        mixT = hT
        vS, a3 = more(0, 3, 512)
        s2, a3 = more(a3, 2, 4, T)
        pT2, a3 = more(a3, 3, 4 * P)
        h2T = projT[:, 0:KC, :]
        yacc = projT[:, 8:16, :]
        hid = projT[:, 16:20, :]
        e1b = projT[:, 20:24, :]
        cbb = projT[:, 24:26, :]
        comb2f, _ = more(1300, (EXPERTS // 2) * T)
        comb2 = comb2f.rearrange("p (g t) -> p g t", t=T)
        combT = projT[0:EXPERTS, 27, :]
        rtmp, _ = more(end2, T)
        odT = projT[:, NK_:NK_ + 4, :]
        gate_silu = projT[:, NV:NV + 4, :]
        rl = projT[:, NQ:NQ + 4, :]
        sc, wk = projT[:, NV, :], projT[:, NV + 1, :]
        masks = [const("mla_mask")[:, P:2 * P], projT[:, NV + 2, :], projT[:, NV + 3, :]]
        logitT = projT[0:36, 28, :]
        bcones4 = ones[0:4, :]
        junk = arena[:, end2 - D:end2]
        lg = arena[:, 0:3 * 400].rearrange("p (t n) -> p t n", n=400)

        def prm1(name):
            lo, hi = P1[name]
            return prm[:, lo:hi]

        def prm2(name):
            lo, hi = P2[name]
            return prm[:, lo:hi]

        rstd = small[:, 0:4]
        ssum = small[:, 4:8]
        mx = small[:, 8:16]
        rsum = small[:, 16:24]
        sinkn = small[:, 24:32]
        eps6 = small[:, 32:33]
        eps5 = small[:, 33:34]
        nega = small[:, 34:35]
        lnm = small[:, 36:40]
        lnv = small[:, 40:44]
        kdf = small[:, 44:48]
        neg_e = small[:, 48:60]
        max8 = small[:, 60:68]
        ssq = small[:, 68:72]
        wi = small[:, 72:96]
        elast = small[:, 96:108]
        ecol = small[:, 108:120]

        xy, ax = more(1300, GROUPS, D)
        xg, ax = more(ax, KC, P)
        xselT, ax = more(ax, GROUPS, T)
        XSELT = ax - GROUPS * T
        xsel, ax = more(ax, 3, P)
        xe, ax = more(ax, 2, 256)
        xh, ax = more(ax, 2, 256)
        xhT, ax = more(ax, 2, 256)
        xcg, ax = more(ax, PER_GROUP)
        flag = ctx.enter_context(nc.sbuf_tensor("flag", [P, 1], I32))

        def branch(eng):
            eng.wait_ge(s("m_flag"), 1)
            return eng.value_load(flag[0:1, 0:1], min_val=0, max_val=1)

        def bc(ap, n, axis):
            shape = list(ap.shape)
            shape.insert(axis, n)
            return ap.unsqueeze(axis).broadcast_to(shape)

        JOBS1 = [("swa", 1), ("swa", 2), ("mla", 1), ("mla", 2)]
        JOBS2 = [("dsa", t, half) for t in (0, 1, 2) for half in (0, 1)]

        def job_keys(job):
            t = job[1]
            first = COL[1] if job[0] != "dsa" else 0
            tiles = range(1 if job[0] != "dsa" else 0, t + 1)
            return first, COL[t] + ROWS[t] - first, tiles

        def job_qk(job, h):
            t = job[1]
            first, nk, _ = job_keys(job)
            qc = slice(COL[t], COL[t] + ROWS[t])
            kcols = slice(first, first + nk)
            r = slice(64 * (h % 2), 64 * (h % 2) + 64)
            if job[0] == "swa":
                return projT[r, SQ + h // 2, qc], projT[r, SK + h // 2, kcols]
            if job[0] == "mla":
                return (qh[0:96, h, COL[t] - META:COL[t] - META + P], kh[0:96, h, 0:nk])
            c = 2 * job[2] + h // 2
            return projT[r, AQ + c, qc], projT[r, AK + c, kcols]

        def job_v(job, h, kt):
            n = ROWS[kt]
            if job[0] == "swa":
                return vA[0:n, kt - 1, 64 * (h // 2):64 * (h // 2) + 64]
            if job[0] == "mla":
                return vC[0:n, kt - 1, P * h + 64:P * h + P]
            c = 256 * job[2] + 64 * h
            return vS[0:n, kt, c:c + 64]

        def pe_scores(pe, jobs, j):
            job = jobs[j]
            nk = job_keys(job)[1]
            if j:
                pe.wait_ge(s("stt_done"), j)
            for h in range(4):
                q, k = job_qk(job, h)
                mm = pe.matmul(ps[0:ROWS[job[1]], h, 0:nk], q, k, start=True, stop=True)
            mm.then_inc(s("s_ready"), 1)

        def pe_attend(pe, jobs, j, ready=None):
            for jj in range(j, j + 1):
                job = jobs[jj]
                rows = ROWS[job[1]]
                first, nk, tiles = job_keys(job)
                sbuf = s1 if job[0] != "dsa" else s2
                pTx = pT1 if job[0] != "dsa" else pT2
                pe.wait_ge(s("p_ready"), jj + 1)
                if jj:
                    pe.wait_ge(s("pt_evicted"), jj)
                for kt in tiles:
                    c0 = COL[kt] - first
                    for h in range(4):
                        tr = pe.transpose(ps[0:ROWS[kt], 4 + kt, h * rows:(h + 1) * rows],
                                          sbuf[0:rows, jj % 2, h, c0:c0 + ROWS[kt]], ident[0:rows, 0:rows])
                tr.then_inc(s("pt_done"), 1)
                pe.wait_ge(s("pt_evicted"), jj + 1)
                if jj >= 2:
                    pe.wait_ge(s("o_evicted"), jj - 1)
                for h in range(4):
                    o = ps[64 * (h % 2):64 * (h % 2) + 64, 7,
                           256 * (jj % 2) + P * (h // 2):256 * (jj % 2) + P * (h // 2) + rows]
                    for kt in tiles:
                        mm = pe.matmul(o, job_v(job, h, kt), pTx[0:ROWS[kt], kt, h * rows:(h + 1) * rows],
                                       start=(kt == tiles[0]), stop=(kt == tiles[-1]))
                mm.then_inc(s("o_done"), 1)

        def vec_mask(v, V, jobs, j):
            job = jobs[j]
            rows = ROWS[job[1]]
            _, nk, _ = job_keys(job)
            sbuf = (s1 if job[0] != "dsa" else s2)[0:rows, j % 2, :, 0:nk]
            scale = {"swa": 64, "mla": 96, "dsa": 64}[job[0]] ** -0.5
            v.wait_ge(s("s_ready"), j + 1)
            if job[0] == "dsa":
                mask = masks[job[1]][0:rows, 0:nk]
            else:
                mask = const(job[0] + "_mask")[:, 2 * P - nk:2 * P]
            V(v.scalar_tensor_tensor(out=sbuf, in0=ps[0:rows, 0:4, 0:nk], scalar=scale, in1=bc(mask, 4, 1),
                                     op0=ALU.mult, op1=ALU.add), s("stt_done"))
            k = slice(4 * (j % 2), 4 * (j % 2) + 4)
            V(v.tensor_reduce(mx[0:rows, k], sbuf, AX, ALU.max))
            if job[0] == "swa":
                V(v.tensor_tensor(mx[:, k], mx[:, k], prm1("sinks"), ALU.max))
            V(v.tensor_scalar(mx[0:rows, k], mx[0:rows, k], -1.0, None, ALU.mult))
            V(v.tensor_tensor(sinkn[:, k], mx[:, k], prm1("sinks") if job[0] == "swa" else mx[:, k], ALU.add)
              if job[0] == "swa" else v.tensor_copy(sinkn[0:rows, k], mx[0:rows, k]), s("nm_ready"))

        def act_exp(a, L, jobs, j):
            job = jobs[j]
            rows = ROWS[job[1]]
            _, nk, _ = job_keys(job)
            sbuf = s1 if job[0] != "dsa" else s2
            a.wait_ge(s("nm_ready"), j + 1)
            k0 = 4 * (j % 2)
            if job[0] == "swa":
                L(a.activation(sinkn[:, k0:k0 + 4], sinkn[:, k0:k0 + 4], ACT.Exp))
            for h in range(4):
                L(a.activation(sbuf[0:rows, j % 2, h, 0:nk], sbuf[0:rows, j % 2, h, 0:nk], ACT.Exp,
                               bias=mx[0:rows, k0 + h:k0 + h + 1], accum_out=rsum[0:rows, k0 + h:k0 + h + 1]),
                  s("exp_done") if h == 3 else None)

        def vec_norm(v, V, jobs, j):
            job = jobs[j]
            rows = ROWS[job[1]]
            _, nk, _ = job_keys(job)
            sbuf = (s1 if job[0] != "dsa" else s2)[0:rows, j % 2, :, 0:nk]
            k = slice(4 * (j % 2), 4 * (j % 2) + 4)
            v.wait_ge(s("exp_done"), j + 1)
            if job[0] == "swa":
                V(v.tensor_tensor(rsum[:, k], rsum[:, k], sinkn[:, k], ALU.add))
            V(v.reciprocal(rsum[0:rows, k], rsum[0:rows, k]))
            V(v.tensor_tensor(sbuf, sbuf, bc(rsum[0:rows, k], nk, 2), ALU.mult), s("p_ready"))

        def act_evict(a, L, jobs, j):
            job = jobs[j]
            rows = ROWS[job[1]]
            _, _, tiles = job_keys(job)
            pTx = pT1 if job[0] != "dsa" else pT2
            a.wait_ge(s("pt_done"), j + 1)
            if 0 in tiles:
                L(a.activation(pTx[0:META, 0, 0:4 * rows], ps[0:META, 4, 0:4 * rows], ACT.Copy),
                  s("pt_evicted") if len(tiles) == 1 else None)
            if tiles[-1] > 0:
                L(a.activation(pTx[:, 1:tiles[-1] + 1, :], ps[:, 5:5 + tiles[-1], :], ACT.Copy), s("pt_evicted"))
            a.wait_ge(s("o_done"), j + 1)
            o = ps[:, 7, 256 * (j % 2):256 * (j % 2) + 256].rearrange("p (a b) -> p a b", a=2)[:, :, 0:rows]
            c0 = COL[job[1]]
            if job[0] == "dsa":
                c = 4 + 2 * job[2]
                dst = mixT[:, c:c + 2, c0:c0 + rows]
            else:
                c = 0 if job[0] == "swa" else 4
                dst = yT[:, c:c + 2, c0 - META:c0 - META + rows]
            L(a.activation(dst, o, ACT.Copy), s("o_evicted"))

        def sigmoid(a, L, dst, src, last):
            L(a.activation(dst, src, ACT.Exp, scale=-1.0))
            L(a.activation(dst, dst, ACT.Ln, bias=ones[:, 0:1]))
            L(a.activation(dst, dst, ACT.Exp, scale=-1.0), last)

        def rsqrt_act(a, L, dst, src, scale, eps, last):
            L(a.activation(dst, src, ACT.Ln, bias=eps, scale=scale))
            L(a.activation(dst, dst, ACT.Exp, scale=-0.5), last)

        @block.tensor
        def _(pe):
            pe.sem_inc(ring_used, CREDIT)
            pe.wait_ge(start_in, 16 * 4)
            pe.wait_ge(tables_done, 2)

            def project(blk, l, n, ncols, c0):
                pe.wait_ge(s("ht_ready"), KC)
                for j in range(n):
                    w = slot_wait(pe, blk, l, j // 2) if j % 2 == 0 else ring[:, ring_slot(blk, j // 2), :]
                    w = w.rearrange("p (c k m) -> p c k m", c=2, k=KC)
                    if j >= 4:
                        pe.wait_ge(s("proj_ev_vec" if j % 2 else "proj_ev_act"), (j - 4) // 2 + 1)
                    for k in range(KC):
                        mm = pe.matmul(ps[:, 4 + j % 4, 0:ncols], w[:, j % 2, k, :], hT[:, k, c0:c0 + ncols],
                                       start=(k == 0), stop=(k == KC - 1))
                    mm.then_inc(s("proj_done"), 1)
                    if j % 2 == 1 or j == n - 1:
                        pe.wait_ge(s("proj_done"), j + 1)
                        pe.sem_inc(ring_used, 1)
                pe.wait_ge(s("proj_ev_act"), (n + 1) // 2)
                pe.wait_ge(s("proj_ev_vec"), n // 2)

            def project_out(blk, l, tiles, src, first_item):
                for t in tiles:
                    c0 = COL[t] - (META if blk == 1 else 0)
                    for i in range(ITEMS_WO):
                        w = (slot_wait(pe, blk, l, first_item + i) if t == tiles[0] else
                             ring[:, ring_slot(blk, first_item + i), :]).rearrange("p (c n) -> p c n", c=2)
                        for c in range(2):
                            k = 2 * i + c
                            for half in range(2):
                                mm = pe.matmul(ps[0:ROWS[t], 2 * (t - tiles[0]) + half, :],
                                               src[:, k, c0:c0 + ROWS[t]], w[:, c, 512 * half:512 * half + 512],
                                               start=(k == 0), stop=(k == KC - 1))
                    mm.then_inc(s("out_ready"), 1)
                pe.wait_ge(s("out_ready"), len(tiles))
                pe.sem_inc(ring_used, ITEMS_WO)

            with pe.Fori(0, LAYERS) as l:
                pe.wait_ge(s("xn_ready"), 2)
                for k in range(KC):
                    if k >= 4:
                        pe.wait_ge(s("ht_ready"), k - 3)
                    for t in range(2):
                        tr = pe.transpose(ps[:, k % 4, t * P:(t + 1) * P], xn[:, t, k * P:(k + 1) * P], ident)
                    tr.then_inc(s("ht_done"), 1)
                project(1, l, N1, SEQ, META)

                for t in range(2):
                    cs = slice(COL[t + 1], COL[t + 1] + P)
                    pe.transpose(ps[:, 5, t * P:(t + 1) * P], projT[:, SV, cs], ident)
                    for c in range(2):
                        tr = pe.transpose(ps[:, 6, (2 * t + c) * P:(2 * t + c + 1) * P], projT[:, DV + c, cs], ident)
                tr.then_inc(s("v_done"), 1)
                pe.wait_ge(s("mla_sq"), 1)
                for c in range(2):
                    pe.matmul(ps[:, 0, 0:SEQ], ones, sq3[:, c, :], start=(c == 0), stop=(c == 1))
                pe.matmul(ps[:, 0, SEQ:2 * SEQ], ones, sq3[:, 2, :], start=True, stop=True).then_inc(s("mla_ss"), 1)
                pe.wait_ge(s("mla_n"), 1)
                pe.wait_ge(s("v_evicted"), 1)
                pe.wait_ge(s("params_late"), 16)
                uq = prm1("w_uq").rearrange("p (c n) -> p c n", c=2)
                for h in range(4):
                    for c in range(2):
                        pe.matmul(ps[0:96, h, 0:SEQ], uq[:, c, 96 * h:96 * h + 96], cn[:, c, :],
                                  start=(c == 0), stop=(c == 1))
                for h in range(4):
                    mm = pe.matmul(ps[0:64, 4 + h, 0:SEQ], prm1("w_ukv")[:, P * h:P * h + 64], cn[:, 2, :],
                                   start=True, stop=True)
                mm.then_inc(s("mla_qk"), 1)
                pe.wait_ge(s("mla_qh"), 1)
                for t in range(2):
                    mm = pe.matmul(ps[:, t, :], cn[:, 2, t * P:(t + 1) * P], prm1("w_ukv"), start=True, stop=True)
                for h in range(2):
                    pe.matmul(ps[64:96, 2 + h, :], const("rot96")[0:96, :], qh[0:96, 2 * h:2 * h + 2, :],
                              start=True, stop=True)
                pe.wait_ge(s("mla_kh"), 1)
                pe.matmul(ps[64:96, 4, 0:SEQ], const("rot96")[0:96, :], projT[0:96, MKR, META:T],
                          start=True, stop=True).then_inc(s("mla_rot"), 1)
                pe.wait_ge(s("mla_rope"), 1)
                pe.wait_ge(s("mla_v"), 1)
                pe_scores(pe, JOBS1, 0)
                for j in range(len(JOBS1)):
                    if j + 1 < len(JOBS1):
                        pe_scores(pe, JOBS1, j + 1)
                    pe_attend(pe, JOBS1, j)

                pe.wait_ge(s("stt_done"), len(JOBS1))
                pe.wait_ge(s("o_evicted"), len(JOBS1))
                for kt in (1, 2):
                    for h in range(4):
                        r = slice(64 * (h % 2), 64 * (h % 2) + 64)
                        mm = pe.matmul(ps[:, 4 * (kt - 1) + h, 0:SEQ - P * (kt - 1)],
                                       projT[r, DK + h // 2, COL[kt]:COL[kt] + P],
                                       projT[r, DQ + h // 2, COL[kt]:T], start=True, stop=True)
                mm.then_inc(s("sb_z"), 1)
                pe.wait_ge(s("sb_sp"), 1)
                for h in range(4):
                    pe.matmul(ps[:, h, 0:SEQ], tri, sp1[:, h, :], start=True, stop=False)
                    pe.matmul(ps[:, h, P:SEQ], ones, sp2[:, h, :], start=False, stop=True)
                    mm = pe.matmul(ps[:, 4 + h, 0:P], tri, sp2[:, h, :], start=True, stop=True)
                mm.then_inc(s("sb_r"), 1)
                pe.wait_ge(s("sb_am"), 1)
                for h in range(4):
                    o = ps[64 * (h % 2):64 * (h % 2) + 64, h // 2, :]
                    pe.matmul(o[:, 0:SEQ], vD[:, 0, 64 * h:64 * h + 64], sp1[:, h, :], start=True, stop=False)
                    mm = pe.matmul(o[:, P:SEQ], vD[:, 1, 64 * h:64 * h + 64], sp2[:, h, :], start=False, stop=True)
                mm.then_inc(s("sb_o"), 1)

                pe.wait_ge(s("y_sq"), 1)
                for g in range(4):
                    for c in range(2):
                        mm = pe.matmul(ps[:, 4 + g, 0:SEQ], ones, ysq[:, 2 * g + c, :], start=(c == 0), stop=(c == 1))
                mm.then_inc(s("y_ss"), 1)
                pe.wait_ge(s("y_ready"), 1)
                project_out(1, l, (1, 2), yT, ITEMS_P1)
                new_layer(pe, l, 0, 0)

            with pe.Fori(0, LAYERS) as l:
                for k in range(KC):
                    if k >= 4:
                        pe.wait_ge(s("ht_ready"), k - 3)
                    for t in range(3):
                        tr = pe.transpose(ps[:, k % 4, COL[t]:COL[t] + ROWS[t]],
                                          res[0:ROWS[t], t, k * P:(k + 1) * P], ident[0:ROWS[t], 0:ROWS[t]])
                    tr.then_inc(s("ht_done"), 1)

                pe.wait_ge(s("ht_ready"), KC)
                lev = 0
                for step in mixer_order():
                    kind = step[0]
                    if kind == "project":
                        j = step[1]
                        w = slot_wait(pe, 2, l, j // 2) if j % 2 == 0 else ring[:, ring_slot(2, j // 2), :]
                        w = w.rearrange("p (c k m) -> p c k m", c=2, k=KC)
                        if j >= 2:
                            pe.wait_ge(s("proj_ev_act"), j - 1)
                        for k in range(KC):
                            mm = pe.matmul(ps[:, 5 + j % 2, 0:T], w[:, j % 2, k, :], hT[:, k, 0:T],
                                           start=(k == 0), stop=(k == KC - 1))
                        mm.then_inc(s("proj_done"), 1)
                        if j % 2 == 1:
                            pe.wait_ge(s("proj_done"), j + 1)
                            pe.sem_inc(ring_used, 1)
                    elif kind == "decay_rows":
                        pe.wait_ge(s("g_scan"), 1)
                        for h in range(4):
                            mm = pe.matmul(ps[:, h, 0:T], const("sel")[0:4, h * P:(h + 1) * P], gsm[0:4, :],
                                           start=True, stop=True)
                        mm.then_inc(s("g_bc"), 1)
                    elif kind == "beta_rows":
                        pe.wait_ge(s("g_bcev"), 1)
                        for h in range(4):
                            mm = pe.matmul(ps[:, h, 0:T], const("selb")[32:36, h * P:(h + 1) * P], gsm[32:36, :],
                                           start=True, stop=True)
                        mm.then_inc(s("g_bc"), 1)
                    elif kind == "gate_columns":
                        pe.wait_ge(s("g_bcev"), 2)
                        for t in range(3):
                            tr = pe.transpose(ps[0:ROWS[t], 0, t * P:(t + 1) * P], gsm[:, COL[t]:COL[t] + ROWS[t]], ident)
                        tr.then_inc(s("g_cols"), 1)
                    elif kind == "length":
                        pe.wait_ge(s("cv_sq"), 4 * step[1] + 4)
                        if step[1] == 0:
                            pe.wait_ge(s("g_colsev"), 1)
                        else:
                            pe.wait_ge(s("cv_rs"), 1)
                        for h in range(4):
                            mm = pe.matmul(ps[:, h, 0:T], ones, projT[:, NQ + 4 * step[1] + h, :], start=True, stop=True)
                        mm.then_inc(s("cv_ss"), 1)
                    elif kind == "rope":
                        i = step[1]
                        pe.wait_ge(s("proj_ev_act"), ROPE_CHUNKS[i] + 1)
                        if i:
                            pe.wait_ge(s("rp_used"), i)
                        pe.matmul(ps[:, 7, 0:T], const("rot"), projT[:, ROPE_CHUNKS[i], :], start=True, stop=True)\
                            .then_inc(s("rp_done"), 1)
                    elif kind == "index":
                        _, t, q = step
                        nix = 4 * (t - 1) + q
                        nk = COL[t] + ROWS[t]
                        pe.wait_ge(s("rp_ready"), len(ROPE_CHUNKS) - 3 + q)
                        if nix:
                            pe.wait_ge(s("ix_relu"), nix)
                        else:
                            pe.wait_ge(s("proj_ev_act"), N2)
                        for h in range(2):
                            r = slice(64 * h, 64 * h + 64)
                            mm = pe.matmul(ps[:, 5 + h, 0:nk], projT[r, IQ + q, COL[t]:COL[t] + P], projT[r, IK, 0:nk],
                                           start=True, stop=True)
                        mm.then_inc(s("ix_s"), 1)
                    elif kind == "tokens":
                        pe.wait_ge(s("ix_relu"), 8)
                        pe.wait_ge(s("rp_used"), len(ROPE_CHUNKS))
                        for t in range(3):
                            for c in range(4):
                                tr = pe.transpose(ps[0:ROWS[t], 5 + t, c * P:(c + 1) * P],
                                                  projT[:, AV + c, COL[t]:COL[t] + ROWS[t]], ident)
                        tr.then_inc(s("v_done"), 1)
                    if kind not in ("scores", "lower", "level_p", "level_q", "values", "outputs"):
                        continue
                    t = step[1]
                    n = ROWS[t]
                    cs = slice(COL[t], COL[t] + n)
                    if kind == "scores":
                        if t == 0:
                            pe.wait_ge(s("cv_norm"), 1)
                            pe.wait_ge(s("cv_silu"), 12)
                        else:
                            pe.wait_ge(s("d_stv"), t)
                            pe.wait_ge(s("d_oev"), t)
                        for h in range(4):
                            pe.transpose(ps[0:n, 0, h * P:(h + 1) * P], cv[:, 4 + h, cs], ident)
                            tr = pe.transpose(ps[0:n, 1, h * P:(h + 1) * P], cv[:, 8 + h, cs], ident)
                        tr.then_inc(s("kv_done"), 1)
                        for h in range(4):
                            pe.matmul(ps[0:n, 2, h * n:(h + 1) * n], cv[:, 4 + h, cs], cv[:, 4 + h, cs],
                                      start=True, stop=True)
                            mm = pe.matmul(ps[0:n, 3, h * n:(h + 1) * n], cv[:, 4 + h, cs], cv[:, h, cs],
                                           start=True, stop=True)
                        mm.then_inc(s("gq_done"), 1)
                    elif kind == "lower":
                        pe.wait_ge(s("d_u"), t + 1)
                        pe.wait_ge(s("kv_ev"), t + 1)
                        for h in range(4):
                            tr = pe.transpose(ps[0:n, 0, h * n:(h + 1) * n], uT[0:n, h, 0:n], ident[0:n, 0:n])
                        tr.then_inc(s("d_lt"), 1)
                        if t:
                            for h in range(4):
                                mm = pe.matmul(ps[0:n, 1, h * P:(h + 1) * P], cv[:, 4 + h, cs], st[:, h, :],
                                               start=True, stop=True)
                            mm.then_inc(s("d_ks"), 1)
                    elif kind == "level_p":
                        pe.wait_ge(s("d_ls"), lev + 1)
                        pe.wait_ge(s("d_y"), lev + t + 1)
                        for h in range(4):
                            mm = pe.matmul(ps[0:n, 4, h * n:(h + 1) * n], lS[0:n, h, 0:n], yU[0:n, h, 0:n],
                                           start=True, stop=True)
                        mm.then_inc(s("d_p"), 1)
                    elif kind == "level_q":
                        pe.wait_ge(s("d_pev"), lev + 1)
                        for h in range(4):
                            mm = pe.matmul(ps[0:n, 2, h * n:(h + 1) * n], yL[0:n, h, 0:n], pP[0:n, h, 0:n],
                                           start=True, stop=True)
                        if step[2] < levels(t) - 1:
                            mm.then_inc(s("d_q"), 1)
                            for h in range(4):
                                mm = pe.matmul(ps[0:n, 3, h * n:(h + 1) * n], pP[0:n, h, 0:n], yL[0:n, h, 0:n],
                                               start=True, stop=True)
                            mm.then_inc(s("d_q2"), 1)
                        else:
                            mm.then_inc(s("d_q"), 1)
                        lev += 1
                    elif kind == "values":
                        pe.wait_ge(s("d_r"), t + 1)
                        pe.wait_ge(s("d_y"), lev + t + 1)
                        for h in range(4):
                            mm = pe.matmul(ps[0:n, 2, h * P:(h + 1) * P], yU[0:n, h, 0:n], rr[0:n, h, :],
                                           start=True, stop=True)
                        mm.then_inc(s("d_vn"), 1)
                    elif kind == "outputs":
                        pe.wait_ge(s("d_vnev"), t + 1)
                        if t < 2:
                            pe.wait_ge(s("d_kd"), t + 1)
                            for h in range(4):
                                mm = pe.matmul(ps[:, 4, h * P:(h + 1) * P], kd[0:n, h, :], vn[0:n, h, :],
                                               start=True, stop=True)
                            mm.then_inc(s("d_st"), 1)
                        for h in range(4):
                            o = ps[:, 3, h * n:(h + 1) * n]
                            if t:
                                pe.matmul(o, st[:, h, :], ebc[:, h, cs], start=True, stop=False)
                            mm = pe.matmul(o, vn[0:n, h, :], atT[0:n, h, 0:n], start=(t == 0), stop=True)
                        mm.then_inc(s("d_o"), 1)
                pe.wait_ge(s("d_oev"), 3)
                pe.wait_ge(s("v_evicted"), 1)
                pe_scores(pe, JOBS2, 0)
                pe.wait_ge(s("od_sq"), 1)
                for h in range(4):
                    mm = pe.matmul(ps[:, 4 + h, 0:T], ones, projT[:, NQ + h, :], start=True, stop=True)
                mm.then_inc(s("od_ss"), 1)
                pe.wait_ge(s("od_rs"), 1)
                for j in range(len(JOBS2)):
                    if j + 1 < len(JOBS2):
                        pe_scores(pe, JOBS2, j + 1)
                    pe_attend(pe, JOBS2, j)
                pe.wait_ge(s("o_evicted"), len(JOBS2))
                pe.wait_ge(s("od_ready"), 1)
                project_out(2, l, (0, 1, 2), mixT, ITEMS_P2)

                pe.wait_ge(s("ln_done"), 3)
                pe.wait_ge(s("params_late"), 16)
                wr = prm2("wr").rearrange("p (k n) -> p k n", k=KC)
                for k in range(KC + 1):
                    if k < KC:
                        if k >= 2:
                            pe.wait_ge(s("m_htev"), k - 1)
                        for t in range(3):
                            tr = pe.transpose(ps[:, 6 + k % 2, COL[t]:COL[t] + ROWS[t]],
                                              res[0:ROWS[t], t, k * P:(k + 1) * P], ident[0:ROWS[t], 0:ROWS[t]])
                        tr.then_inc(s("m_ht"), 1)
                    if k:
                        pe.wait_ge(s("m_htev"), k)
                        mm = pe.matmul(ps[0:36, 0, 0:T], wr[:, k - 1, :], h2T[:, k - 1, :],
                                       start=(k == 1), stop=(k == KC))
                mm.then_inc(s("m_lt"), 1)
                pe.wait_ge(s("m_ltev"), 1)
                for t in range(3):
                    tr = pe.transpose(ps[:, 1, 64 * t:64 * t + 36], logitT[:, COL[t]:COL[t] + P], ident[0:36, 0:36])
                tr.then_inc(s("m_lg"), 1)
                pe.wait_ge(s("m_grp"), 1)
                for t in range(3):
                    for u in range(t + 1):
                        m = ROWS[u]
                        pe.matmul(ps[:, 6, 256 + 8 * t:260 + 8 * t], const("strict" if u == t else "ones")[0:m, :],
                                  lg[0:m, u, 52:56], start=(u == 0), stop=(u == t))
                for t in range(3):
                    mm = pe.matmul(ps[:, 6, 288:292], ones[0:ROWS[t], :], lg[0:ROWS[t], t, 52:56],
                                   start=(t == 0), stop=(t == 2))
                mm.then_inc(s("m_sizes"), 1)


                def expert_wait(k, half, j):
                    slot = ring_slot(2, ITEMS_MIX2 + 3 * j + k)
                    before = LAYERS * uses_before(1, ITEMS1, slot) + uses_before(2, ITEMS_MIX2, slot)
                    per = uses_before(2, ITEMS2, slot)
                    pe.wait_ge(slot_in[slot], l * (16 * per) + half * 16 + 16 * (before + 1))
                    return slot

                def up_all(n, j, half):
                    w1 = ring[:, expert_wait(0, half, j), :].rearrange("p (k n) -> p k n", k=KC)
                    pe.wait_ge(s("m_cb"), n + 1)
                    pe.matmul(ps[:, 4, 0:T], const("sel2")[0:2, j * P:(j + 1) * P],
                              comb2f[0:2, bass.ds(half * T, T)] if not isinstance(half, int) else
                              comb2f[0:2, half * T:half * T + T], start=True, stop=True)
                    w3 = ring[:, expert_wait(1, half, j), :].rearrange("p (k n) -> p k n", k=KC)
                    for f in range(2):
                        pe.wait_ge(s("m_hid"), n * 2 + (f + 1))
                        for k in range(KC):
                            pe.matmul(ps[:, f, 0:T], w1[:, k, P * f:P * f + P], h2T[:, k, :],
                                      start=(k == 0), stop=(k == KC - 1))
                        for k in range(KC):
                            mm = pe.matmul(ps[:, 2 + f, 0:T], w3[:, k, P * f:P * f + P], h2T[:, k, :],
                                           start=(k == 0), stop=(k == KC - 1))
                        mm.then_inc(s("m_up"), 1)
                    pe.wait_ge(s("m_up"), n * 2 + 2)
                    pe.sem_inc(up_used, 1)

                def down_all(n, j, half):
                    w = ring[:, expert_wait(2, half, j), :].rearrange("p (c n) -> p c n", c=2)
                    pe.wait_ge(s("m_hid"), n * 2 + 4)
                    for d in range(KC):
                        ago = 3 if d > 2 else (2, 2, 5)[d]
                        pe.wait_ge(s("m_yadd"), n * KC + (d - ago + 1 + 3))
                        for f in range(2):
                            mm = pe.matmul(ps[:, 5 + d % 3, 0:T], w[:, f, P * d:P * d + P], hid[:, 2 * j + f, :],
                                           start=(f == 0), stop=(f == 1))
                        mm.then_inc(s("m_y"), 1)
                    pe.wait_ge(s("m_y"), n * KC + KC)
                    pe.sem_inc(down_used, 1)

                def experts_all():
                    pe.wait_ge(s("m_comb"), 1)
                    for t in range(3):
                        tr = pe.transpose(ps[0:EXPERTS, 7, COL[t]:COL[t] + ROWS[t]], lg[0:ROWS[t], t, 256:288],
                                          ident[0:ROWS[t], 0:ROWS[t]])
                    tr.then_inc(s("m_combT"), 1)
                    pe.wait_ge(s("cin"), 16)
                    up_all(0, 0, 0)
                    with pe.Fori(0, TURNS) as g:
                        up_all(g * 2 + 1, 1, g)
                        down_all(g * 2, 0, g)
                        up_all(g * 2 + 2, 0, g + 1)
                        down_all(g * 2 + 1, 1, g)
                    up_all(EXPERTS - 1, 1, TURNS)
                    down_all(EXPERTS - 2, 0, TURNS)
                    down_all(EXPERTS - 1, 1, TURNS)
                    pe.wait_ge(s("m_yadd"), KC * EXPERTS + 3)
                    for t in range(3):
                        for d in range(KC):
                            tr = pe.transpose(ps[0:ROWS[t], 2 * t + d // 4, (d % 4) * P:(d % 4 + 1) * P],
                                              yacc[:, d, COL[t]:COL[t] + ROWS[t]], ident)
                        tr.then_inc(s("m_back"), 1)

                def gather(g):
                    pe.wait_ge(s("x_sel"), g + 1)
                    if isinstance(g, int):
                        pe.wait_ge(s("m_comb"), 1)
                    for k in range(KC):
                        for t in range(3):
                            n = ROWS[t]
                            pe.matmul(ps[:, 6 + k // 4, (k % 4) * P:(k % 4 + 1) * P],
                                      res[0:n, t, k * P:(k + 1) * P], xsel[0:n, t, :],
                                      start=(t == 0), stop=(t == 2))
                    for t in range(3):
                        n = ROWS[t]
                        pe.transpose(ps[:, 3, COL[t]:COL[t] + n], xsel[0:n, t, :], ident[0:n, 0:n])
                    for t in range(3):
                        n = ROWS[t]
                        w = (lg[0:n, t, 256 + PER_GROUP * g:256 + PER_GROUP * (g + 1)] if isinstance(g, int)
                             else lg[0:n, t, bass.ds(g * PER_GROUP + 256, PER_GROUP)])
                        mm = pe.matmul(ps[:, 3, 288:288 + PER_GROUP], xsel[0:n, t, :], w, start=(t == 0), stop=(t == 2))
                    mm.then_inc(s("x_g"), 1)

                def up(g, e):
                    if e == 0:
                        pe.wait_ge(s("x_ge"), g + 1)
                    half = g * (PER_GROUP // 2) + e // 2
                    slot = expert_wait(0, half, e % 2)
                    expert_wait(1, half, e % 2)
                    w = ring[:, slot:slot + 2, :].rearrange("p w (k n) -> p w k n", k=KC)
                    pe.wait_ge(s("x_hid"), g * PER_GROUP + (e + 1))
                    for k in range(KC):
                        if k == KC // 2 and e:
                            turn(g, e - 1)
                        mm = pe.matmul(ps[:, e % 2, :].rearrange("p (w n) -> p w n", w=2), xg[:, k, :], w[:, :, k, :],
                                       start=(k == 0), stop=(k == KC - 1))
                    mm.then_inc(up_used, 1)

                def turn(g, e):
                    pe.wait_ge(s("x_hid"), g * PER_GROUP + (e + 3))
                    for f in range(2):
                        tr = pe.transpose(ps[:, 2, 256 * (e % 2) + P * f:256 * (e % 2) + P * (f + 1)],
                                          xh[:, e % 2, P * f:P * (f + 1)], ident)
                    tr.then_inc(s("x_t"), 1)

                def down(g, e):
                    w = ring[:, expert_wait(2, g * (PER_GROUP // 2) + e // 2, e % 2), :].rearrange("p (c n) -> p c n", c=2)
                    pe.wait_ge(s("x_te"), g * PER_GROUP + (e + 1))
                    if e == 0:
                        pe.wait_ge(s("x_ye"), g + 1)
                    for f in range(2):
                        for half in range(2):
                            mm = pe.matmul(ps[:, 4 + half, :], xhT[:, e % 2, P * f:P * (f + 1)],
                                           w[:, f, 512 * half:512 * half + 512],
                                           start=(e == 0 and f == 0), stop=(e == PER_GROUP - 1 and f == 1))
                    mm.then_inc(down_used, 1)

                def group(g, last):
                    up(g, 0)
                    for e in range(PER_GROUP):
                        if e < PER_GROUP - 1:
                            up(g, e + 1)
                        else:
                            if not last:
                                gather(g + 1)
                            turn(g, e)
                        down(g, e)

                def experts_grouped():
                    gather(0)
                    with pe.Fori(0, GROUPS - 1) as g:
                        group(g, False)
                    group(GROUPS - 1, True)
                    pe.wait_ge(s("x_ye"), GROUPS + 1)
                    for t in range(3):
                        for half in range(2):
                            for g in range(GROUPS):
                                mm = pe.matmul(ps[0:ROWS[t], 2 * t + half, :], xselT[:, g, COL[t]:COL[t] + ROWS[t]],
                                               xy[:, g, 512 * half:512 * half + 512],
                                               start=(g == 0), stop=(g == GROUPS - 1))
                        mm.then_inc(s("m_back"), 1)

                crowded = branch(pe)
                with pe.If(crowded > 0):
                    experts_all()
                with pe.Else():
                    experts_grouped()
                pe.wait_ge(s("m_back"), 3)
                pe.sem_inc(ring_used, 3 * EXPERTS)
                new_layer(pe, l, LAYERS, 1)

        @block.scalar
        def _(a):
            a.dma_start(cst[:, :], A["consts"]).then_inc(start_in, 16)
            a.dma_start(res[:, 1:3, :], A["x"][0].rearrange("(t p) d -> p t d", p=P)).then_inc(start_in, 16)
            a.dma_start(res[0:META, 0, :], A["meta_tokens_2"]).then_inc(start_in, 16)
            a.dma_start(posi[:, :], A["positions"].broadcast_to([P, SEQ])).then_inc(start_in, 16)
            a.wait_ge(seen, 1)
            a.activation(sinT, sinT, ACT.Sin).then_inc(tables_done, 1)
            a.activation(cosT, cosT, ACT.Sin).then_inc(tables_done, 1)
            a.wait_ge(tables_done, 2)

            with a.Fori(0, LAYERS) as l:
                L = Linked(a, s("act_order"))
                nc.scalar.preload_act_table_set("natural_log_exp_and_others")
                first = P1["w_uq"][0]
                a.dma_start(prm[:, 0:first], A["params_1"][bass.ds(l * P, P), 0:first]).then_inc(s("params_in"), 16)
                a.dma_start(prm[:, first:NP1], A["params_1"][bass.ds(l * P, P), first:NP1])\
                    .then_inc(s("params_late"), 16)
                for t in (1, 2):
                    L(a.activation(yT[:, 0:4, :], res[:, t, :], ACT.Square, accum_out=ssum[:, t:t + 1]))
                rsqrt_act(a, L, rstd[:, 1:3], ssum[:, 1:3], 1.0 / D, eps6, s("rstd_ready"))
                for j in range(0, N1, 2):
                    a.wait_ge(s("proj_done"), j + 1)
                    L(a.activation(projT[:, j, META:T], ps[:, 4 + j % 4, 0:SEQ], ACT.Copy), s("proj_ev_act"))
                a.wait_ge(s("proj_ev_vec"), N1 // 2)
                L(a.activation(sq3, projT[:, MQ:MQ + 3, META:T], ACT.Square), s("mla_sq"))
                a.wait_ge(s("v_done"), 1)
                L(a.activation(vA, ps[:, 5, 0:2 * P], ACT.Copy))
                L(a.activation(vD, ps[:, 6, :], ACT.Copy), s("v_evicted"))
                a.wait_ge(s("mla_ss"), 1)
                rs = sq3[:, 0:2, :]
                L(a.activation(rs[:, 0, :], ps[:, 0, 0:SEQ], ACT.Ln, bias=eps6, scale=1.0 / 256))
                L(a.activation(rs[:, 1, :], ps[:, 0, SEQ:2 * SEQ], ACT.Ln, bias=eps6, scale=1.0 / P))
                L(a.activation(rs, rs, ACT.Exp, scale=-0.5), s("mla_rs"))
                a.wait_ge(s("mla_qk"), 1)
                L(a.activation(qh[0:96], ps[0:96, 0:4, 0:SEQ], ACT.Copy), s("mla_qh"))
                a.wait_ge(s("mla_rot"), 1)
                L(a.activation(vC, ps[:, 0:2, :], ACT.Copy), s("mla_v"))
                for j in range(len(JOBS1)):
                    if j == 0:
                        act_exp(a, L, JOBS1, 0)
                    if j + 1 < len(JOBS1):
                        act_exp(a, L, JOBS1, j + 1)
                    act_evict(a, L, JOBS1, j)
                a.wait_ge(s("sb_u"), 2)
                for u, lo in ((u1, l1), (u2, l2)):
                    L(a.activation(lo, u, ACT.Abs))
                    L(a.activation(lo, lo, ACT.Exp, scale=-1.0))
                    L(a.activation(lo, lo, ACT.Ln, bias=ones[:, 0:1]), s("sb_l"))
                a.wait_ge(s("sb_d"), 2)
                L(a.activation(sp1, u1, ACT.Exp))
                L(a.activation(sp2, u2, ACT.Exp), s("sb_a"))
                L(a.activation(sg, projT[:, GATE:GATE + KC, META:T], ACT.Exp, scale=-1.0), s("gate_exp"))
                a.wait_ge(s("sb_o"), 1)
                L(a.activation(yT[:, 6:8, :], ps[:, 0:2, 0:SEQ], ACT.Copy), s("sb_oe"))
                a.wait_ge(s("conv_ready"), 1)
                L(a.activation(ysq, yT, ACT.Square), s("y_sq"))
                a.wait_ge(s("y_ss"), 1)
                rsqrt_act(a, L, yrs, ps[:, 4:8, 0:SEQ], 1.0 / 256, eps6, s("y_rs"))
                for t in (1, 2):
                    a.wait_ge(s("out_ready"), t)
                    L(a.activation(xn[:, t - 1, :], ps[:, 2 * t - 2:2 * t, :].rearrange("p a b -> p (a b)"), ACT.Square,
                                   accum_out=ssum[:, t:t + 1]))
                    rsqrt_act(a, L, rstd[:, t:t + 1], ssum[:, t:t + 1], 1.0 / D, eps6, s("out_ss"))
                new_layer(a, l, 0, 0)

            with a.Fori(0, LAYERS) as l:
                L = Linked(a, s("act_order"))
                nc.scalar.preload_act_table_set("natural_log_exp_and_others")
                first = P2["br"][0]
                a.dma_start(prm[:, 0:first], A["params_2"][bass.ds(l * P, P), 0:first]).then_inc(s("params_in"), 16)
                a.dma_start(prm[:, first:NP2], A["params_2"][bass.ds(l * P, P), first:NP2])\
                    .then_inc(s("params_late"), 16)
                lev = 0
                for step in mixer_order():
                    kind = step[0]
                    if kind == "project":
                        j = step[1]
                        a.wait_ge(s("proj_done"), j + 1)
                        L(a.activation(projT[:, j, :], ps[:, 5 + j % 2, 0:T], ACT.Copy), s("proj_ev_act"))
                    elif kind == "gates":
                        a.wait_ge(s("g_sm"), 1)
                        L(a.activation(gtmp[0:4, :], gsm[0:4, :], ACT.Abs))
                        L(a.activation(gtmp[0:4, :], gtmp[0:4, :], ACT.Exp, scale=-1.0))
                        L(a.activation(gtmp[0:4, :], gtmp[0:4, :], ACT.Ln, bias=ones[0:4, 0:1]))
                        L(a.activation(nega[0:4, :], prm2("a_log")[0:4, :], ACT.Exp))
                        L(a.activation(gsm[32:36, :], projT[32:36, SM, :], ACT.Exp, scale=-1.0), s("g_ln"))
                    elif kind == "decay_rows":
                        a.wait_ge(s("g_bc"), 1)
                        L(a.activation(gcb, ps[:, 0:4, 0:T], ACT.Copy), s("g_bcev"))
                        L(a.activation(ebc, gcb, ACT.Exp))
                    elif kind == "beta_rows":
                        a.wait_ge(s("g_bc"), 2)
                        L(a.activation(btb, ps[:, 0:4, 0:T], ACT.Copy), s("g_bcev"))
                    elif kind == "gate_columns":
                        a.wait_ge(s("g_cols"), 1)
                        L(a.activation(cols[0:META, 0, :], ps[0:META, 0, 0:P], ACT.Copy))
                        L(a.activation(cols[:, 1:3, :], ps[:, 0, P:3 * P].rearrange("p (a b) -> p a b", a=2), ACT.Copy))
                        L(a.activation(ecol[:, 4:12].rearrange("p (a b) -> p a b", a=2), cols[:, 1:3, 0:4], ACT.Exp),
                          s("g_colsev"))
                    elif kind == "sigmoid":
                        c = step[1]
                        a.wait_ge(s("cv_ready"), c + 1)
                        sigmoid(a, L, projT[:, NQ + c, :], cv[:, c, :], s("cv_exp"))
                    elif kind == "silu" and step[1] < 8:
                        c = step[1]
                        a.wait_ge(s("cv_silu"), c + 1)
                        L(a.activation(projT[:, NQ + c, :], cv[:, c, :], ACT.Square), s("cv_sq"))
                    elif kind == "length":
                        q = NQ + 4 * step[1]
                        a.wait_ge(s("cv_ss"), step[1] + 1)
                        rsqrt_act(a, L, projT[:, q:q + 4, :], ps[:, 0:4, 0:T], 1.0, eps6, s("cv_rs"))
                    elif kind == "silu_z":
                        a.wait_ge(s("cv_silu"), 12)
                        sigmoid(a, L, gate_silu, projT[:, NZ:NZ + 4, :], s("z_exp"))
                    elif kind == "index":
                        _, t, q = step
                        nix = 4 * (t - 1) + q
                        nk = COL[t] + ROWS[t]
                        a.wait_ge(s("ix_s"), nix + 1)
                        if nix >= 2:
                            a.wait_ge(s("ix_used"), nix - 1)
                        L(a.activation(rl[:, 2 * (q % 2):2 * (q % 2) + 2, 0:nk], ps[:, 5:7, 0:nk], ACT.Relu,
                                       scale=64 ** -0.5), s("ix_relu"))
                    elif kind == "tokens":
                        a.wait_ge(s("d_ks"), 2)
                        a.wait_ge(s("v_done"), 1)
                        L(a.activation(vS[0:META, 0, :], ps[0:META, 5, :], ACT.Copy))
                        L(a.activation(vS[:, 1:3, :], ps[:, 6:8, :], ACT.Copy), s("v_evicted"))
                    if kind not in ("scores", "lower", "level_p", "level_q", "values", "outputs"):
                        continue
                    t = step[1]
                    n = ROWS[t]
                    if kind == "scores":
                        a.wait_ge(s("kv_done"), t + 1)
                        if t:
                            a.wait_ge(s("d_kd"), t)
                            a.wait_ge(s("d_r"), t)
                        L(a.activation(kN[0:n], ps[0:n, 0, :], ACT.Copy))
                        L(a.activation(vN[0:n], ps[0:n, 1, :], ACT.Copy), s("kv_ev"))
                        a.wait_ge(s("d_diff"), t + 1)
                        L(a.activation(kdf[0:n, :], kdf[0:n, :], ACT.Exp))
                        L(a.activation(dif[0:n, :, 0:n], dif[0:n, :, 0:n], ACT.Exp), s("d_exp"))
                    elif kind == "lower":
                        a.wait_ge(s("d_lt"), t + 1)
                        if t:
                            a.wait_ge(s("d_ls"), lev)
                        L(a.activation(lT[0:n, :, 0:n], ps[0:n, 0, 0:4 * n].rearrange("p (a b) -> p a b", a=4), ACT.Copy),
                          s("d_l"))
                    elif kind == "level_p":
                        a.wait_ge(s("d_p"), lev + 1)
                        L(a.activation(pP[0:n, :, 0:n], ps[0:n, 4, 0:4 * n].rearrange("p (a b) -> p a b", a=4), ACT.Copy),
                          s("d_pev"))
                        lev += 1
                    elif kind == "values":
                        a.wait_ge(s("d_vn"), t + 1)
                        L(a.activation(vn[0:n], ps[0:n, 2, :], ACT.Copy), s("d_vnev"))
                    elif kind == "outputs":
                        a.wait_ge(s("d_o"), t + 1)
                        L(a.activation(odT[:, :, COL[t]:COL[t] + n],
                                       ps[:, 3, 0:4 * n].rearrange("p (a b) -> p a b", a=4), ACT.Copy), s("d_oev"))
                a.wait_ge(s("ix_used"), 8)
                L(a.activation(projT[:, NQ:NQ + 4, :], odT, ACT.Square), s("od_sq"))
                a.wait_ge(s("od_ss"), 1)
                rsqrt_act(a, L, projT[:, NQ:NQ + 4, :], ps[:, 4:8, 0:T], 1.0 / P, eps6, s("od_rs"))
                for j in range(len(JOBS2)):
                    if j == 0:
                        act_exp(a, L, JOBS2, 0)
                    if j + 1 < len(JOBS2):
                        act_exp(a, L, JOBS2, j + 1)
                    act_evict(a, L, JOBS2, j)
                for norm in range(2):
                    for t in range(3):
                        n = ROWS[t]
                        k = 3 * norm + t + 1
                        a.wait_ge(s("ln_mean"), k)
                        L(a.activation(junk[0:n], res[0:n, t, :], ACT.Square, bias=lnm[0:n, t:t + 1],
                                       accum_out=ssq[0:n, t:t + 1]))
                        rsqrt_act(a, L, rstd[0:n, t:t + 1], ssq[0:n, t:t + 1], 1.0 / D, eps5[0:n], s("ln_rstd"))
                    if norm:
                        break
                    for k in range(KC):
                        a.wait_ge(s("m_ht"), k + 1)
                        L(a.activation(h2T[:, k, :], ps[:, 6 + k % 2, 0:T], ACT.Copy), s("m_htev"))
                    a.wait_ge(s("m_lt"), 1)
                    L(a.activation(logitT, ps[0:36, 0, 0:T], ACT.Copy), s("m_ltev"))
                    a.wait_ge(s("m_e1"), 1)
                    L(a.activation(lg[:, :, 40:44], lg[:, :, 40:44], ACT.Exp))
                    L(a.activation(lg[:, :, 99:100], lg[:, :, 99:100], ACT.Exp), s("m_e1d"))

                    def gate_exp(n, j):
                        for f in range(2):
                            a.wait_ge(s("m_up"), n * 2 + (f + 1))
                            if f == 0:
                                a.activation(cbb[:, j, :], ps[:, 4, 0:T], ACT.Copy).then_inc(s("m_cb"), 1)
                            a.activation(e1b[:, 2 * j + f, :], ps[:, f, 0:T], ACT.Exp, scale=-1.0)\
                                .then_inc(s("m_exp"), 1)

                    def experts_all():
                        a.wait_ge(s("m_combev"), 1)
                        a.dma_start(comb_dram, combT).then_inc(s("m_combst"), 16)
                        a.wait_ge(s("m_combst"), 16)
                        a.dma_start(comb2[0:2], comb_dram.rearrange("(g j) t -> j g t", j=2)).then_inc(s("cin"), 16)
                        a.sem_inc(s("m_cb"), 1)
                        gate_exp(0, 0)
                        with a.Fori(0, TURNS) as g:
                            gate_exp(g * 2 + 1, 1)
                            gate_exp(g * 2 + 2, 0)
                        gate_exp(EXPERTS - 1, 1)

                    def exp_gate(g, e):
                        a.wait_ge(up_used, l * EXPERTS + g * PER_GROUP + (e + 1))
                        a.activation(xe[:, e % 2, :], ps[:, e % 2, 0:256], ACT.Exp, scale=-1.0).then_inc(s("x_exp"), 1)

                    def tokens_in(g):
                        a.wait_ge(s("x_g"), g + 1)
                        to = xselT[:, g, :] if isinstance(g, int) else \
                            arena[:, bass.ds(g * T + XSELT, T)]
                        a.activation(to, ps[:, 3, 0:T], ACT.Copy).then_inc(s("act_group"), 1)
                        a.activation(xg, ps[:, 6:8, :], ACT.Copy).then_inc(s("x_ge"), 1)
                        a.wait_ge(s("x_hid"), g * PER_GROUP + 2)
                        a.activation(xcg, ps[:, 3, 288:288 + PER_GROUP], ACT.Copy).then_inc(s("x_cg"), 1)

                    def group(g, last):
                        exp_gate(g, 0)
                        for e in range(PER_GROUP):
                            if e < PER_GROUP - 1:
                                exp_gate(g, e + 1)
                            elif not last:
                                tokens_in(g + 1)
                            a.wait_ge(s("x_t"), g * PER_GROUP + (e + 1))
                            a.activation(xhT[:, e % 2, :], ps[:, 2, 256 * (e % 2):256 * (e % 2) + 256], ACT.Copy)\
                                .then_inc(s("x_te"), 1)
                        a.wait_ge(down_used, l * EXPERTS + g * PER_GROUP + PER_GROUP)
                        to = xy[:, g, :] if isinstance(g, int) else arena[:, bass.ds(g * D + 1300, D)]
                        a.activation(to, ps[:, 4:6, :].rearrange("p a b -> p (a b)"), ACT.Copy).then_inc(s("x_ye"), 1)

                    def experts_grouped():
                        a.sem_inc(s("x_ye"), 1)
                        tokens_in(0)
                        with a.Fori(0, GROUPS - 1) as g:
                            group(g, False)
                        group(GROUPS - 1, True)

                    crowded = branch(a)
                    with a.If(crowded > 0):
                        experts_all()
                    with a.Else():
                        experts_grouped()
                new_layer(a, l, LAYERS, 1)

        @block.vector
        def _(v):
            MAGIC = 12582912.0
            C1, C2 = 6.28125, 0.0019353071795864769
            V0 = Linked(v, tables_vec)
            V0(v.memset(eps6, 1e-6))
            V0(v.memset(eps5, 1e-5))
            V0(v.memset(small[:, 0:32], 0.0))
            V0(v.memset(gsm, 0.0))
            v.wait_ge(start_in, 16 * 4)
            V0(v.tensor_copy(cosT, posi[:, :]))
            V0(v.tensor_scalar(cosT, cosT, const("freq"), None, ALU.mult))
            V0(v.tensor_scalar(sinT, cosT, float(1.0 / (2.0 * np.pi)), MAGIC, ALU.mult, ALU.add))
            V0(v.tensor_scalar(sinT, sinT, -MAGIC, None, ALU.add))
            V0(v.scalar_tensor_tensor(out=cosT, in0=sinT, scalar=-C1, in1=cosT, op0=ALU.mult, op1=ALU.add))
            V0(v.scalar_tensor_tensor(out=cosT, in0=sinT, scalar=-C2, in1=cosT, op0=ALU.mult, op1=ALU.add))
            V0(v.tensor_scalar(sinT, cosT, 3.1415925, -3.1415925, ALU.min, ALU.max))
            V0(v.tensor_scalar(cosT, sinT, float(np.pi / 2), None, ALU.add))
            V0(v.tensor_scalar(arena[:, 0:SEQ], cosT, float(np.pi), float(-2 * np.pi), ALU.is_gt, ALU.mult))
            V0(v.tensor_tensor(cosT, cosT, arena[:, 0:SEQ], ALU.add))
            V0(v.tensor_scalar(cosT, cosT, 3.1415925, -3.1415925, ALU.min, ALU.max), seen)

            with v.Fori(0, LAYERS) as l:
                V = Linked(v, s("vec_order"))
                v.wait_ge(s("rstd_ready"), 1)
                for t in (1, 2):
                    V(v.tensor_scalar(xn[:, t - 1, :], res[:, t, :], rstd[:, t:t + 1], None, ALU.mult), s("xn_ready"))
                v.wait_ge(s("params_in"), 16)
                for k in range(KC):
                    v.wait_ge(s("ht_done"), k + 1)
                    V(v.tensor_scalar(hT[:, k, META:T], ps[:, k % 4, 0:SEQ], prm1("g_pre")[:, k:k + 1], None, ALU.mult),
                      s("ht_ready"))
                for j in range(1, N1, 2):
                    v.wait_ge(s("proj_done"), j + 1)
                    V(v.tensor_copy(projT[:, j, META:T], ps[:, 4 + j % 4, 0:SEQ]), s("proj_ev_vec"))
                v.wait_ge(s("proj_ev_act"), (N1 + 1) // 2)
                v.wait_ge(s("mla_rs"), 1)
                rs = sq3[:, 0:2, :]
                for c in range(3):
                    g = prm1("g_q")[:, c:c + 1] if c < 2 else prm1("g_kv")
                    V(v.scalar_tensor_tensor(out=cn[:, c, :], in0=projT[:, MQ + c, META:T], scalar=g,
                                             in1=rs[:, c // 2, :], op0=ALU.mult, op1=ALU.mult),
                      s("mla_n") if c == 2 else None)
                v.wait_ge(s("mla_qk"), 1)
                V(v.tensor_copy(kh[0:64], ps[0:64, 4:8, 0:SEQ]), s("mla_kh"))
                R = slice(64, 96)
                v.wait_ge(s("mla_rot"), 1)
                tq = yT[R, 0:4, :]
                V(v.tensor_tensor(tq, ps[R, 2:4, :].rearrange("p a (b c) -> p (a b) c", b=2), bc(sinT[R], 4, 1), ALU.mult))
                V(v.tensor_tensor(qh[R], qh[R], bc(cosT[R], 4, 1), ALU.mult))
                V(v.tensor_tensor(qh[R], qh[R], tq, ALU.add))
                V(v.tensor_tensor(yT[R, 0, :], ps[R, 4, 0:SEQ], sinT[R], ALU.mult))
                V(v.tensor_tensor(yT[R, 1, :], projT[R, MKR, META:T], cosT[R], ALU.mult))
                V(v.tensor_tensor(kh[R], bc(yT[R, 0, :], 4, 1), bc(yT[R, 1, :], 4, 1), ALU.add), s("mla_rope"))
                for j in range(len(JOBS1)):
                    if j == 0:
                        vec_mask(v, V, JOBS1, 0)
                    if j + 1 < len(JOBS1):
                        vec_mask(v, V, JOBS1, j + 1)
                    vec_norm(v, V, JOBS1, j)
                cw = prm1("conv_w")
                for c in range(2):
                    y = yT[:, 2 + c, :]
                    u = sq3[:, c, :]
                    V(v.tensor_tensor(u, projT[:, CC + c, META:T], projT[:, CX + c, META:T], ALU.mult))
                    V(v.tensor_scalar(y, u, cw[:, 4 + c:5 + c], prm1("conv_b")[:, c:c + 1], ALU.mult, ALU.add))
                    for d in (1, 2):
                        k = 2 - d
                        V(v.scalar_tensor_tensor(out=y[:, d:SEQ], in0=u[:, 0:SEQ - d], scalar=cw[:, 2 * k + c:2 * k + c + 1],
                                                 in1=y[:, d:SEQ], op0=ALU.mult, op1=ALU.add))
                    V(v.tensor_tensor(y, y, projT[:, CB + c, META:T], ALU.mult))
                v.wait_ge(s("sb_z"), 1)
                V(v.tensor_scalar(u1, ps[:, 0:4, 0:SEQ], 0.125, None, ALU.mult), s("sb_u"))
                V(v.tensor_scalar(u2, ps[:, 4:8, 0:P], 0.125, None, ALU.mult), s("sb_u"))
                strict4 = bc(const("strict"), 4, 1)
                for i, (u, lo, sp_) in enumerate(((u1, l1, sp1), (u2, l2, sp2))):
                    v.wait_ge(s("sb_l"), i + 1)
                    V(v.scalar_tensor_tensor(out=sp_, in0=u, scalar=0.0, in1=lo, op0=ALU.max, op1=ALU.add))
                    V(v.tensor_tensor(sp_[:, :, 0:P], sp_[:, :, 0:P], strict4, ALU.mult), s("sb_sp") if i else None)
                v.wait_ge(s("sb_r"), 1)
                for i, (u, r) in enumerate(((u1, ps[:, 0:4, 0:SEQ]), (u2, ps[:, 4:8, 0:P]))):
                    V(v.scalar_tensor_tensor(out=u, in0=r, scalar=-1.0, in1=u, op0=ALU.mult, op1=ALU.add))
                    V(v.tensor_scalar(u, u, 0.0, None, ALU.min), s("sb_d"))
                v.wait_ge(s("sb_a"), 1)
                V(v.tensor_tensor(sp1[:, :, 0:P], sp1[:, :, 0:P], strict4, ALU.mult))
                V(v.tensor_tensor(sp2, sp2, strict4, ALU.mult), s("sb_am"))
                v.wait_ge(s("gate_exp"), 1)
                V(v.tensor_scalar(sg, sg, 1.0, None, ALU.add))
                V(v.reciprocal(sg, sg))
                V(v.tensor_tensor(sg, sg, projT[:, GATE:GATE + KC, META:T], ALU.mult))
                v.wait_ge(s("sb_oe"), 1)
                V(v.tensor_copy(small[:, 120:121], ones[:, 0:1]), s("conv_ready"))
                v.wait_ge(s("y_rs"), 1)
                for c in range(KC):
                    V(v.scalar_tensor_tensor(out=yT[:, c, :], in0=yT[:, c, :], scalar=prm1("g_grp")[:, c:c + 1],
                                             in1=yrs[:, c // 2, :], op0=ALU.mult, op1=ALU.mult))
                V(v.tensor_tensor(yT, yT, sg, ALU.mult), s("y_ready"))
                v.wait_ge(s("params_late"), 16)
                for t in (1, 2):
                    v.wait_ge(s("out_ss"), t)
                    o = ps[:, 2 * t - 2:2 * t, :].rearrange("p a b -> p (a b)")
                    V(v.scalar_tensor_tensor(out=xn[:, t - 1, :], in0=o, scalar=rstd[:, t:t + 1], in1=prm1("g_post"),
                                             op0=ALU.mult, op1=ALU.mult))
                    V(v.tensor_tensor(res[:, t, :], res[:, t, :], xn[:, t - 1, :], ALU.add), s("res_ready"))
                new_layer(v, l, 0, 0)

            with v.Fori(0, LAYERS) as l:
                V = Linked(v, s("vec_order"))
                for k in range(KC):
                    v.wait_ge(s("ht_done"), k + 1)
                    V(v.tensor_copy(hT[:, k, :], ps[:, k % 4, 0:T]), s("ht_ready"))
                v.wait_ge(s("params_in"), 16)
                cw = prm2("conv_w").rearrange("p (c k) -> p c k", k=4)
                levu = const("lev_u").rearrange("p (i m) -> p i m", m=P)
                levl = const("lev_l").rearrange("p (i m) -> p i m", m=P)
                lev, lev2 = 0, 0
                for step in mixer_order():
                    kind = step[0]
                    if kind == "gates":
                        V(v.memset(gsm, 0.0))
                        v.wait_ge(s("proj_ev_act"), SM + 1)
                        V(v.tensor_scalar(gsm[0:4, :], projT[0:4, SM, :], prm2("dt")[0:4, :], None, ALU.add))
                        V(v.tensor_copy(gsm[64:72, :], projT[64:72, SM, :]), s("g_sm"))
                        v.wait_ge(s("g_ln"), 1)
                        V(v.scalar_tensor_tensor(out=gtmp[0:4, :], in0=gsm[0:4, :], scalar=0.0, in1=gtmp[0:4, :],
                                                 op0=ALU.max, op1=ALU.add))
                        V(v.tensor_scalar(gtmp[0:4, :], gtmp[0:4, :], nega[0:4, :], -1.0, ALU.mult, ALU.mult))
                        V(v.tensor_scalar(gsm[32:36, :], gsm[32:36, :], 1.0, None, ALU.add))
                        V(v.reciprocal(gsm[32:36, :], gsm[32:36, :]))
                        for t in range(3):
                            cs = slice(COL[t], COL[t] + ROWS[t])
                            V(v.tensor_tensor_scan(gsm[0:4, cs], bcones4[:, 0:ROWS[t]], gtmp[0:4, cs], 0.0, ALU.mult,
                                                   ALU.add), s("g_scan") if t == 2 else None)
                    elif kind == "gate_columns":
                        v.wait_ge(s("g_colsev"), 1)
                        for t in range(3):
                            V(v.tensor_copy(elast[:, 4 * t:4 * t + 4], ebc[:, :, COL[t] + ROWS[t] - 1]))
                        V(v.tensor_scalar(neg_e[:, 4:12], ecol[:, 4:12], -1.0, None, ALU.mult))
                        V(v.tensor_scalar(wi[:, 8:24].rearrange("p (a b) -> p a b", a=2), cols[:, 1:3, 64:72], 8 ** -0.5,
                                          None, ALU.mult))
                    elif kind == "conv":
                        c = step[1]
                        x = projT[:, NQ + c, :]
                        v.wait_ge(s("proj_ev_act"), NQ + c + 1)
                        V(v.tensor_scalar(cv[:, c, :], x, cw[:, c, 3:4], None, ALU.mult))
                        for d in (1, 2, 3):
                            V(v.scalar_tensor_tensor(out=cv[:, c, d:T], in0=x[:, 0:T - d], scalar=cw[:, c, 3 - d:4 - d],
                                                     in1=cv[:, c, d:T], op0=ALU.mult, op1=ALU.add),
                              s("cv_ready") if d == 3 else None)
                    elif kind == "silu":
                        c = step[1]
                        v.wait_ge(s("cv_exp"), c + 1)
                        V(v.tensor_tensor(cv[:, c, :], cv[:, c, :], projT[:, NQ + c, :], ALU.mult), s("cv_silu"))
                    elif kind == "unit":
                        v.wait_ge(s("cv_rs"), step[1] + 1)
                        if step[1] == 0:
                            V(v.scalar_tensor_tensor(out=cv[:, 0:4, :], in0=cv[:, 0:4, :], scalar=float(P) ** -0.5,
                                                     in1=projT[:, NQ:NQ + 4, :], op0=ALU.mult, op1=ALU.mult))
                            V(v.tensor_tensor(ebc, ebc, cv[:, 0:4, :], ALU.mult))
                        else:
                            V(v.tensor_tensor(cv[:, 4:8, :], cv[:, 4:8, :], projT[:, NK_:NK_ + 4, :], ALU.mult),
                              s("cv_norm"))
                    elif kind == "silu_z":
                        v.wait_ge(s("z_exp"), 1)
                        V(v.tensor_tensor(projT[:, NZ:NZ + 4, :], projT[:, NZ:NZ + 4, :], gate_silu, ALU.mult))
                    elif kind == "rope":
                        i = step[1]
                        x = projT[:, ROPE_CHUNKS[i], :]
                        v.wait_ge(s("rp_done"), i + 1)
                        V(v.tensor_tensor(rtmp, ps[:, 7, 0:T], const("sin"), ALU.mult), s("rp_used"))
                        V(v.tensor_tensor(x, x, const("cos"), ALU.mult))
                        V(v.tensor_tensor(x, x, rtmp, ALU.add), s("rp_ready"))
                    elif kind == "index":
                        _, t, q = step
                        nk = COL[t] + ROWS[t]
                        v.wait_ge(s("ix_relu"), 4 * (t - 1) + q + 1)
                        for h in range(2):
                            w = wi[:, 8 * t + 2 * q + h:8 * t + 2 * q + h + 1]
                            x = rl[:, 2 * (q % 2) + h, 0:nk]
                            if q == 0 and h == 0:
                                caus = const("caus" if t == 1 else "caus2")[:, 0:nk]
                                V(v.tensor_scalar(sc[:, 0:nk], x, w, None, ALU.mult))
                            else:
                                V(v.scalar_tensor_tensor(out=sc[:, 0:nk], in0=x, scalar=w, in1=sc[:, 0:nk],
                                                         op0=ALU.mult, op1=ALU.add), s("ix_used") if h else None)
                        if q == 3:
                            V(v.tensor_tensor(sc[:, 0:nk], sc[:, 0:nk], caus, ALU.add))
                    elif kind == "strike":
                        nk = COL[step[1]] + ROWS[step[1]]
                        for cur, nxt in ((sc, wk), (wk, sc)):
                            V(v.max(max8, cur[:, 0:nk]))
                            V(v.match_replace(nxt[:, 0:nk], max8, cur[:, 0:nk], -3.0e38))
                    elif kind == "mask":
                        t = step[1]
                        nk = COL[t] + ROWS[t]
                        V(v.tensor_scalar(sc[:, 0:nk], sc[:, 0:nk], -2.0e38, NEG, ALU.is_gt, ALU.mult))
                        V(v.tensor_tensor(masks[t][:, 0:nk], sc[:, 0:nk], caus, ALU.add))
                    if kind not in ("scores", "lower", "level_p", "level_q", "values", "outputs"):
                        continue
                    t = step[1]
                    n = ROWS[t]
                    cs = slice(COL[t], COL[t] + n)
                    idn = bc(ident[0:n, 0:n], 4, 1)

                    def psv(b, w=n):
                        return ps[0:n, b, 0:4 * w].rearrange("p (a b) -> p a b", a=4)

                    if kind == "scores":
                        for h in range(4):
                            V(v.tensor_scalar(dif[0:n, h, 0:n], gcb[0:n, h, cs], cols[0:n, t, h:h + 1], 0.0,
                                              ALU.subtract, ALU.min))
                        V(v.tensor_tensor(kdf[0:n, :], gcb[0:n, :, COL[t] + n - 1], cols[0:n, t, 0:4], ALU.subtract),
                          s("d_diff"))
                        v.wait_ge(s("d_exp"), t + 1)
                        V(v.tensor_tensor(dif[0:n, :, 0:n], dif[0:n, :, 0:n], bc(const("upper")[0:n, 0:n], 4, 1), ALU.mult))
                        v.wait_ge(s("gq_done"), t + 1)
                        if t:
                            v.wait_ge(s("d_o"), t)
                        V(v.tensor_tensor(uT[0:n, :, 0:n], psv(2), dif[0:n, :, 0:n], ALU.mult))
                        V(v.tensor_tensor(uT[0:n, :, 0:n], uT[0:n, :, 0:n], btb[0:n, :, cs], ALU.mult))
                        V(v.tensor_tensor(uT[0:n, :, 0:n], uT[0:n, :, 0:n], bc(const("strict")[0:n, 0:n], 4, 1), ALU.mult),
                          s("d_u"))
                        V(v.tensor_tensor(atT[0:n, :, 0:n], psv(3), dif[0:n, :, 0:n], ALU.mult))
                        V(v.tensor_tensor(yU[0:n, :, 0:n], uT[0:n, :, 0:n], bc(levu[0:n, 0, 0:n], 4, 1), ALU.mult))
                        V(v.tensor_tensor(yU[0:n, :, 0:n], idn, yU[0:n, :, 0:n], ALU.subtract))
                    elif kind == "lower":
                        v.wait_ge(s("d_l"), t + 1)
                        V(v.tensor_tensor(yL[0:n, :, 0:n], lT[0:n, :, 0:n], bc(levl[0:n, 0, 0:n], 4, 1), ALU.mult))
                        V(v.tensor_tensor(yL[0:n, :, 0:n], idn, yL[0:n, :, 0:n], ALU.subtract), s("d_y"))
                        beta = bc(cols[0:n, t, 32:36], P, 2)
                        v.wait_ge(s("kv_ev"), t + 1)
                        if t:
                            v.wait_ge(s("d_ks"), t)
                            V(v.tensor_tensor(rr[0:n], psv(1, P), bc(neg_e[0:n, 4 * t:4 * t + 4], P, 2), ALU.mult))
                            V(v.tensor_tensor(rr[0:n], rr[0:n], vN[0:n], ALU.add))
                            V(v.tensor_tensor(rr[0:n], rr[0:n], beta, ALU.mult), s("d_r"))
                        else:
                            V(v.tensor_tensor(rr[0:n], vN[0:n], beta, ALU.mult), s("d_r"))
                        if t < 2:
                            V(v.tensor_tensor(kd[0:n], kN[0:n], bc(kdf[0:n, :], P, 2), ALU.mult), s("d_kd"))
                    elif kind == "level_q":
                        v.wait_ge(s("d_q"), lev + 1)
                        V(v.tensor_tensor(yU[0:n, :, 0:n], yU[0:n, :, 0:n], psv(2), ALU.subtract),
                          s("d_y") if step[2] == levels(t) - 1 else None)
                        if step[2] < levels(t) - 1:
                            lev2 += 1
                            v.wait_ge(s("d_q2"), lev2)
                            V(v.tensor_tensor(yL[0:n, :, 0:n], yL[0:n, :, 0:n], psv(3), ALU.subtract), s("d_y"))
                        lev += 1
                    elif kind == "outputs" and t < 2:
                        v.wait_ge(s("d_st"), t + 1)
                        sview = ps[:, 4, :].rearrange("p (a b) -> p a b", a=4)
                        if t:
                            v.wait_ge(s("d_o"), t + 1)
                            V(v.tensor_tensor(st, st, bc(elast[:, 4 * t:4 * t + 4], P, 2), ALU.mult))
                            V(v.tensor_tensor(st, st, sview, ALU.add), s("d_stv"))
                        else:
                            V(v.tensor_copy(st, sview), s("d_stv"))
                vec_mask(v, V, JOBS2, 0)
                v.wait_ge(s("od_rs"), 1)
                V(v.scalar_tensor_tensor(out=mixT[:, 0:4, :], in0=odT, scalar=prm2("norm_g"),
                                         in1=projT[:, NQ:NQ + 4, :], op0=ALU.mult, op1=ALU.mult))
                V(v.tensor_tensor(mixT[:, 0:4, :], mixT[:, 0:4, :], projT[:, NZ:NZ + 4, :], ALU.mult), s("od_ready"))
                for j in range(len(JOBS2)):
                    if j + 1 < len(JOBS2):
                        vec_mask(v, V, JOBS2, j + 1)
                    vec_norm(v, V, JOBS2, j)

                def layer_norm(t, which, add):
                    n = ROWS[t]
                    r = res[0:n, t, :]
                    V(v.scalar_tensor_tensor(out=r, in0=r, scalar=ALPHA, in1=add, op0=ALU.mult, op1=ALU.add,
                                             accum_out=ssum[0:n, t:t + 1]))
                    V(v.tensor_scalar(lnm[0:n, t:t + 1], ssum[0:n, t:t + 1], -1.0 / D, None, ALU.mult), s("ln_mean"))
                    v.wait_ge(s("ln_rstd"), 3 * (which - 1) + t + 1)
                    V(v.scalar_tensor_tensor(out=r, in0=r, scalar=lnm[0:n, t:t + 1], in1=prm2(f"ln{which}_g")[0:n],
                                             op0=ALU.add, op1=ALU.mult))
                    V(v.scalar_tensor_tensor(out=r, in0=r, scalar=rstd[0:n, t:t + 1], in1=prm2(f"ln{which}_b")[0:n],
                                             op0=ALU.mult, op1=ALU.add), s("ln_done"))

                v.wait_ge(s("params_late"), 16)
                for t in range(3):
                    v.wait_ge(s("out_ready"), t + 1)
                    layer_norm(t, 1, ps[0:ROWS[t], 2 * t:2 * t + 2, :].rearrange("p a b -> p (a b)"))

                def c(i, w):
                    return lg[:, :, i:i + w]

                def each(i, w):
                    return bc(lg[:, :, i], w, 2)

                v.wait_ge(s("m_lg"), 1)
                desc = bc(const("desc"), 3, 1)
                desc4 = bc(const("desc")[:, 0:4], 3, 1)
                logits = ps[:, 1, 0:192].rearrange("p (t n) -> p t n", t=3)[:, :, 0:36]
                V(v.tensor_tensor(c(0, 36), logits, bc(prm2("br"), 3, 1), ALU.add))
                V(v.tensor_reduce(lg[:, :, 36], c(0, 4), AX, ALU.max))
                V(v.tensor_tensor(c(40, 4), c(0, 4), each(36, 4), ALU.subtract))
                V(v.tensor_tensor(c(48, 4), c(0, 4), each(36, 4), ALU.is_equal))
                V(v.tensor_tensor(c(48, 4), c(48, 4), desc4, ALU.mult))
                V(v.tensor_reduce(lg[:, :, 37], c(48, 4), AX, ALU.max))
                V(v.tensor_tensor(c(52, 4), c(48, 4), each(37, 4), ALU.is_equal), s("m_grp"))
                V(v.tensor_scalar(c(56, 4), c(52, 4), -NEG, NEG, ALU.mult, ALU.add))
                V(v.tensor_tensor(c(64, 32).rearrange("p t (a b) -> p t a b", a=4),
                                  c(4, 32).rearrange("p t (a b) -> p t a b", a=4), bc(c(56, 4), 8, 3), ALU.add))
                for k in range(2):
                    src = 64 if k == 0 else 164
                    m, oh = 96 + 2 * k, 132 + 64 * k
                    V(v.tensor_reduce(lg[:, :, m], c(src, 32), AX, ALU.max))
                    V(v.tensor_tensor(c(300, 32), c(src, 32), each(m, 32), ALU.is_equal))
                    V(v.tensor_tensor(c(300, 32), c(300, 32), desc, ALU.mult))
                    V(v.tensor_reduce(lg[:, :, m + 1], c(300, 32), AX, ALU.max))
                    V(v.tensor_tensor(c(oh, 32), c(300, 32), each(m + 1, 32), ALU.is_equal))
                    if k == 0:
                        V(v.scalar_tensor_tensor(out=c(164, 32), in0=c(132, 32), scalar=NEG, in1=c(64, 32),
                                                 op0=ALU.mult, op1=ALU.add))
                V(v.tensor_tensor(c(99, 1), c(98, 1), c(96, 1), ALU.subtract), s("m_e1"))
                V(v.tensor_scalar(c(332, 4), c(52, 4), -1000.0, 1000.0, ALU.mult, ALU.add))
                v.wait_ge(s("m_sizes"), 1)
                V(v.tensor_tensor(c(332, 4), c(332, 4), ps[:, 6, 256:280].rearrange("p (t n) -> p t n", t=3)[:, :, 0:4],
                                  ALU.add))
                V(v.tensor_reduce(mx[:, 0:1], ps[:, 6, 288:292], AX, ALU.max))
                V(v.tensor_scalar(mx[:, 0:1], mx[:, 0:1], GROUP_SLOTS + 0.5, None, ALU.is_gt))
                V(v.tensor_copy(flag[:, :], mx[:, 0:1]), s("m_flag"))
                v.wait_ge(s("m_e1d"), 1)
                V(v.tensor_reduce(lg[:, :, 45], c(40, 4), AX, ALU.add))
                V(v.tensor_scalar(c(100, 1), c(99, 1), 1.0, None, ALU.add))
                V(v.tensor_tensor(c(100, 1), c(100, 1), c(45, 1), ALU.mult))
                V(v.reciprocal(c(100, 1), c(100, 1)))
                V(v.tensor_tensor(c(101, 1), c(100, 1), c(99, 1), ALU.mult))
                V(v.tensor_tensor(c(256, 32), c(132, 32), each(100, 32), ALU.mult))
                V(v.tensor_tensor(c(300, 32), c(196, 32), each(101, 32), ALU.mult))
                V(v.tensor_tensor(c(256, 32), c(256, 32), c(300, 32), ALU.add), s("m_comb"))

                def hidden(n, j, at=0):
                    for f in range(2):
                        e = e1b[:, 2 * j + f, :]
                        v.wait_ge(s("m_exp"), n * 2 + (f + 1))
                        v.tensor_scalar(e, e, 1.0, None, ALU.add).then_inc(s("vec_loop"), 1)
                        v.wait_ge(s("vec_loop"), at + 4 * f + 1)
                        v.reciprocal(e, e).then_inc(s("vec_loop"), 1)
                        v.wait_ge(s("vec_loop"), at + 4 * f + 2)
                        v.tensor_tensor(e, e, ps[:, f, 0:T], ALU.mult).then_inc(s("vec_loop"), 1)
                        v.wait_ge(s("vec_loop"), at + 4 * f + 3)
                        v.tensor_tensor(e, e, ps[:, 2 + f, 0:T], ALU.mult).then_inc(s("vec_loop"), 1)
                        v.wait_ge(s("vec_loop"), at + 4 * f + 4)
                        v.tensor_tensor(hid[:, 2 * j + f, :], e, cbb[:, j, :], ALU.mult).then_inc(s("m_hid"), 1)
                        v.wait_ge(s("m_hid"), n * 2 + (f + 1 + 2))

                def add_up(n):
                    for d in range(KC):
                        v.wait_ge(s("m_y"), n * KC + (d + 1))
                        v.tensor_tensor(yacc[:, d, :], yacc[:, d, :], ps[:, 5 + d % 3, 0:T], ALU.add)\
                            .then_inc(s("m_yadd"), 1)
                    v.wait_ge(s("m_yadd"), n * KC + (KC + 3))

                def experts_all():
                    v.wait_ge(s("m_combT"), 1)
                    v.tensor_copy(combT, ps[0:EXPERTS, 7, 0:T]).then_inc(s("m_combev"), 1)
                    v.memset(yacc, 0.0).then_inc(s("vec_loop"), 1)
                    v.wait_ge(s("vec_loop"), 1)
                    v.sem_clear(s("vec_loop"))
                    v.sem_inc(s("m_hid"), 2)
                    v.sem_inc(s("m_yadd"), 3)
                    hidden(0, 0)
                    v.sem_inc(s("vec_turns"), 1)
                    v.sem_clear(s("vec_loop"))
                    with v.Fori(0, TURNS) as g:
                        hidden(g * 2 + 1, 1)
                        add_up(g * 2)
                        hidden(g * 2 + 2, 0, 8)
                        add_up(g * 2 + 1)
                        v.sem_inc(s("vec_turns"), 1)
                        v.sem_clear(s("vec_loop"))
                    hidden(EXPERTS - 1, 1)
                    add_up(EXPERTS - 2)
                    add_up(EXPERTS - 1)

                def select(g):
                    for t in range(3):
                        n = ROWS[t]
                        at = lg[0:n, t, 332 + g:333 + g] if isinstance(g, int) else lg[0:n, t, bass.ds(g + 332, 1)]
                        v.tensor_scalar(xsel[0:n, t, :], const("slots")[0:n], at, None, ALU.is_equal)\
                            .then_inc(s("x_sel") if t == 2 else s("vec_sel"), 1)
                    

                def group(g, last):
                    at = 0
                    v.wait_ge(s("x_cg"), g + 1)
                    for e in range(PER_GROUP):
                        x = xe[:, e % 2, :]
                        v.wait_ge(s("x_exp"), g * PER_GROUP + (e + 1))
                        v.tensor_scalar(x, x, 1.0, None, ALU.add).then_inc(s("vec_loop"), 1)
                        v.wait_ge(s("vec_loop"), at + 1)
                        v.reciprocal(x, x).then_inc(s("vec_loop"), 1)
                        v.wait_ge(s("vec_loop"), at + 2)
                        v.tensor_tensor(x, x, ps[:, e % 2, 0:256], ALU.mult).then_inc(s("vec_loop"), 1)
                        at += 3
                        v.wait_ge(s("vec_loop"), at)
                        v.scalar_tensor_tensor(out=xh[:, e % 2, :], in0=ps[:, e % 2, 256:512], scalar=xcg[:, e:e + 1], in1=x,
                                               op0=ALU.mult, op1=ALU.mult).then_inc(s("x_hid"), 1)
                        if e == PER_GROUP - 3 and not last:
                            select(g + 1)
                    if not last:
                        v.sem_clear(s("vec_loop"))

                def experts_grouped():
                    v.sem_inc(s("x_hid"), 2)
                    select(0)
                    with v.Fori(0, GROUPS - 1) as g:
                        group(g, False)
                    group(GROUPS - 1, True)

                crowded = branch(v)
                with v.If(crowded > 0):
                    experts_all()
                with v.Else():
                    experts_grouped()
                for t in range(3):
                    v.wait_ge(s("m_back"), t + 1)
                    layer_norm(t, 2, ps[0:ROWS[t], 2 * t:2 * t + 2, :].rearrange("p a b -> p (a b)"))
                new_layer(v, l, LAYERS, 1)

        @block.gpsimd
        def _(g):
            def clear(base, l):
                g.wait_ge(layer_done, l * 4 + (4 * base + 3))
                g.sem_inc(layer_seen, 1)
                g.sem_clear(range(layer_sems[0].num, layer_sems[-1].num + 1))
                g.sem_inc(layer_done, 1)
                g.sem_inc(layer_go, 1)

            with g.Fori(0, LAYERS) as l:
                clear(0, l)
            with g.Fori(0, LAYERS) as l:
                G = Linked(g, s("pool_order"))
                levl = const("lev_l").rearrange("p (i m) -> p i m", m=P)
                lev = 0
                for t in range(3):
                    n = ROWS[t]
                    g.wait_ge(s("d_l"), t + 1)
                    for i in range(n.bit_length() - 2):
                        if lev:
                            g.wait_ge(s("d_p"), lev)
                        G(g.tensor_tensor(lS[0:n, :, 0:n], lT[0:n, :, 0:n], bc(levl[0:n, i + 1, 0:n], 4, 1), ALU.mult),
                          s("d_ls"))
                        lev += 1
                clear(LAYERS, l)


def _ins(inputs):
    f = {k: np.ascontiguousarray(v) for k, v in inputs.items()}
    a1 = np.cumsum([0, 256, 128, 128, 256, 256, 256, 256, 128, 32, 256, 256, 256, 1024])
    r = [np.arange(a1[i], a1[i + 1]) for i in range(13)]
    kv0, kv1 = r[1][:64], r[1][64:]
    cols1 = np.concatenate([r[0], kv0, kv0, kv1, kv1, r[2], r[3], r[4], r[5], r[6], r[7],
                            np.tile(r[8], 4), r[9], r[10], r[11], r[12], np.tile(r[8], 4)])
    a2 = np.cumsum([0, 512, 512, 512, 512, 4, 4, 512, 512, 512, 512, 64, 8])
    q = [np.arange(a2[i], a2[i + 1]) for i in range(12)]
    cols2 = np.concatenate([np.tile(q[5], 8), np.tile(q[4], 8), np.tile(q[11], 8), q[10], q[10],
                            q[0], q[1], q[2], q[3], q[6], q[7], q[8], q[9]])

    def items(w, cols):
        n = len(cols) // 256
        w = w[:, :, cols].reshape(LAYERS, KC, P, n, 2, P)
        return np.ascontiguousarray(w.transpose(0, 3, 2, 4, 1, 5)).reshape(LAYERS * n * P, 2 * D)

    def by_feature(w):
        w = w.reshape(LAYERS * EXPERTS, KC, P, D_EXP).transpose(0, 2, 1, 3)
        return np.ascontiguousarray(w).reshape(LAYERS * EXPERTS * P, KC * D_EXP)

    def col(v, n):
        return v.reshape(LAYERS, n, P).transpose(0, 2, 1)

    def rows(v):
        return np.broadcast_to(v[:, None, :], (LAYERS, P, v.shape[-1]))

    def pad4(v):
        return np.tile(v, (1, P // 4))[:, :, None]

    p1 = np.concatenate([col(f["norm_pre"], KC), col(f["mla_q_norm"], 2), col(f["mla_kv_norm"], 1),
                         f["conv_w"].reshape(LAYERS, 6, P).transpose(0, 2, 1), col(f["conv_b"], 2),
                         col(f["group_norm"], KC), rows(f["attn_sinks"]),
                         f["mla_w_uq"].reshape(LAYERS, 2, P, 384).transpose(0, 2, 1, 3).reshape(LAYERS, P, 768),
                         f["mla_w_ukv"], rows(f["norm_post"])], 2)
    wr = np.concatenate([f["w_grp_2"], f["w_rtr_2"]], 2).reshape(LAYERS, KC, P, 36)
    wr = wr.transpose(0, 2, 1, 3).reshape(LAYERS, P, KC * 36)
    br = np.concatenate([f["b_grp_2"], f["b_rtr_2"]], 1)
    p2 = np.concatenate([f["conv_w_2"].reshape(LAYERS, 4, 12, P).transpose(0, 3, 2, 1).reshape(LAYERS, P, 48),
                         f["dn_norm_g_2"][:, :, None], pad4(f["a_log_2"]), pad4(f["dt_bias_2"]), rows(br), wr,
                         rows(f["ln1_g_2"]), rows(f["ln1_b_2"]), rows(f["ln2_g_2"]), rows(f["ln2_b_2"])], 2)
    return {
        "x": f["x"], "meta_tokens_2": f["meta_tokens_2"], "positions": f["positions"], "consts": constants(),
        "w_in_1": items(f["w_in"], cols1), "w_in_2": items(f["w_in_2"], cols2),
        "w_out_1": f["w_out"].reshape(LAYERS * D, D), "w_out_2": f["w_out_2"].reshape(LAYERS * D, D),
        "params_1": np.ascontiguousarray(p1).reshape(LAYERS * P, NP1),
        "params_2": np.ascontiguousarray(p2).reshape(LAYERS * P, NP2),
        "w1_2": by_feature(f["w1_2"]), "w3_2": by_feature(f["w3_2"]),
        "w2_2": f["w2_2"].reshape(LAYERS * EXPERTS * D_EXP, D),
    }


def kernel(**inputs):
    import concourse.bacc as bacc
    from concourse.bass_utils import run_bass_kernel_spmd

    nc = bacc.Bacc("TRN2", target_bir_lowering=False, num_devices=1)
    arrays = _ins(inputs)
    aps = {k: nc.dram_tensor(k, v.shape, mybir.dt.from_np(v.dtype), kind="ExternalInput").ap() for k, v in arrays.items()}
    out = nc.dram_tensor("out", (1, SEQ, D), F32, kind="ExternalOutput").ap()
    program(nc, aps, out)
    r = run_bass_kernel_spmd(nc, [arrays], core_ids=[0])
    return r.results[0]["out"]
```
